# Optimizing a Trainium2 kernel written in Bass

```python
import jax, jax.numpy as jnp
from jax import lax
import numpy as np

D_MODEL = 1024
BATCH = 1
SEQ = 1024
DEPTH = 1

CHUNK = 64
Q_BLOCK = 128
MLA_HEADS = 8
QK_NOPE_DIM = 64
QK_ROPE_DIM = 32
QK_HEAD_DIM = QK_NOPE_DIM + QK_ROPE_DIM
V_HEAD_DIM = 64
Q_LORA_RANK = 256
KV_LORA_RANK = 128
ROPE_THETA = 10000.0
CONV_WIDTH = D_MODEL // 2
CONV_KERNEL = 31
N_BRANCHES = 2
N_GROUPS = 4
EXPERTS_PER_GROUP = 8
N_EXPERTS = N_GROUPS * EXPERTS_PER_GROUP
TOP_K_IN_GROUP = 2
EXPERT_FF = 256
EPS = 1e-6

IN_SIZES = (Q_LORA_RANK, KV_LORA_RANK, QK_ROPE_DIM, 2 * CONV_WIDTH, N_BRANCHES * D_MODEL)
IN_COLS = sum(IN_SIZES)
IN_SPLITS = tuple(int(v) for v in np.cumsum(IN_SIZES)[:-1])

kernel_name = "hybrid_mla_conformer_hiermoe_block"

def rms_norm(x, g):
    xf = x.astype(jnp.float32)
    y = xf * lax.rsqrt(jnp.mean(xf * xf, axis=-1, keepdims=True) + EPS)
    return (y * g.astype(jnp.float32)).astype(x.dtype)

def layer_norm(x, g, b):
    xf = x.astype(jnp.float32)
    mu = jnp.mean(xf, axis=-1, keepdims=True)
    var = jnp.mean(jnp.square(xf - mu), axis=-1, keepdims=True)
    y = (xf - mu) * lax.rsqrt(var + EPS)
    return (y * g.astype(jnp.float32) + b.astype(jnp.float32)).astype(x.dtype)

def apply_rope(x, positions):
    half = QK_ROPE_DIM // 2
    inv_freq = ROPE_THETA ** (-jnp.arange(half, dtype=jnp.float32) / half)
    ang = positions.astype(jnp.float32)[..., None] * inv_freq
    cos = jnp.cos(ang)[:, :, None, :]
    sin = jnp.sin(ang)[:, :, None, :]
    xf = x.astype(jnp.float32)
    x1, x2 = xf[..., :half], xf[..., half:]
    out = jnp.concatenate([x1 * cos - x2 * sin, x2 * cos + x1 * sin], axis=-1)
    return out.astype(x.dtype)

def chunk_causal_attention(q, k, v):
    B, T, H, Dh = q.shape
    Dv = v.shape[-1]
    nb = T // Q_BLOCK
    qb = q.reshape(B, nb, Q_BLOCK, H, Dh).transpose(1, 0, 2, 3, 4)
    key_chunk = jnp.arange(T) // CHUNK
    scale = Dh ** -0.5

    def one_block(args):
        qi, bi = args
        s = jnp.einsum('bqhd,bkhd->bhqk', qi, k, preferred_element_type=jnp.float32) * scale
        q_chunk = (bi * Q_BLOCK + jnp.arange(Q_BLOCK)) // CHUNK
        mask = key_chunk[None, :] <= q_chunk[:, None]
        s = jnp.where(mask[None, None], s, -jnp.inf)
        p = jax.nn.softmax(s, axis=-1).astype(v.dtype)
        return jnp.einsum('bhqk,bkhd->bqhd', p, v)

    out = lax.map(one_block, (qb, jnp.arange(nb)))
    return out.transpose(1, 0, 2, 3, 4).reshape(B, T, H, Dv)

def causal_depthwise_conv(u, w, b):
    K, C = w.shape
    y = lax.conv_general_dilated(
        u, w[:, None, :].astype(u.dtype), window_strides=(1,), padding=[(K - 1, 0)],
        dimension_numbers=('NWC', 'WIO', 'NWC'), feature_group_count=C)
    return y + b.astype(u.dtype)

def hierarchical_moe(h, w_gr, b_gr, w_er, b_er, w_eg, w_eu, w_ed):
    B, T, D = h.shape
    n = h.reshape(B * T, D)
    group_logits = jnp.matmul(n, w_gr).astype(jnp.float32) + b_gr.astype(jnp.float32)
    group_prob = jax.nn.softmax(group_logits, axis=-1)
    g_idx = jnp.argmax(group_logits, axis=-1)
    g_p = jnp.take_along_axis(group_prob, g_idx[:, None], axis=-1)
    exp_logits = (jnp.matmul(n, w_er).astype(jnp.float32) + b_er.astype(jnp.float32))
    exp_logits = exp_logits.reshape(B * T, N_GROUPS, EXPERTS_PER_GROUP)
    sel = jnp.take_along_axis(exp_logits, g_idx[:, None, None], axis=1)[:, 0]
    within = jax.nn.softmax(sel, axis=-1)
    top_p, top_i = lax.top_k(within, TOP_K_IN_GROUP)
    top_p = top_p / jnp.sum(top_p, axis=-1, keepdims=True)
    expert_id = g_idx[:, None] * EXPERTS_PER_GROUP + top_i
    weights = g_p * top_p
    combine = jnp.sum(jax.nn.one_hot(expert_id, N_EXPERTS, dtype=jnp.float32) * weights[..., None], axis=1)
    combine = combine.reshape(B, T, N_EXPERTS).astype(h.dtype)

    def per_sequence(args):
        xb, cb = args
        a = jnp.einsum('td,edf->tef', xb, w_eg)
        u = jnp.einsum('td,edf->tef', xb, w_eu)
        mid = jax.nn.silu(a) * u * cb[..., None]
        return jnp.einsum('tef,efd->td', mid, w_ed)

    return lax.map(per_sequence, (h, combine))

def setup_inputs(seed: int = 0) -> dict:
    key = jax.random.key(seed)
    ks = jax.random.split(key, 24)
    f32 = jnp.float32
    L, D, H = DEPTH, D_MODEL, MLA_HEADS

    def nrm(k, shape, fan_in):
        return jax.random.normal(k, shape, f32) * (fan_in ** -0.5)

    def gain(k, shape):
        return 1.0 + 0.02 * jax.random.normal(k, shape, f32)

    def bias(k, shape, s=0.02):
        return s * jax.random.normal(k, shape, f32)

    x = jax.random.normal(ks[0], (BATCH, SEQ, D), f32)
    offset = jax.random.randint(ks[1], (BATCH, 1), 0, 4096, dtype=jnp.int32)
    positions = (offset + jnp.arange(SEQ, dtype=jnp.int32)[None, :]).astype(jnp.int32)
    return {
        "x": x,
        "positions": positions,
        "g_mix": gain(ks[2], (L, D)),
        "w_in": nrm(ks[3], (L, D, IN_COLS), D),
        "g_q_lora": gain(ks[4], (L, Q_LORA_RANK)),
        "w_uq": nrm(ks[5], (L, Q_LORA_RANK, H * QK_HEAD_DIM), Q_LORA_RANK),
        "g_kv_lora": gain(ks[6], (L, KV_LORA_RANK)),
        "w_ukv": nrm(ks[7], (L, KV_LORA_RANK, H * (QK_NOPE_DIM + V_HEAD_DIM)), KV_LORA_RANK),
        "g_qk_q": gain(ks[8], (L, QK_HEAD_DIM)),
        "g_qk_k": gain(ks[9], (L, QK_HEAD_DIM)),
        "w_o_mla": nrm(ks[10], (L, H * V_HEAD_DIM, D), H * V_HEAD_DIM),
        "w_dw": nrm(ks[11], (L, CONV_KERNEL, CONV_WIDTH), CONV_KERNEL),
        "b_dw": bias(ks[12], (L, CONV_WIDTH)),
        "g_conv_ln": gain(ks[13], (L, CONV_WIDTH)),
        "b_conv_ln": bias(ks[14], (L, CONV_WIDTH)),
        "w_conv_out": nrm(ks[15], (L, CONV_WIDTH, D), CONV_WIDTH),
        "b_gates": bias(ks[16], (L, N_BRANCHES * D)),
        "w_out": nrm(ks[17], (L, D, D), D),
        "g_ffn": gain(ks[18], (L, D)),
        "w_group_router": nrm(ks[19], (L, D, N_GROUPS), D),
        "b_group_router": bias(ks[20], (L, N_GROUPS), 0.01),
        "w_expert_router": nrm(ks[21], (L, D, N_EXPERTS), D),
        "b_expert_router": bias(ks[22], (L, N_EXPERTS), 0.01),
        "w_e_gate": nrm(jax.random.fold_in(ks[23], 0), (L, N_EXPERTS, D, EXPERT_FF), D),
        "w_e_up": nrm(jax.random.fold_in(ks[23], 1), (L, N_EXPERTS, D, EXPERT_FF), D),
        "w_e_down": nrm(jax.random.fold_in(ks[23], 2), (L, N_EXPERTS, EXPERT_FF, D), EXPERT_FF),
    }

def reference(x, positions, g_mix, w_in, g_q_lora, w_uq, g_kv_lora, w_ukv, g_qk_q, g_qk_k,
              w_o_mla, w_dw, b_dw, g_conv_ln, b_conv_ln, w_conv_out, b_gates, w_out,
              g_ffn, w_group_router, b_group_router, w_expert_router, b_expert_router,
              w_e_gate, w_e_up, w_e_down):
    B, T, D = x.shape
    H = MLA_HEADS
    for l in range(DEPTH):
        h = rms_norm(x, g_mix[l])
        proj = jnp.matmul(h, w_in[l])
        q_down, kv_down, k_rope, conv_in, gate_logits = jnp.split(proj, IN_SPLITS, axis=-1)

        q = jnp.matmul(rms_norm(q_down, g_q_lora[l]), w_uq[l]).reshape(B, T, H, QK_HEAD_DIM)
        kv = jnp.matmul(rms_norm(kv_down, g_kv_lora[l]), w_ukv[l]).reshape(B, T, H, QK_NOPE_DIM + V_HEAD_DIM)
        k_nope, v = kv[..., :QK_NOPE_DIM], kv[..., QK_NOPE_DIM:]
        k_r = jnp.broadcast_to(k_rope[:, :, None, :], (B, T, H, QK_ROPE_DIM))
        k = jnp.concatenate([k_nope, k_r], axis=-1)
        q = rms_norm(q, g_qk_q[l])
        k = rms_norm(k, g_qk_k[l])
        q = jnp.concatenate([q[..., :QK_NOPE_DIM], apply_rope(q[..., QK_NOPE_DIM:], positions)], axis=-1)
        k = jnp.concatenate([k[..., :QK_NOPE_DIM], apply_rope(k[..., QK_NOPE_DIM:], positions)], axis=-1)
        attn = chunk_causal_attention(q, k, v).reshape(B, T, H * V_HEAD_DIM)
        y_a = jnp.matmul(attn, w_o_mla[l])

        c_val, c_gate = conv_in[..., :CONV_WIDTH], conv_in[..., CONV_WIDTH:]
        u = c_val * jax.nn.sigmoid(c_gate)
        u = causal_depthwise_conv(u, w_dw[l], b_dw[l])
        u = jax.nn.silu(layer_norm(u, g_conv_ln[l], b_conv_ln[l]))
        y_b = jnp.matmul(u, w_conv_out[l])

        gates = jax.nn.sigmoid(gate_logits + b_gates[l].astype(gate_logits.dtype))
        merged = gates[..., :D] * y_a + gates[..., D:] * y_b
        x = x + jnp.matmul(merged, w_out[l])

        h2 = rms_norm(x, g_ffn[l])
        x = x + hierarchical_moe(h2, w_group_router[l], b_group_router[l], w_expert_router[l],
                                 b_expert_router[l], w_e_gate[l], w_e_up[l], w_e_down[l])
    return x


_drawn_inputs = setup_inputs


def setup_inputs(seed=0):
    import zlib

    import numpy as np

    out = dict(_drawn_inputs(seed))
    spreads = {}
    factors = {'g_mix': 2.807,
     'g_q_lora': 6.095,
     'g_kv_lora': 7.642,
     'g_qk_q': 8.0,
     'g_qk_k': 5.027,
     'b_conv_ln': 22.512,
     'b_gates': 4.496,
     'b_group_router': 58.487,
     'b_expert_router': 29.288,
     'b_dw': 8.0,
     'g_conv_ln': 8.0,
     'g_ffn': 7.825}
    for name, (base, spread) in spreads.items():
        noise = np.random.default_rng([zlib.crc32(name.encode()), seed]).standard_normal(out[name].shape)
        drawn = base * np.exp(spread * noise) if base else spread * noise
        out[name] = __import__('jax').numpy.asarray(drawn.astype(out[name].dtype))
    for name, factor in factors.items():
        out[name] = (out[name] * factor).astype(out[name].dtype)
    return out
```

```python
import concourse.bass as bass
from concourse import mybir
from contextlib import ExitStack

F32 = mybir.dt.float32
F32R = mybir.dt.float32r
BF16 = mybir.dt.bfloat16
I32 = mybir.dt.int32
U32 = mybir.dt.uint32
ALU = mybir.AluOpType
ACT = mybir.ActivationFunctionType
AX = mybir.AxisListType

P = 128
D = 1024
T = 1024
NTILE = T // P
KD = D // P
HEADS, NOPE, ROPE, VD = 8, 64, 32, 64
QK = NOPE + ROPE
HALF = ROPE // 2
QL, KVL = 256, 128
DOWN = QL + KVL + ROPE
CW = 512
NC = CW // P
TAPS = 31
PAD = TAPS - 1
NG, EPG, FF = 4, 8, 256
NE = NG * EPG
EPS = 1e-6
CHUNK = 64
MASKED = -1e30
THETA = 10000.0
MAXB = 2 * T // P + NE
NBT = MAXB + 2
GLU_UNITS = 2 * NC
GATE_UNITS = 2 * D // P
IN_UNITS = GLU_UNITS + GATE_UNITS
OUT_UNITS = D // P
TAPS_PER_UNIT = 7
LN_UNIT = 20


def build(nc, x, positions, g_mix, w_in, g_q_lora, w_uq, g_kv_lora, w_ukv, g_qk_q, g_qk_k,
          w_o_mla, w_dw, b_dw, g_conv_ln, b_conv_ln, w_conv_out, b_gates, w_out, g_ffn,
          w_group_router, b_group_router, w_expert_router, b_expert_router,
          w_e_gate, w_e_up, w_e_down, out):
    K = 1024
    base = (nc.sbuf_base + 127) // 128 * 128
    at = {"top": base}

    def place(name, shape, dt, offset):
        return nc.alloc_sbuf_tensor_at(name, shape, dt, offset=offset)

    def room(nbytes):
        o = at["top"]
        at["top"] += (nbytes + 31) // 32 * 32
        assert at["top"] <= nc.sbuf_usable_end, at["top"]
        return o

    def small(name, shape, dt=F32):
        n = 2 if dt == BF16 else 4
        for s in shape[1:]:
            n *= s
        return place(name, shape, dt, room(n))

    R1 = room(64 * K)
    R2 = room(64 * K)
    R3 = room(32 * K)
    R6 = room(24 * K)
    hT = [place("hT_hi", [P, KD, T], F32R, R1), place("hT_lo", [P, KD, T], F32R, R1 + 32 * K)]
    xs = place("xs", [P, NTILE, D], F32, R2)
    xn = place("xn", [P, 2, D], F32, R2 + 32 * K)
    hp = place("hp", [P, 2, KD, P], F32, R2 + 40 * K)
    sqj = place("sqj", [P, D], F32, R2 + 48 * K)
    wdn_raw = place("wdn_raw", [P, KD, DOWN], F32, R6)
    wdn = [place("wdn_hi", [P, KD, DOWN], F32R, R3), place("wdn_lo", [P, KD, DOWN], F32R, R3 + 14 * K)]
    ws_raw = place("ws_raw", [P, 2, KD, P], F32, R6)
    ws = [place("ws_hi", [P, 2, KD, P], F32R, R6 + 8 * K), place("ws_lo", [P, 2, KD, P], F32R, R6 + 16 * K)]
    gates = place("gates", [P, 2 * KD, T], F32, R2)
    cv = place("cv", [P, NC, T], F32, R3)
    UW = T + PAD
    up = [place(f"up{c}", [P, UW], F32, o) for c, o in enumerate((R3 + 16 * K, R3 + 20 * K + 256, R2 + 48 * K, R2 + 56 * K))]
    sg = place("sg", [P, T], F32, R3 + 25 * K)
    QTO = room(8 * K)
    qT = place("qT", [P, 2, HEADS * P], F32, QTO)
    attnT = place("attnT", [P, 4, T], F32, R3 + 16 * K)
    kT = place("kT", [P, HEADS, T], F32, R1)
    vv = place("vv", [P, NTILE, HEADS * VD], F32, R1 + 32 * K)
    pr = place("pr", [P, 2, T], F32, R1 + 48 * K)
    pT = place("pT", [P, 2, T], F32, R1 + 56 * K)
    wuq = place("wuq", [P, 2, HEADS * QK], F32, R6)
    On = place("On", [P, HEADS * VD], F32, R6 + 6 * K)
    wukv = place("wukv", [P, HEADS * (NOPE + VD)], F32, R6 + 8 * K)
    qn = place("qn", [P, HEADS, QK], F32, R6 + 12 * K)
    kn = place("kn", [P, HEADS, QK], F32, R6 + 15 * K)
    sq2 = place("sq2", [P, HEADS, QK], F32, R6 + 18 * K)
    tmpr = place("tmpr", [P, HEADS, ROPE], F32, R6 + 21 * K)
    qdT = place("qdT", [P, 3, P], F32, R6 + 22 * K)
    lnt = [place(f"lnt{c}", [P, T], F32, o) for c, o in enumerate((QTO, QTO + 4 * K, R3 + 16 * K, R3 + 20 * K))]
    lnr = place("lnr", [P, T], F32, R3 + 25 * K)
    aT = [place("aT_hi", [P, 8, T], F32R, R1), place("aT_lo", [P, 8, T], F32R, R1 + 32 * K)]
    wout = place("wout", [P, KD, D], F32, R3)
    x1 = place("x1", [P, NTILE, D], F32, R1)
    xb = place("xb", [P, 2, D], F32, R1 + 32 * K)
    h2 = place("h2", [P, 2, D], F32, R1 + 40 * K)
    h2T = place("h2T", [P, 2, KD, P], F32, R1 + 48 * K)
    sq7 = place("sq7", [P, D], F32, R1 + 56 * K)
    gffb = place("gffb", [P, D], F32, R1 + 60 * K)
    wgu = [place(f"wgu{i}", [P, KD, 2 * FF], F32, R2 + 16 * K * i) for i in range(2)]
    wed = [place(f"wed{i}", [P, 2, D], F32, R2 + 32 * K + 8 * K * i) for i in range(2)]
    hg = [place(f"hg{i}", [P, D], F32, R2 + 48 * K + 4 * K * i) for i in range(2)]
    hgT = [place(f"hgT{i}", [P, KD, P], F32, R2 + 56 * K + 4 * K * i) for i in range(2)]
    yb = [place(f"yb{i}", [P, D], F32, R3 + 4 * K * i) for i in range(2)]
    sil = place("sil", [P, FF], F32, R3 + 8 * K)
    mid = place("mid", [P, FF], F32, R3 + 9 * K)
    midT = place("midT", [P, 2, P], F32, R3 + 10 * K)
    yg = [place(f"yg{i}", [P, 2, D], F32, R2 + 8 * K * i) for i in range(2)]
    ob = [place(f"ob{i}", [P, D], F32, R2 + 16 * K + 4 * K * i) for i in range(2)]

    qd = small("qd", [P, NTILE, DOWN])
    ident = small("ident", [P, P])
    mean_w = small("mean_w", [P, P])
    mrow = small("mrow", [1, 2, P], BF16)
    before = small("before", [P, P], BF16)
    ones_b = small("ones_b", [P, P], BF16)
    one_row = small("one_row", [1, P])
    vecs = place("vecs", [48, P], F32, R6 + 14 * K)
    V_GM, V_BG, V_BD, V_GL, V_BL, V_GQ, V_GK, V_NQ, V_NK = 0, 8, 24, 28, 32, 36, 38, 39, 40
    NV = 41
    vcol = small("vcol", [P, 48])
    dwr = place("dwr", [TAPS * NC, P], F32, R6 + 14 * K + 512)
    dwc = small("dwc", [P, TAPS * NC])
    posi = place("posi", [NTILE, P], I32, R6 + 15 * K)
    posf = place("posf", [NTILE, P], F32, R6 + 15 * K + 512)
    posc = small("posc", [P, NTILE])
    gqk = small("gqk", [P, 2, QK])
    invf = small("invf", [P, HALF])
    ang = place("ang", [P, NTILE, HALF], F32, R2 + 36 * K)
    turns = place("turns", [P, NTILE, HALF], F32, R2 + 36 * K + 512)
    sincos = small("sincos", [P, 2, NTILE, HALF])
    krr = small("krr", [P, NTILE, ROPE])
    krt = place("krt", [P, NTILE, ROPE], F32, R3 + 29 * K)
    rtab = small("rtab", [P, 2, NTILE, ROPE])
    ss1 = small("ss1", [P, NTILE])
    rs1 = small("rs1", [P, NTILE])
    ss3 = small("ss3", [P, 3, NTILE])
    ssh = small("ssh", [P, 2, HEADS])
    nmax = small("nmax", [P, 2])
    rsum = small("rsum", [P, 2, HEADS])
    rinv = small("rinv", [P, HEADS])
    wr = place("wr", [P, KD, NG + NE], F32, R6)
    br = place("br", [1, NG + NE], F32, R6 + 2 * K)
    lg = place("lg", [P, NTILE, NG], F32, R6 + 3 * K)
    le = place("le", [P, NTILE, NE], F32, R6 + 4 * K)
    pen = place("pen", [P, NTILE, NG], F32, R6 + 5 * K)
    tg = place("tg", [P, NTILE, NG], F32, R6 + 5 * K + 512)
    oh = [place(f"oh{i}", [P, NTILE, NE], F32, R3 + 12 * K + i * K) for i in range(2)]
    te = place("te", [P, NTILE, NE], F32, R3 + 14 * K)
    ab = small("ab", [P, NTILE, NE], BF16)
    s8 = [small(f"s8_{i}", [P, NTILE]) for i in range(6)]
    wt = small("wt", [P, 2, NTILE])
    pre = place("pre", [P, NTILE + 1, NE], F32, R3 + 17 * K)
    nb = small("nb", [P, NE])
    incl = small("incl", [P, NE])
    b128 = small("b128", [P, NE])
    rank = place("rank", [P, NTILE, NE], F32, R3 + 15 * K)
    cmp8 = place("cmp8", [P, NE, 8], F32, R3 + 16 * K)
    pos2 = small("pos2", [P, 2, NTILE])
    pidx = small("pidx", [P, 2, NTILE], I32)
    phi = small("phi", [P, 2, NTILE], I32)
    plo = small("plo", [P, 2, NTILE], I32)
    tidx = small("tidx", [P, 2, NTILE], I32)
    dst = small("dst", [P, 2, NTILE], I32)
    down4 = small("down4", [P, NG])
    down32 = small("down32", [P, NE])
    io8 = small("io8", [P, 8])
    iob = small("iob", [1, NBT])
    io2 = small("io2", [1, MAXB // 2])
    cmpb = place("cmpb", [1, NBT, NE], F32, R2 + 32 * K)
    cmp2 = small("cmp2", [1, MAXB // 2])
    bexp_f = small("bexp_f", [1, NBT])
    bexp = small("bexp", [1, NBT], I32)
    npair_f = small("npair_f", [1, 1])
    npair_i = small("npair_i", [1, 1], I32)
    zer = small("zer", [P, NBT], I32)
    srow = small("srow", [P, NBT], I32)
    stok = small("stok", [P, NBT], I32)
    icol = [small(f"icol{i}", [P, 1], I32) for i in range(2)]
    rcol = [small(f"rcol{i}", [P, 1], I32) for i in range(2)]
    eps = small("eps", [P, 1])
    mhalf = small("mhalf", [P, 2, HEADS])
    tick_a, tick_d, tick_p = [small(f"tick_{e}", [1, 2]) for e in "adp"]

    h2_d = nc.dram_tensor("h2_rows", (T, D), F32, kind="Internal").ap()
    y_d = nc.dram_tensor("y_rows", (2 * T, D), F32, kind="Internal").ap()
    first_d = nc.dram_tensor("first", (2, P), I32, kind="Internal").ap()
    slot_d = nc.dram_tensor("slot_tab", (P * NBT, 1), I32, kind="Internal").ap()
    slot_v = slot_d.rearrange("(p b) o -> p (b o)", p=P)

    pb = nc.alloc_psum_tensor("pb", [P, 8, 512], F32)

    def banks(a, n):
        return pb[:, a:a + n, :].rearrange("p b f -> p (b f)")

    ctx = ExitStack()
    with ctx:
        ctx.enter_context(nc.allow_non_contiguous_dma(reason="small per-channel vectors"))

        def sem(name):
            return ctx.enter_context(nc.semaphore(name))

        x_in = [sem(f"x_in{j}") for j in range(NTILE)]
        small_in = sem("small_in")
        late_in, gff_in = sem("late_in"), sem("gff_in")
        wdn_in, uq_in, zero_in = sem("wdn_in"), sem("uq_in"), sem("zero_in")
        ws_in = [sem("ws_in0"), sem("ws_in1")]
        wout_in = sem("wout_in")
        xb_in = [sem("xb_in0"), sem("xb_in1")]
        h2_out = [sem("h2_out0"), sem("h2_out1")]
        consts, ident_ok = sem("consts"), sem("ident_ok")
        vec_t, vec_c = sem("vec_t"), sem("vec_c")
        dch, ach, pch = sem("dve_chain"), sem("act_chain"), sem("pool_chain")
        s_ss, s_rs, s_xn, s_xt, s_hp, s_hi, s_lo = [sem(n) for n in
            ("sumsq", "rstd", "x_scaled", "x_transposed", "h_product", "h_hi", "h_lo")]
        dn_hi, dn_lo, dn_ps, dn_ev = [sem(n) for n in ("wdn_hi_ok", "wdn_lo_ok", "down_ps", "down_sb")]
        u_hi, u_lo, u_mm, u_ev = [sem(n) for n in ("unit_hi", "unit_lo", "unit_mm", "unit_ev")]
        u_sg = sem("glu_sigmoid")
        down_rs, head_ss, head_rs = sem("down_rstd"), sem("head_ss"), sem("head_rstd")
        conv_done = sem("conv_done")
        ss3_ok, qd_ok, sin_in, sin_ok, tab_ok = [sem(n) for n in ("ss3_ok", "qd_ok", "sin_in", "sin_ok", "tab_ok")]
        ln_mu, ln_d, ln_sq, ln_var, ln_sd, ln_y, ln_u = [sem(n) for n in ("ln_mu", "ln_d", "ln_sq", "ln_var", "ln_sd", "ln_y", "ln_u")]
        m_full, m_free = sem("misc_full"), sem("misc_free")
        qk_raw, qk_sq, qk_ok, qT_ok = [sem(n) for n in ("qk_raw", "qk_sq", "qk_ok", "qT_ok")]
        sc_ok, mx_ok, ex_ok, pt_ok, pt_a, pt_d, pv_ok = [sem(n) for n in
            ("scores", "row_max", "probs", "probs_T_ps", "probs_T_a", "probs_T_d", "pv")]
        on_ok = sem("attn_norm")
        sp_hi, sp_lo = sem("branch_hi"), sem("branch_lo")
        yab, yab_used, mg_ok = sem("branches_ps"), sem("branches_used"), sem("merged")
        x1_ps, x1_ok, ss7, rs7, h2_ok, h2t_ps, h2t_ok, lg_ps, lg_ok = [sem(n) for n in
            ("x1_ps", "x1_ok", "ss7", "rs7", "h2_ok", "h2T_ps", "h2T_ok", "logits_ps", "logits_ok")]
        r_in, r_exp, a_ok, rc_ps, route_ok = [sem(n) for n in ("r_in", "r_exp", "assign", "rank_ps", "route_ok")]
        scat, stok_in = sem("slots_scattered"), sem("slots_in")
        w_in0 = [sem("wgu_in0"), sem("wgu_in1")]
        w_in1 = [sem("wed_in0"), sem("wed_in1")]
        ic_ok, hg_zero = sem("index_col"), sem("hg_zero")
        hg_in = [sem("hg_in0"), sem("hg_in1")]
        hgt_ps, hgt_ok, gu_ps, sil_ok, mid_ok, mt_ps, mt_ok, y_ps, y_a, y_d_ok = [sem(n) for n in
            ("hgT_ps", "hgT_ok", "gate_up", "silu", "mid", "midT_ps", "midT_ok", "y_ps", "y_sb_a", "y_sb_d")]
        y_out = [sem("y_out0"), sem("y_out1")]
        y_all = sem("y_all")
        yg_in = [sem(f"yg_in{i}") for i in range(2)]
        ob_ok = sem("ob_ok")
        o_out = [sem("o_out0"), sem("o_out1")]

        x_v = x[0].rearrange("(j p) d -> j p d", p=P)
        out_v = out[0].rearrange("(j p) d -> j p d", p=P)
        win_v = w_in[0].rearrange("(k p) c -> p k c", p=P)
        wo_v = w_o_mla[0].rearrange("(k p) c -> p k c", p=P)
        wco_v = w_conv_out[0].rearrange("(k p) c -> p k c", p=P)

        def unit_col(u):
            if u < GLU_UNITS:
                return DOWN + (CW if u % 2 == 0 else 0) + (u // 2) * P
            return DOWN + 2 * CW + (u - GLU_UNITS) * P

        PREP = ["qdT", "q0", "q1", "kv0", "kv1", "qT0", "qT1", "kT0", "kT1"]

        def slots(j, h, part):
            got = [("oT", j - 1)] if (h, part) == (2, 1) and j else []
            nxt = {(0, 0): "qdT", (0, 1): "q0", (1, 0): "q1", (1, 1): "kv0", (2, 0): "kv1",
                   (4, 1): "qT0", (5, 0): "qT1", (5, 1): "kT0", (6, 0): "kT1"}
            return got + ([(nxt[h, part], j + 1)] if j + 1 < NTILE and (h, part) in nxt else [])

        order = [(k, 0) for k in PREP]
        for j in range(NTILE):
            for h in range(HEADS):
                order += slots(j, h, 0) + slots(j, h, 1)
        order.append(("oT", NTILE - 1))
        at_stage = {s: i for i, s in enumerate(order)}

        block = ctx.enter_context(nc.Block())

        @block.sync
        def _(sp):
            sp.dma_start(xs[:, 0, :], x_v[0]).then_inc(x_in[0], 16)
            for row, src, n in ((V_GM, g_mix, 8), (V_BG, b_gates, 16), (V_BD, b_dw, 4),
                                (V_GL, g_conv_ln, 4), (V_BL, b_conv_ln, 4), (V_GQ, g_q_lora, 2),
                                (V_GK, g_kv_lora, 1)):
                sp.dma_start(vecs[row:row + n, :], src[0].rearrange("(a p) -> a p", p=P)).then_inc(small_in, 16)
            for row, src in ((V_NQ, g_qk_q), (V_NK, g_qk_k)):
                for half in range(2):
                    sp.dma_start(vecs[row:row + 1, half * NOPE:(half + 1) * NOPE], src[:, 0:NOPE]).then_inc(small_in, 16)
            sp.dma_start(dwr[:, :], w_dw[0].rearrange("t (c p) -> (t c) p", p=P)).then_inc(small_in, 16)
            sp.dma_start(posi[:, :], positions[0].rearrange("(a p) -> a p", p=P)).then_inc(small_in, 16)
            for j in range(1, NTILE):
                sp.dma_start(xs[:, j, :], x_v[j]).then_inc(x_in[j], 16)
            sp.dma_start(wdn_raw[:, :, :], win_v[:, :, 0:DOWN]).then_inc(wdn_in, 16)
            sp.dma_start(gqk[:, 0, :], g_qk_q[0].partition_broadcast(P)).then_inc(late_in, 16)
            sp.dma_start(gqk[:, 1, :], g_qk_k[0].partition_broadcast(P)).then_inc(late_in, 16)
            sp.wait_ge(consts, 1)
            sp.dma_start(slot_v, zer[:, :]).then_inc(zero_in, 16)
            sp.wait_ge(dn_hi, 1)
            sp.wait_ge(dn_lo, 1)
            for u in range(IN_UNITS):
                if u >= 2:
                    sp.wait_ge(u_hi, u - 1)
                    sp.wait_ge(u_lo, u - 1)
                sp.dma_start(ws_raw[:, u % 2, :, :], win_v[:, :, unit_col(u):unit_col(u) + P]).then_inc(ws_in[u % 2], 16)
            sp.wait_ge(u_hi, IN_UNITS)
            sp.wait_ge(u_lo, IN_UNITS)
            sp.dma_start(wuq[:, :, :], w_uq[0].rearrange("(k p) c -> p k c", p=P)).then_inc(uq_in, 16)
            sp.wait_ge(u_mm, IN_UNITS - 1)
            sp.dma_start(wukv[:, :], w_ukv[0]).then_inc(uq_in, 16)
            sp.wait_ge(m_free, len(order))
            for c in range(OUT_UNITS):
                u = IN_UNITS + c
                if c >= 2:
                    sp.wait_ge(u_hi, u - 1)
                    sp.wait_ge(u_lo, u - 1)
                sp.dma_start(ws_raw[:, u % 2, 0:4, :], wo_v[:, :, c * P:(c + 1) * P]).then_inc(ws_in[u % 2], 16)
                sp.dma_start(ws_raw[:, u % 2, 4:8, :], wco_v[:, :, c * P:(c + 1) * P]).then_inc(ws_in[u % 2], 16)
                if c == 1:
                    sp.wait_ge(sp_hi, 4)
                    sp.wait_ge(sp_lo, 4)
                    sp.dma_start(wout[:, :, :], w_out[0].rearrange("(k p) c -> p k c", p=P)).then_inc(wout_in, 16)
            sp.wait_ge(u_mm, IN_UNITS + OUT_UNITS)
            sp.dma_start(wr[:, :, 0:NG], w_group_router[0].rearrange("(k p) c -> p k c", p=P)).then_inc(gff_in, 16)
            sp.dma_start(wr[:, :, NG:NG + NE], w_expert_router[0].rearrange("(k p) c -> p k c", p=P)).then_inc(gff_in, 16)
            sp.dma_start(br[:, 0:NG], b_group_router).then_inc(gff_in, 16)
            sp.dma_start(br[:, NG:NG + NE], b_expert_router).then_inc(gff_in, 16)
            sp.dma_start(gffb[:, :], g_ffn[0].partition_broadcast(P)).then_inc(gff_in, 16)
            for j in range(NTILE + 1):
                if j < NTILE:
                    if j >= 2:
                        sp.wait_ge(x1_ok, j - 1)
                    sp.dma_start(xb[:, j % 2, :], x_v[j]).then_inc(xb_in[j % 2], 16)
                if j >= 1:
                    sp.wait_ge(h2_ok, j)
                    sp.dma_start(h2_d[(j - 1) * P:j * P, :], h2[:, (j - 1) % 2, :]).then_inc(h2_out[(j - 1) % 2], 16)
            sp.wait_ge(route_ok, 1)
            npair = sp.value_load(npair_i[0:1, 0:1], min_val=2, max_val=MAXB // 2)

            def load_expert(b, e, used):
                if used is not None:
                    sp.wait_ge(gu_ps, used)
                sp.dma_start(wgu[b][:, :, 0:FF], w_e_gate[0][bass.ds(e, 1), :, :].rearrange("e (k p) f -> p (e k) f", p=P)).then_inc(w_in0[b], 16)
                sp.dma_start(wgu[b][:, :, FF:2 * FF], w_e_up[0][bass.ds(e, 1), :, :].rearrange("e (k p) f -> p (e k) f", p=P)).then_inc(w_in0[b], 16)
                if used is not None:
                    sp.wait_ge(y_ps, used)
                sp.dma_start(wed[b][:, :, :], w_e_down[0][bass.ds(e, 1), :, :].rearrange("e (k p) f -> p (e k) f", p=P)).then_inc(w_in1[b], 16)

            for b in range(2):
                load_expert(b, sp.value_load(bexp[0:1, b:b + 1], min_val=0, max_val=NE - 1), None)
            with sp.Fori(0, npair - 1) as i:
                for b in range(2):
                    e = sp.value_load(bexp[0:1, bass.ds(i * 2 + (b + 2), 1)], min_val=0, max_val=NE - 1)
                    load_expert(b, e, i * 2 + (b + 1))
            sp.wait_ge(y_all, 2)
            y_v = y_d.rearrange("(j p c) d -> j p c d", p=P, c=2)
            for j in range(NTILE + 1):
                if j < NTILE:
                    if j >= 2:
                        sp.wait_ge(ob_ok, j - 1)
                    sp.dma_start(yg[j % 2][:, :, :], y_v[j]).then_inc(yg_in[j % 2], 16)
                if j >= 1:
                    sp.wait_ge(ob_ok, j)
                    sp.dma_start(out_v[j - 1], ob[(j - 1) % 2][:, :]).then_inc(o_out[(j - 1) % 2], 16)
            for i in range(2):
                sp.wait_ge(o_out[i], 16 * NTILE // 2)

        @block.gpsimd
        def _(pool):
            g = nc.gpsimd
            n = [0]

            def link(ins):
                n[0] += 1
                ins.then_inc(pch, 1)
                pool.wait_ge(pch, n[0])

            g.memset(zer[:, :], 2 * T).then_inc(consts, 1)
            link(g.memset(ident[:, :], 0.0))
            g.affine_select(out=ident[:, :], in_=ident[:, :], compare_op=ALU.not_equal, fill=1.0, base=0,
                            pattern=[[-1, P]], channel_multiplier=1).then_inc(ident_ok, 1)
            g.memset(mean_w[:, :], 1.0 / CW)
            g.memset(tick_a[:, :], 0.0)
            g.memset(eps[:, :], EPS)
            g.memset(mhalf[:, :, :], -0.5)
            g.memset(tick_p[:, :], 0.0)
            for f in range(HALF):
                g.memset(invf[:, f:f + 1], float(THETA ** (-f / HALF)))
            g.memset(ones_b[:, :], 1.0)
            g.memset(one_row[:, :], 1.0)
            link(g.memset(before[:, :], 0.0))
            g.affine_select(out=before[:, :], in_=before[:, :], compare_op=ALU.is_ge, fill=1.0, base=0,
                            pattern=[[-1, P]], channel_multiplier=1)
            link(g.memset(mrow[:, :, :], 0.0))
            g.memset(mrow[:, 0, 0:CHUNK], 1.0)
            g.memset(mrow[:, 1, CHUNK:P], MASKED)
            g.iota(dst[:, :, :], pattern=[[1, 2], [2 * P, NTILE]], base=0, channel_multiplier=2)
            g.iota(down4[:, :], pattern=[[-1, NG]], base=NG, channel_multiplier=0, allow_small_or_imprecise_dtypes=True)
            g.iota(down32[:, :], pattern=[[-1, NE]], base=NE, channel_multiplier=0, allow_small_or_imprecise_dtypes=True)
            g.iota(io8[:, :], pattern=[[P, 8]], base=0, channel_multiplier=0, allow_small_or_imprecise_dtypes=True)
            g.iota(iob[:, :], pattern=[[1, NBT]], base=0, channel_multiplier=0, allow_small_or_imprecise_dtypes=True)
            g.iota(io2[:, :], pattern=[[2, MAXB // 2]], base=0, channel_multiplier=0, allow_small_or_imprecise_dtypes=True).then_inc(consts, 1)

            def rstd(dst, src, count, power):
                link(g.tensor_scalar(dst, src, 1.0 / count, EPS, ALU.mult, ALU.add))
                return g.tensor_tensor(dst, dst, power, ALU.pow)

            for j in range(NTILE):
                pool.wait_ge(s_ss, j + 1)
                rstd(rs1[:, j:j + 1], ss1[:, j:j + 1], D, mhalf[:, 0, 0:1]).then_inc(s_rs, 1)
            pool.wait_ge(ss3_ok, NTILE)
            for c, width in enumerate((QL, KVL)):
                rstd(ss3[:, c, :], ss3[:, c, :], width, mhalf[:, 0, :]).then_inc(down_rs, 1)
            for t in range(NTILE):
                pool.wait_ge(head_ss, 2 * t + 1)
                link(rstd(ssh[:, 0, :], ssh[:, 0, :], QK, mhalf[:, 0, :]))
                link(g.tensor_tensor(qn[:, :, :], qn[:, :, :], ssh[:, 0, :].unsqueeze(2).broadcast_to([P, HEADS, QK]), ALU.mult))
                rot = qn[:, :, NOPE:QK]
                if t == 0:
                    pool.wait_ge(tab_ok, 1)
                g.tensor_tensor(tmpr[:, :, 0:HALF], rot[:, :, HALF:ROPE], rtab[:, 1, t:t + 1, 0:HALF].broadcast_to([P, HEADS, HALF]), ALU.mult)
                link(g.tensor_tensor(tmpr[:, :, HALF:ROPE], rot[:, :, 0:HALF], rtab[:, 1, t:t + 1, HALF:ROPE].broadcast_to([P, HEADS, HALF]), ALU.mult))
                link(g.tensor_tensor(rot, rot, rtab[:, 0, t:t + 1, :].broadcast_to([P, HEADS, ROPE]), ALU.mult))
                g.tensor_tensor(rot, rot, tmpr[:, :, :], ALU.add).then_inc(qk_ok, 1)
                pool.wait_ge(head_ss, 2 * t + 2)
                link(rstd(ssh[:, 1, :], ssh[:, 1, :], QK, mhalf[:, 0, :]))
                g.tensor_tensor(kn[:, :, 0:NOPE], kn[:, :, 0:NOPE], ssh[:, 1, :].unsqueeze(2).broadcast_to([P, HEADS, NOPE]), ALU.mult)
                g.tensor_tensor(kn[:, :, NOPE:QK], krr[:, t:t + 1, :].broadcast_to([P, HEADS, ROPE]),
                                ssh[:, 1, :].unsqueeze(2).broadcast_to([P, HEADS, ROPE]), ALU.mult).then_inc(qk_ok, 1)
            for j in range(NTILE):
                pool.wait_ge(ss7, j + 1)
                rstd(rs1[:, j:j + 1], ss1[:, j:j + 1], D, mhalf[:, 0, 0:1]).then_inc(rs7, 1)
            pool.wait_ge(route_ok, 1)
            pool.wait_ge(zero_in, 16)
            for c in range(2):
                for j in range(NTILE):
                    g.indirect_dma_start(out=slot_d, out_offset=bass.IndirectOffsetOnAxis(ap=tidx[:, c, j:j + 1].bitcast(U32), axis=0),
                                         in_=dst[:, c, j:j + 1], in_offset=None).then_inc(scat, 16)
            pool.wait_ge(scat, 16 * 2 * NTILE)
            pool.dma_start(srow[:, :], slot_v).then_inc(stok_in, 16)
            npair = pool.value_load(npair_i[0:1, 0:1], min_val=1, max_val=MAXB // 2)
            for i in range(2):
                pool.wait_ge(h2_out[i], 16 * NTILE // 2)
            for b in range(2):
                pool.dma_start(first_d[b:b + 1, :].rearrange("a p -> p a"), zer[:, 0:1]).then_inc(y_out[b], 16)

            def gather(b, count):
                pool.wait_ge(ic_ok, count)
                pool.sem_inc(pch, 1)
                g.indirect_dma_start(out=hg[b][:, :], out_offset=None, in_=h2_d,
                                     in_offset=bass.IndirectOffsetOnAxis(ap=icol[b][:, 0:1].bitcast(U32), axis=0),
                                     bounds_check=T - 1, oob_is_err=False).then_inc(hg_in[b], 16)

            def scatter(b, count):
                pool.wait_ge(y_a, count + 1)
                pool.sem_inc(pch, 1)
                pool.wait_ge(y_d_ok, count + 1)
                pool.sem_inc(pch, 1)
                g.indirect_dma_start(out=y_d, out_offset=bass.IndirectOffsetOnAxis(ap=rcol[b][:, 0:1].bitcast(U32), axis=0),
                                     in_=yb[b][:, :], in_offset=None,
                                     bounds_check=2 * T - 1, oob_is_err=False).then_inc(y_out[b], 16)

            pool.wait_ge(hg_zero, 2)
            gather(0, 1)
            with pool.Fori(0, npair) as i:
                gather(1, i * 2 + 2)
                scatter(0, i * 2 + 1)
                gather(0, i * 2 + 3)
                scatter(1, i * 2 + 2)
            for b in range(2):
                pool.wait_ge(y_out[b], npair * 16 + 16)
                pool.sem_inc(y_all, 1)

        @block.scalar
        def _(act):
            a = nc.scalar

            def sumsq(j):
                act.wait_ge(x_in[j], 16)
                if j:
                    act.wait_ge(s_ss, j)
                a.activation(sqj[:, :], xs[:, j, :], ACT.Square, accum_out=ss1[:, j:j + 1]).then_inc(s_ss, 1)

            sumsq(0)
            for j in range(NTILE):
                if j + 1 < NTILE:
                    sumsq(j + 1)
                act.wait_ge(s_rs, j + 1)
                if j >= 2:
                    act.wait_ge(s_xt, j - 1)
                a.activation(xn[:, j % 2, :], xs[:, j, :], ACT.Copy, scale=rs1[:, j:j + 1]).then_inc(s_xn, 1)
                act.wait_ge(s_hp, j + 1)
                a.activation(hT[0][:, :, j * P:(j + 1) * P], hp[:, j % 2, :, :], ACT.Copy).then_inc(s_hi, 1)
            act.wait_ge(wdn_in, 16)
            act.wait_ge(s_ss, NTILE)
            a.activation(wdn[0][:, :, :], wdn_raw[:, :, :], ACT.Copy).then_inc(dn_hi, 1)
            for j in range(NTILE):
                act.wait_ge(dn_ps, j + 1)
                a.activation(qd[:, j, :], pb[:, j % 2, 0:DOWN], ACT.Copy).then_inc(dn_ev, 1)
                act.wait_ge(dn_ev, j + 1)
                if j:
                    act.wait_ge(ss3_ok, j)
                for s, (lo, hi) in enumerate(((0, QL), (QL, QL + KVL), (QL + KVL, DOWN))):
                    i = a.activation(sqj[:, lo:hi], qd[:, j, lo:hi], ACT.Square, accum_out=ss3[:, s, j:j + 1])
                i.then_inc(ss3_ok, 1)

            def unit_hi(u):
                act.wait_ge(ws_in[u % 2], 16 * (u // 2 + 1) if u < IN_UNITS else 16 * (IN_UNITS // 2) + 32 * ((u - IN_UNITS) // 2 + 1))
                if u >= 2:
                    act.wait_ge(u_mm, u - 1)
                a.activation(ws[0][:, u % 2, :, :], ws_raw[:, u % 2, :, :], ACT.Copy).then_inc(u_hi, 1)

            unit_hi(0)
            unit_hi(1)
            for u in range(IN_UNITS):
                act.wait_ge(u_mm, u + 1)
                src = banks(2 * (u % 2) + 2, 2)
                if u < GLU_UNITS:
                    if u % 2 == 0:
                        if u >= 2:
                            act.wait_ge(u_ev, u)
                        a.activation(sg[:, :], src, ACT.Sigmoid).then_inc(u_ev, 1)
                else:
                    c = u - GLU_UNITS
                    if c == 0:
                        act.wait_ge(u_ev, GLU_UNITS)
                    if c in (12, 14):
                        act.wait_ge(conv_done, c // 2 - 3)
                    a.activation(gates[:, c, :], src, ACT.Sigmoid, bias=vcol[:, V_BG + c:V_BG + c + 1]).then_inc(u_ev, 1)
                if u + 2 < IN_UNITS:
                    unit_hi(u + 2)
                if u == 1:
                    act.wait_ge(sin_in, 1)
                    a.activation(sincos[:, :, :, :], sincos[:, :, :, :], ACT.Sin).then_inc(sin_ok, 1)
                if u == LN_UNIT:
                    for c in range(NC):
                        act.wait_ge(ln_d, c + 1)
                        a.activation(lnt[c][:, :], cv[:, c, :], ACT.Square).then_inc(ln_sq, 1)
                if u == LN_UNIT + 1:
                    act.wait_ge(ln_var, 1)
                    a.activation(lnr[:, :], banks(6, 2), ACT.Sqrt, bias=eps[:, :]).then_inc(ln_sd, 1)
                if u == LN_UNIT + 2:
                    for c in range(NC):
                        act.wait_ge(ln_y, c + 1)
                        a.activation(cv[:, c, :], cv[:, c, :], ACT.Silu, scale=vcol[:, V_GL + c:V_GL + c + 1],
                                     bias=vcol[:, V_BL + c:V_BL + c + 1]).then_inc(ln_u, 1)

            def misc(kind, t):
                s = at_stage[kind, t]
                M = pb[:, 7, :]
                if kind in ("q0", "q1"):
                    act.wait_ge(m_full, s + 1)
                    h = 4 * (kind == "q1")
                    a.activation(qn[:, h:h + 4, :], M[:, 0:4 * QK].rearrange("p (h c) -> p h c", h=4), ACT.Copy).then_inc(m_free, 1)
                    if kind == "q1":
                        act.wait_ge(m_free, s + 1)
                        if t:
                            act.wait_ge(head_ss, 2 * t)
                        a.activation(sq2[:, :, :], qn[:, :, :], ACT.Square).then_inc(qk_sq, 1)
                if kind in ("kv0", "kv1"):
                    act.wait_ge(m_full, s + 1)
                    h = 4 * (kind == "kv1")
                    kv = M.rearrange("p (h c) -> p h c", h=4)
                    a.activation(kn[:, h:h + 4, 0:NOPE], kv[:, :, 0:NOPE], ACT.Copy)
                    a.activation(vv[:, t, h * VD:(h + 4) * VD].rearrange("p (h c) -> p h c", h=4), kv[:, :, NOPE:], ACT.Copy).then_inc(m_free, 1)
                    if kind == "kv1":
                        act.wait_ge(m_free, s + 1)
                        act.wait_ge(head_ss, 2 * t + 1)
                        a.activation(sq2[:, :, 0:NOPE], kn[:, :, 0:NOPE], ACT.Square).then_inc(qk_sq, 1)
                if kind in ("qT0", "qT1"):
                    act.wait_ge(m_full, s + 1)
                    h = 4 * (kind == "qT1")
                    a.activation(qT[0:QK, t % 2, h * P:(h + 4) * P], M[0:QK, :], ACT.Copy, scale=vcol[0:QK, V_NQ:V_NQ + 1]).then_inc(m_free, 1)
                if kind == "oT":
                    act.wait_ge(m_full, s + 1)
                    a.activation(attnT[:, :, t * P:(t + 1) * P], M.rearrange("p (c t) -> p c t", c=4), ACT.Copy).then_inc(m_free, 1)

            def exps(n):
                j, h = divmod(n, HEADS)
                w = (j + 1) * P
                act.wait_ge(mx_ok, n + 1)
                if n >= 2:
                    act.wait_ge(pt_ok, n - 1)
                a.activation(pr[:, n % 2, 0:w], banks(2 * (n % 2), 2)[:, 0:w], ACT.Exp,
                             bias=nmax[:, n % 2:n % 2 + 1], accum_out=rsum[:, j % 2, h:h + 1]).then_inc(ex_ok, 1)

            for k in PREP:
                misc(k, 0)
            exps(0)
            exps(1)
            for n in range(NTILE * HEADS):
                j, h = divmod(n, HEADS)
                if j >= 4:
                    act.wait_ge(pt_ok, n + 1)
                    act.wait_ge(pv_ok, n - 1)
                    a.activation(pT[:, n % 2, 512:(j + 1) * P], banks(5, 1)[:, 0:(j + 1) * P - 512], ACT.Copy).then_inc(pt_a, 1)
                for k, t in slots(j, h, 0):
                    misc(k, t)
                if n + 2 < NTILE * HEADS:
                    exps(n + 2)
                for k, t in slots(j, h, 1):
                    misc(k, t)
            misc("oT", NTILE - 1)

            act.wait_ge(pv_ok, NTILE * HEADS)
            act.wait_ge(m_free, len(order))
            for c in range(2):
                a.activation(aT[0][:, 4 + 2 * c:6 + 2 * c, :], cv[:, 2 * c:2 * c + 2, :], ACT.Copy).then_inc(sp_hi, 1)
            for c in range(2):
                a.activation(aT[0][:, 2 * c:2 * c + 2, :], attnT[:, 2 * c:2 * c + 2, :], ACT.Copy).then_inc(sp_hi, 1)
            for c in range(OUT_UNITS):
                unit_hi(IN_UNITS + c)
            def half_two(j):
                act.wait_ge(h2t_ps, j + 1)
                if j >= 2:
                    act.wait_ge(lg_ps, j - 1)
                a.activation(h2T[:, j % 2, :, :], banks(4, 2).rearrange("p (k t) -> p k t", k=KD), ACT.Copy).then_inc(h2t_ok, 1)

            for j in range(NTILE):
                act.wait_ge(x1_ok, j + 1)
                if j:
                    act.wait_ge(ss7, j)
                a.activation(sq7[:, :], x1[:, j, :], ACT.Square, accum_out=ss1[:, j:j + 1]).then_inc(ss7, 1)
                if j >= 1:
                    half_two(j - 1)
            half_two(NTILE - 1)
            for k in range(2):
                act.wait_ge(r_in, k + 1)
                if k == 0:
                    a.activation(tg[:, :, :], tg[:, :, :], ACT.Exp).then_inc(r_exp, 1)
                else:
                    a.activation(s8[3][:, :], s8[3][:, :], ACT.Exp).then_inc(r_exp, 1)

            act.wait_ge(route_ok, 1)
            npair = act.value_load(npair_i[0:1, 0:1], min_val=1, max_val=MAXB // 2)
            with act.Fori(0, npair) as i:
                for b in range(2):
                    act.wait_ge(gu_ps, i * 2 + (b + 1))
                    a.activation(sil[:, :], pb[:, 2, 0:FF], ACT.Silu).then_inc(sil_ok, 1)
                    act.wait_ge(y_ps, i * 2 + (b + 1))
                    act.wait_ge(y_out[b], i * 16 + 16)
                    a.activation(yb[b][:, 0:512], pb[:, 4, :], ACT.Copy).then_inc(y_a, 1)
        @block.vector
        def _(dve):
            v = nc.vector
            n = [0]

            def link(ins):
                n[0] += 1
                ins.then_inc(dch, 1)
                dve.wait_ge(dch, n[0])

            dve.wait_ge(consts, 2)
            dve.wait_ge(small_in, 16 * 13)
            link(v.tensor_copy(posf[:, :], posi[:, :]))
            v.tensor_copy(posf[:, :], posf[:, :]).then_inc(vec_c, 1)
            dve.wait_ge(vec_t, 1)
            v.tensor_copy(vcol[:, 0:NV], pb[:, 6, 0:NV])
            v.tensor_copy(dwc[:, :], pb[:, 6, 64:64 + TAPS * NC])
            link(v.tensor_copy(posc[:, :], pb[:, 6, 256:256 + NTILE]))
            v.memset(vcol[NOPE:P, V_NQ:V_NQ + 2], 1.0)
            v.tensor_scalar(vcol[0:NOPE, V_NQ:V_NQ + 1], vcol[0:NOPE, V_NQ:V_NQ + 1], QK ** -0.5, None, ALU.mult)

            for j in range(NTILE):
                dve.wait_ge(s_xt, j + 1)
                if j >= 2:
                    dve.wait_ge(s_hi, j - 1)
                    dve.wait_ge(s_lo, j - 1)
                v.tensor_tensor(hp[:, j % 2, :, :], banks(2 * (j % 2), 2).rearrange("p (k t) -> p k t", k=KD),
                                vcol[:, V_GM:V_GM + KD].unsqueeze(2).broadcast_to([P, KD, P]), ALU.mult).then_inc(s_hp, 1)
                dve.wait_ge(s_hi, j + 1)
                v.tensor_tensor(hT[1][:, :, j * P:(j + 1) * P], hp[:, j % 2, :, :],
                                hT[0][:, :, j * P:(j + 1) * P].bitcast(F32), ALU.subtract).then_inc(s_lo, 1)
            dve.wait_ge(dn_hi, 1)
            v.tensor_tensor(wdn[1][:, :, :], wdn_raw[:, :, :], wdn[0][:, :, :].bitcast(F32), ALU.subtract).then_inc(dn_lo, 1)

            def unit_lo(u):
                dve.wait_ge(u_hi, u + 1)
                if u >= 2:
                    dve.wait_ge(u_mm, u - 1)
                v.tensor_tensor(ws[1][:, u % 2, :, :], ws_raw[:, u % 2, :, :], ws[0][:, u % 2, :, :].bitcast(F32), ALU.subtract).then_inc(u_lo, 1)

            def tap(k):
                c, t = divmod(k, TAPS)
                w = dwc[:, t * NC + c:t * NC + c + 1]
                src = up[c][:, t:t + T]
                if t == 0:
                    link(v.tensor_scalar(cv[:, c, :], src, w, vcol[:, V_BD + c:V_BD + c + 1], ALU.mult, ALU.add))
                else:
                    i = v.scalar_tensor_tensor(out=cv[:, c, :], in0=src, scalar=w, in1=cv[:, c, :], op0=ALU.mult, op1=ALU.add)
                    if t < TAPS - 1:
                        link(i)
                    else:
                        i.then_inc(conv_done, 1)

            def rotary_angles():
                dve.wait_ge(late_in, 16 * 2)
                link(v.tensor_scalar(gqk[:, 0, :], gqk[:, 0, :], QK ** -0.5, None, ALU.mult))
                link(v.tensor_tensor(ang[:, :, :], posc[:, :].unsqueeze(2).broadcast_to([P, NTILE, HALF]),
                                     invf[:, :].unsqueeze(1).broadcast_to([P, NTILE, HALF]), ALU.mult))
                TWO_PI = 6.283185307179586
                link(v.tensor_scalar(turns[:, :, :], ang[:, :, :], 1.0 / TWO_PI, 12582912.0, ALU.mult, ALU.add))
                link(v.tensor_scalar(turns[:, :, :], turns[:, :, :], 12582912.0, None, ALU.subtract))
                left = TWO_PI
                for bits in (-5, -14, -23):
                    part = float(int(left / 2.0 ** bits)) * 2.0 ** bits
                    left -= part
                    link(v.scalar_tensor_tensor(out=ang[:, :, :], in0=turns[:, :, :], scalar=-part, in1=ang[:, :, :], op0=ALU.mult, op1=ALU.add))
                link(v.scalar_tensor_tensor(out=ang[:, :, :], in0=turns[:, :, :], scalar=-left, in1=ang[:, :, :], op0=ALU.mult, op1=ALU.add))
                PI = 3.1415925
                link(v.tensor_scalar(turns[:, :, :], ang[:, :, :], TWO_PI / 4, TWO_PI / 2, ALU.add, ALU.is_gt))
                link(v.scalar_tensor_tensor(out=turns[:, :, :], in0=turns[:, :, :], scalar=-TWO_PI, in1=ang[:, :, :], op0=ALU.mult, op1=ALU.add))
                link(v.tensor_scalar(turns[:, :, :], turns[:, :, :], TWO_PI / 4, PI, ALU.add, ALU.min))
                link(v.tensor_scalar(sincos[:, 1, :, :], turns[:, :, :], -PI, None, ALU.max))
                v.tensor_scalar(sincos[:, 0, :, :], ang[:, :, :], PI, -PI, ALU.min, ALU.max).then_inc(sin_in, 1)

            def rotary_tables():
                dve.wait_ge(sin_ok, 1)
                sin, cos = sincos[:, 0, :, :], sincos[:, 1, :, :]

                def gain(w, half):
                    return gqk[:, w, NOPE + half * HALF:NOPE + (half + 1) * HALF].unsqueeze(1).broadcast_to([P, NTILE, HALF])

                v.tensor_tensor(rtab[:, 0, :, 0:HALF], cos, gain(0, 0), ALU.mult)
                v.tensor_tensor(rtab[:, 0, :, HALF:ROPE], cos, gain(0, 1), ALU.mult)
                v.scalar_tensor_tensor(out=rtab[:, 1, :, 0:HALF], in0=sin, scalar=-1.0, in1=gain(0, 1), op0=ALU.mult, op1=ALU.mult)
                v.tensor_tensor(rtab[:, 1, :, HALF:ROPE], sin, gain(0, 0), ALU.mult)
                link(v.tensor_tensor(krr[:, :, :], qd[:, :, QL + KVL:DOWN], gqk[:, 1, NOPE:QK].unsqueeze(1).broadcast_to([P, NTILE, ROPE]), ALU.mult))
                v.tensor_tensor(krt[:, :, 0:HALF], krr[:, :, HALF:ROPE], sin, ALU.mult)
                link(v.tensor_tensor(krt[:, :, HALF:ROPE], krr[:, :, 0:HALF], sin, ALU.mult))
                v.tensor_tensor(krr[:, :, 0:HALF], krr[:, :, 0:HALF], cos, ALU.mult)
                link(v.tensor_tensor(krr[:, :, HALF:ROPE], krr[:, :, HALF:ROPE], cos, ALU.mult))
                v.tensor_tensor(krr[:, :, 0:HALF], krr[:, :, 0:HALF], krt[:, :, 0:HALF], ALU.subtract)
                v.tensor_tensor(krr[:, :, HALF:ROPE], krr[:, :, HALF:ROPE], krt[:, :, HALF:ROPE], ALU.add).then_inc(tab_ok, 1)

            unit_lo(0)
            unit_lo(1)
            taps_done = 0
            for u in range(IN_UNITS):
                if u == 0:
                    dve.wait_ge(down_rs, 2)
                    v.tensor_tensor(qd[:, :, 0:QL], qd[:, :, 0:QL], ss3[:, 0, :].unsqueeze(2).broadcast_to([P, NTILE, QL]), ALU.mult)
                    v.tensor_tensor(qd[:, :, QL:QL + KVL], qd[:, :, QL:QL + KVL], ss3[:, 1, :].unsqueeze(2).broadcast_to([P, NTILE, KVL]), ALU.mult).then_inc(qd_ok, 1)
                if u < GLU_UNITS and u % 2 == 1:
                    dve.wait_ge(u_mm, u + 1)
                    dve.wait_ge(u_ev, u)
                    v.memset(up[u // 2][:, 0:PAD], 0.0)
                    v.tensor_tensor(up[u // 2][:, PAD:UW], banks(2 * (u % 2) + 2, 2), sg[:, :], ALU.mult).then_inc(u_ev, 1)
                    dve.wait_ge(u_ev, u + 1)
                if u + 2 < IN_UNITS:
                    unit_lo(u + 2)
                target = min(TAPS * NC, TAPS_PER_UNIT * u)
                if u < GLU_UNITS:
                    target = min(target, TAPS * ((u + 1) // 2))
                for k in range(taps_done, target):
                    tap(k)
                taps_done = max(taps_done, target)
                if u == 1:
                    rotary_angles()
                if u == LN_UNIT - 1:
                    rotary_tables()
                if u == LN_UNIT:
                    dve.wait_ge(ln_mu, 1)
                    for c in range(NC):
                        v.tensor_tensor(cv[:, c, :], cv[:, c, :], banks(0, 2), ALU.subtract).then_inc(ln_d, 1)
                if u == LN_UNIT + 1:
                    dve.wait_ge(ln_sd, 1)
                    link(v.reciprocal(lnr[:, :], lnr[:, :]))
                    for c in range(NC):
                        dve.wait_ge(ln_sq, c + 1)
                        dve.wait_ge(ln_d, c + 1)
                        v.tensor_tensor(cv[:, c, :], cv[:, c, :], lnr[:, :], ALU.mult).then_inc(ln_y, 1)
            def misc(kind, t):
                s = at_stage[kind, t]
                M = pb[:, 7, :]
                if kind == "qdT":
                    dve.wait_ge(m_full, s + 1)
                    v.tensor_tensor(qdT[:, :, :], M[:, 0:3 * P].rearrange("p (c t) -> p c t", c=3),
                                    vcol[:, V_GQ:V_GQ + 3].unsqueeze(2).broadcast_to([P, 3, P]), ALU.mult).then_inc(m_free, 1)
                if kind == "q1":
                    dve.wait_ge(qk_sq, 2 * t + 1)
                    v.reduce_sum(ssh[:, 0, :], sq2[:, :, :], axis=AX.X).then_inc(head_ss, 1)
                if kind == "kv1":
                    dve.wait_ge(qk_sq, 2 * t + 2)
                    link(v.reduce_sum(ssh[:, 1, :], sq2[:, :, 0:NOPE], axis=AX.X))
                    v.tensor_scalar(ssh[:, 1, :], ssh[:, 1, :], ss3[:, 2, t:t + 1], None, ALU.add).then_inc(head_ss, 1)
                if kind in ("kT0", "kT1"):
                    dve.wait_ge(m_full, s + 1)
                    h = 4 * (kind == "kT1")
                    v.tensor_scalar(kT[0:QK, h:h + 4, t * P:(t + 1) * P], M[0:QK, :].rearrange("p (h t) -> p h t", h=4),
                                    vcol[0:QK, V_NK:V_NK + 1], None, ALU.mult).then_inc(m_free, 1)

            def rowmax(n):
                j, h = divmod(n, HEADS)
                dve.wait_ge(sc_ok, n + 1)
                if n >= 2:
                    dve.wait_ge(ex_ok, n - 1)
                v.tensor_reduce(out=nmax[:, n % 2:n % 2 + 1], in_=banks(2 * (n % 2), 2)[:, 0:(j + 1) * P],
                                axis=AX.X, op=ALU.max, negate=True).then_inc(mx_ok, 1)

            for k in PREP:
                misc(k, 0)
            rowmax(0)
            rowmax(1)
            for m in range(NTILE * HEADS):
                j, h = divmod(m, HEADS)
                dve.wait_ge(pt_ok, m + 1)
                if m >= 2:
                    dve.wait_ge(pv_ok, m - 1)
                v.tensor_copy(pT[:, m % 2, 0:min(512, (j + 1) * P)], banks(4, 1)[:, 0:min(512, (j + 1) * P)]).then_inc(pt_d, 1)
                for k, t in slots(j, h, 0):
                    misc(k, t)
                if m + 2 < NTILE * HEADS:
                    rowmax(m + 2)
                for k, t in slots(j, h, 1):
                    misc(k, t)
                if h + 1 == HEADS:
                    dve.wait_ge(ex_ok, m + 1)
                    link(v.reciprocal(rinv[:, :], rsum[:, j % 2, :]))
                    dve.wait_ge(pv_ok, m + 1)
                    if j:
                        dve.wait_ge(m_free, at_stage["oT", j - 1] + 1)
                    v.tensor_tensor(On[:, :].rearrange("p (h c) -> p h c", h=HEADS), pb[:, 6, :].rearrange("p (h c) -> p h c", h=HEADS),
                                    rinv[:, :].unsqueeze(2).broadcast_to([P, HEADS, VD]), ALU.mult).then_inc(on_ok, 1)

            for c in range(2):
                dve.wait_ge(sp_hi, c + 1)
                v.tensor_tensor(aT[1][:, 4 + 2 * c:6 + 2 * c, :], cv[:, 2 * c:2 * c + 2, :], aT[0][:, 4 + 2 * c:6 + 2 * c, :].bitcast(F32), ALU.subtract).then_inc(sp_lo, 1)
            for c in range(2):
                dve.wait_ge(sp_hi, c + 3)
                v.tensor_tensor(aT[1][:, 2 * c:2 * c + 2, :], attnT[:, 2 * c:2 * c + 2, :], aT[0][:, 2 * c:2 * c + 2, :].bitcast(F32), ALU.subtract).then_inc(sp_lo, 1)
            unit_lo(IN_UNITS)
            unit_lo(IN_UNITS + 1)
            for c in range(OUT_UNITS):
                dve.wait_ge(u_mm, IN_UNITS + c + 1)
                v.tensor_tensor(gates[:, c, :], gates[:, c, :], banks(4 * (c % 2), 2), ALU.mult)
                v.tensor_tensor(gates[:, KD + c, :], gates[:, KD + c, :], banks(4 * (c % 2) + 2, 2), ALU.mult).then_inc(yab_used, 1)
                dve.wait_ge(yab_used, c + 1)
                v.tensor_tensor(gates[:, c, :], gates[:, c, :], gates[:, KD + c, :], ALU.add).then_inc(mg_ok, 1)
                if c + 2 < OUT_UNITS:
                    unit_lo(IN_UNITS + c + 2)

            dve.wait_ge(gff_in, 16 * 5)
            for j in range(NTILE):
                dve.wait_ge(x1_ps, j + 1)
                dve.wait_ge(xb_in[j % 2], 16 * (j // 2 + 1))
                v.tensor_tensor(x1[:, j, :], xb[:, j % 2, :], banks(2 * (j % 2), 2), ALU.add).then_inc(x1_ok, 1)
                dve.wait_ge(ss7, j + 1)
                dve.wait_ge(rs7, j + 1)
                if j >= 2:
                    dve.wait_ge(h2_out[j % 2], 16 * (j // 2))
                    dve.wait_ge(h2t_ps, j - 1)
                v.scalar_tensor_tensor(out=h2[:, j % 2, :], in0=x1[:, j, :], scalar=rs1[:, j:j + 1], in1=gffb[:, :], op0=ALU.mult, op1=ALU.mult).then_inc(h2_ok, 1)
                if j >= 1:
                    dve.wait_ge(lg_ps, j)
                    v.tensor_copy(lg[:, j - 1, :], pb[:, 6, 0:NG])
                    v.tensor_copy(le[:, j - 1, :], pb[:, 6, NG:NG + NE]).then_inc(lg_ok, 1)
            dve.wait_ge(lg_ps, NTILE)
            v.tensor_copy(lg[:, NTILE - 1, :], pb[:, 6, 0:NG])
            link(v.tensor_copy(le[:, NTILE - 1, :], pb[:, 6, NG:NG + NE]))

            def bc(t, n):
                return t.unsqueeze(2).broadcast_to([P, NTILE, n])

            def row(t, n):
                return t.unsqueeze(1).broadcast_to([P, NTILE, n])

            link(v.reduce_max(s8[0][:, :], lg[:, :, :], axis=AX.X))
            link(v.tensor_tensor(tg[:, :, :], lg[:, :, :], bc(s8[0][:, :], NG), ALU.subtract))
            link(v.scalar_tensor_tensor(out=pen[:, :, :], in0=tg[:, :, :], scalar=0.0, in1=row(down4[:, :], NG), op0=ALU.is_ge, op1=ALU.mult))
            v.reduce_max(s8[1][:, :], pen[:, :, :], axis=AX.X).then_inc(r_in, 1)
            dve.wait_ge(r_in, 1)
            link(v.tensor_tensor(pen[:, :, :], pen[:, :, :], bc(s8[1][:, :], NG), ALU.is_equal))
            link(v.tensor_scalar(pen[:, :, :], pen[:, :, :], -1.0, -MASKED, ALU.add, ALU.mult))
            grp = le[:, :, :].rearrange("p j (g e) -> p (j g) e", g=NG)
            link(v.tensor_tensor(grp, grp, pen[:, :, :].rearrange("p j g -> p (j g)").unsqueeze(2).broadcast_to([P, NTILE * NG, EPG]), ALU.add))
            for c in range(2):
                m = s8[1 + c]
                link(v.reduce_max(m[:, :], le[:, :, :], axis=AX.X))
                link(v.tensor_tensor(te[:, :, :], le[:, :, :], bc(m[:, :], NE), ALU.is_ge))
                link(v.tensor_tensor(te[:, :, :], te[:, :, :], row(down32[:, :], NE), ALU.mult))
                link(v.reduce_max(s8[0][:, :], te[:, :, :], axis=AX.X))
                link(v.tensor_tensor(oh[c][:, :, :], te[:, :, :], bc(s8[0][:, :], NE), ALU.is_equal))
                if c == 0:
                    link(v.scalar_tensor_tensor(out=le[:, :, :], in0=oh[0][:, :, :], scalar=2 * MASKED, in1=le[:, :, :], op0=ALU.mult, op1=ALU.add))
            v.tensor_tensor(ab[:, :, :], oh[0][:, :, :], oh[1][:, :, :], ALU.add).then_inc(a_ok, 1)
            v.tensor_tensor(s8[3][:, :], s8[2][:, :], s8[1][:, :], ALU.subtract).then_inc(r_in, 1)
            dve.wait_ge(r_exp, 1)
            link(v.reduce_sum(s8[4][:, :], tg[:, :, :], axis=AX.X))
            dve.wait_ge(r_exp, 2)
            link(v.tensor_scalar(s8[5][:, :], s8[3][:, :], 1.0, None, ALU.add))
            link(v.tensor_tensor(s8[4][:, :], s8[4][:, :], s8[5][:, :], ALU.mult))
            link(v.reciprocal(wt[:, 0, :], s8[4][:, :]))
            link(v.tensor_tensor(wt[:, 1, :], wt[:, 0, :], s8[3][:, :], ALU.mult))
            dve.wait_ge(rc_ps, 1)
            v.memset(pre[:, 0, :], 0.0)
            link(v.tensor_copy(pre[:, 1:NTILE + 1, :], pb[:, 0, NE * NTILE:2 * NE * NTILE].rearrange("p (j e) -> p j e", j=NTILE)))
            for j in range(1, NTILE):
                link(v.tensor_tensor(pre[:, j + 1, :], pre[:, j + 1, :], pre[:, j, :], ALU.add))
            link(v.tensor_tensor(rank[:, :, :], pb[:, 0, 0:NE * NTILE].rearrange("p (j e) -> p j e", j=NTILE), pre[:, 0:NTILE, :], ALU.add))
            link(v.tensor_tensor(cmp8[:, :, :], pre[:, NTILE, :].unsqueeze(2).broadcast_to([P, NE, 8]), io8[:, :].unsqueeze(1).broadcast_to([P, NE, 8]), ALU.is_gt))
            link(v.reduce_sum(nb[:, :], cmp8[:, :, :], axis=AX.X))
            link(v.memset(b128[:, :], 1.0))
            link(v.tensor_tensor_scan(incl[:, :], b128[:, :], nb[:, :], 0.0, ALU.mult, ALU.add))
            link(v.tensor_tensor(b128[:, :], incl[:, :], nb[:, :], ALU.subtract))
            link(v.scalar_tensor_tensor(out=rank[:, :, :], in0=row(b128[:, :], NE), scalar=float(P), in1=rank[:, :, :], op0=ALU.mult, op1=ALU.add))
            for c in range(2):
                link(v.tensor_tensor(te[:, :, :], oh[c][:, :, :], rank[:, :, :], ALU.mult))
                link(v.reduce_sum(pos2[:, c, :], te[:, :, :], axis=AX.X))
            link(v.tensor_copy(pidx[:, :, :], pos2[:, :, :]))
            v.tensor_single_scalar(phi[:, :, :], pidx[:, :, :], 7, op=ALU.logical_shift_right)
            link(v.tensor_single_scalar(plo[:, :, :], pidx[:, :, :], P - 1, op=ALU.bitwise_and))
            link(v.scalar_tensor_tensor(out=tidx[:, :, :], in0=plo[:, :, :], scalar=float(NBT), in1=phi[:, :, :], op0=ALU.mult, op1=ALU.add))
            link(v.tensor_tensor(cmpb[:, :, :], incl[0:1, :].unsqueeze(1).broadcast_to([1, NBT, NE]), iob[:, :].unsqueeze(2).broadcast_to([1, NBT, NE]), ALU.is_le))
            link(v.reduce_sum(bexp_f[:, :], cmpb[:, :, :], axis=AX.X))
            link(v.tensor_scalar(bexp[:, :], bexp_f[:, :], float(NE - 1), None, ALU.min))
            link(v.tensor_scalar(cmp2[:, :], io2[:, :], incl[0:1, NE - 1:NE], None, ALU.is_lt))
            link(v.reduce_sum(npair_f[:, :], cmp2[:, :], axis=AX.X))
            v.tensor_copy(npair_i[:, :], npair_f[:, :]).then_inc(route_ok, 1)
            dve.wait_ge(route_ok, 1)
            npair = dve.value_load(npair_i[0:1, 0:1], min_val=1, max_val=MAXB // 2)

            dve.wait_ge(stok_in, 16)

            link(v.tensor_single_scalar(stok[:, :], srow[:, :], 1, op=ALU.logical_shift_right))

            def index_col(b, col):
                v.tensor_scalar(icol[b][:, :], stok[:, bass.ds(col, 1)], 0.0, None, ALU.add).then_inc(ic_ok, 1)

            v.tensor_copy(icol[0][:, :], stok[:, 0:1]).then_inc(ic_ok, 1)
            for b in range(2):
                v.memset(hg[b][:, :], 0.0).then_inc(hg_zero, 1)

            def gathered_T(b, count):
                dve.wait_ge(hgt_ps, count)
                v.tensor_copy(hgT[b][:, :, :], banks(0, 2).rearrange("p (k t) -> p k t", k=KD)).then_inc(hgt_ok, 1)

            gathered_T(0, 1)
            with dve.Fori(0, npair) as i:
                for b in range(2):
                    index_col(1 - b, i * 2 + (b + 1))
                    dve.wait_ge(sil_ok, i * 2 + (b + 1))
                    v.tensor_tensor(mid[:, :], sil[:, :], pb[:, 2, FF:2 * FF], ALU.mult).then_inc(mid_ok, 1)
                    dve.wait_ge(mt_ps, i * 2 + (b + 1))
                    v.tensor_copy(midT[:, :, :], pb[:, 3, 0:FF].rearrange("p (f t) -> p f t", f=2)).then_inc(mt_ok, 1)
                    gathered_T(1 - b, i * 2 + (b + 2))
                    dve.wait_ge(y_ps, i * 2 + (b + 1))
                    dve.wait_ge(y_out[b], i * 16 + 16)
                    v.tensor_scalar(rcol[b][:, :], srow[:, bass.ds(i * 2 + b, 1)], 0.0, None, ALU.add)
                    v.tensor_copy(yb[b][:, 512:1024], pb[:, 5, :]).then_inc(y_d_ok, 1)

            for j in range(NTILE):
                dve.wait_ge(yg_in[j % 2], 16 * (j // 2 + 1))
                if j >= 2:
                    dve.wait_ge(o_out[j % 2], 16 * (j // 2))
                link(v.scalar_tensor_tensor(out=ob[j % 2][:, :], in0=yg[j % 2][:, 0, :], scalar=wt[:, 0, j:j + 1], in1=x1[:, j, :], op0=ALU.mult, op1=ALU.add))
                v.scalar_tensor_tensor(out=ob[j % 2][:, :], in0=yg[j % 2][:, 1, :], scalar=wt[:, 1, j:j + 1], in1=ob[j % 2][:, :], op0=ALU.mult, op1=ALU.add).then_inc(ob_ok, 1)

        @block.tensor
        def _(pe):
            t_ = nc.tensor

            def three(out, w, m, start, stop):
                t_.matmul(out, w(0), m(0), start=start, stop=False)
                t_.matmul(out, w(0), m(1), start=False, stop=False)
                return t_.matmul(out, w(1), m(0), start=False, stop=stop)

            pe.wait_ge(ident_ok, 1)
            pe.wait_ge(consts, 2)
            pe.wait_ge(small_in, 16 * 13)
            pe.wait_ge(vec_c, 1)
            t_.transpose(pb[:, 6, 0:NV], vecs[0:NV, :], ident[0:NV, 0:NV])
            t_.transpose(pb[:, 6, 64:64 + TAPS * NC], dwr[:, :], ident[0:TAPS * NC, 0:TAPS * NC])
            t_.transpose(pb[:, 6, 256:256 + NTILE], posf[:, :], ident[0:NTILE, 0:NTILE]).then_inc(vec_t, 1)
            for j in range(NTILE):
                pe.wait_ge(s_xn, j + 1)
                if j >= 2:
                    pe.wait_ge(s_hp, j - 1)
                for k in range(KD):
                    i = t_.transpose(banks(2 * (j % 2), 2)[:, k * P:(k + 1) * P], xn[:, j % 2, k * P:(k + 1) * P], ident[:, :])
                i.then_inc(s_xt, 1)
            pe.wait_ge(dn_lo, 1)
            pe.wait_ge(s_hp, NTILE)
            for j in range(NTILE):
                pe.wait_ge(s_lo, j + 1)
                if j >= 2:
                    pe.wait_ge(dn_ev, j - 1)
                for k in range(KD):
                    i = three(pb[:, j % 2, 0:DOWN], lambda s: hT[s][:, k, j * P:(j + 1) * P], lambda s: wdn[s][:, k, :], k == 0, k == KD - 1)
                i.then_inc(dn_ps, 1)
            for u in range(IN_UNITS):
                    b = u % 2
                    pe.wait_ge(u_lo, u + 1)
                    if u >= 2:
                        pe.wait_ge(u_ev, u - 1)
                    for f in range(2):
                        for k in range(KD):
                            i = three(pb[:, 2 * b + 2 + f, :], lambda s: ws[s][:, b, k, :], lambda s: hT[s][:, k, f * 512:(f + 1) * 512], k == 0, k == KD - 1)
                    i.then_inc(u_mm, 1)
                    if u == LN_UNIT:
                        pe.wait_ge(conv_done, NC)
                        for f in range(2):
                            for c in range(NC):
                                i = t_.matmul(pb[:, f, :], mean_w[:, :], cv[:, c, f * 512:(f + 1) * 512], start=(c == 0), stop=(c == NC - 1))
                        i.then_inc(ln_mu, 1)
                    if u == LN_UNIT + 1:
                        for c in range(NC):
                            pe.wait_ge(ln_sq, c + 1)
                            for f in range(2):
                                i = t_.matmul(pb[:, 6 + f, :], mean_w[:, :], lnt[c][:, f * 512:(f + 1) * 512], start=(c == 0), stop=(c == NC - 1))
                        i.then_inc(ln_var, 1)

            def misc(kind, t):
                s = at_stage[kind, t]
                M = pb[:, 7, :]
                if s:
                    pe.wait_ge(m_free, s)
                if kind == "qdT":
                    pe.wait_ge(qd_ok, 1)
                    for c in range(3):
                        i = t_.transpose(M[:, c * P:(c + 1) * P], qd[:, t, c * P:(c + 1) * P], ident[:, :])
                if kind in ("q0", "q1"):
                    pe.wait_ge(uq_in, 32)
                    c0 = 4 * QK * (kind == "q1")
                    for k in range(2):
                        i = t_.matmul(M[:, 0:4 * QK], qdT[:, k, :], wuq[:, k, c0:c0 + 4 * QK], start=(k == 0), stop=(k == 1))
                if kind in ("kv0", "kv1"):
                    c0 = 512 * (kind == "kv1")
                    i = t_.matmul(M, qdT[:, 2, :], wukv[:, c0:c0 + 512], start=True, stop=True)
                if kind in ("qT0", "qT1", "kT0", "kT1"):
                    src = qn if kind[0] == "q" else kn
                    pe.wait_ge(qk_ok, 2 * t + (1 if kind[0] == "q" else 2))
                    h0 = 4 * (kind[2] == "1")
                    for h in range(4):
                        i = t_.transpose(M[0:QK, h * P:(h + 1) * P], src[:, h0 + h, :], ident[:, :])
                if kind == "oT":
                    pe.wait_ge(on_ok, t + 1)
                    for c in range(4):
                        i = t_.transpose(M[:, c * P:(c + 1) * P], On[:, c * P:(c + 1) * P], ident[:, :])
                i.then_inc(m_full, 1)

            def scores(n):
                j, h = divmod(n, HEADS)
                w = (j + 1) * P
                if h == 0:
                    pe.wait_ge(m_free, at_stage["kT1", j] + 1)
                if n >= 2:
                    pe.wait_ge(ex_ok, n - 1)
                S = banks(2 * (n % 2), 2)
                for f in range(0, w, 512):
                    e = min(w, f + 512)
                    t_.matmul(S[:, f:e], qT[0:QK, j % 2, h * P:(h + 1) * P], kT[0:QK, h, f:e], start=True, stop=(e < w))
                t_.matmul(S[:, w - P:w], mrow[0:1, 0, :], mrow[0:1, 1, :], start=False, stop=True).then_inc(sc_ok, 1)

            def probs_T(n):
                j, h = divmod(n, HEADS)
                pe.wait_ge(ex_ok, n + 1)
                if n >= 1:
                    pe.wait_ge(pt_d, n)
                    if (n - 1) // HEADS >= 4:
                        pe.wait_ge(pt_a, n - 4 * HEADS)
                for k in range(j + 1):
                    i = t_.transpose(banks(4, 2)[:, k * P:(k + 1) * P], pr[:, n % 2, k * P:(k + 1) * P], ident[:, :])
                i.then_inc(pt_ok, 1)

            def pv(n):
                j, h = divmod(n, HEADS)
                pe.wait_ge(pt_d, n + 1)
                if j >= 4:
                    pe.wait_ge(pt_a, n + 1 - 4 * HEADS)
                if h == 0 and j:
                    pe.wait_ge(on_ok, j)
                for k in range(j + 1):
                    i = t_.matmul(pb[:, 6, h * VD:(h + 1) * VD], pT[:, n % 2, k * P:(k + 1) * P], vv[:, k, h * VD:(h + 1) * VD], start=(k == 0), stop=(k == j))
                i.then_inc(pv_ok, 1)

            pe.wait_ge(ln_y, 1)
            pe.wait_ge(u_ev, IN_UNITS)
            for k in PREP:
                misc(k, 0)
            scores(0)
            scores(1)
            for n in range(NTILE * HEADS):
                j, h = divmod(n, HEADS)
                probs_T(n)
                for k, t in slots(j, h, 0):
                    misc(k, t)
                if n + 2 < NTILE * HEADS:
                    scores(n + 2)
                for k, t in slots(j, h, 1):
                    misc(k, t)
                pv(n)
            misc("oT", NTILE - 1)

            pe.wait_ge(m_free, len(order))
            pe.wait_ge(sp_lo, 4)
            for c in range(OUT_UNITS):
                u = IN_UNITS + c
                pe.wait_ge(u_lo, u + 1)
                if c >= 2:
                    pe.wait_ge(yab_used, c - 1)
                for br_ in (1, 0):
                    for f in range(2):
                        for k in range(4):
                            i = three(pb[:, 4 * (c % 2) + 2 * br_ + f, :], lambda s: ws[s][:, u % 2, 4 * br_ + k, :],
                                      lambda s: aT[s][:, 4 * br_ + k, f * 512:(f + 1) * 512], k == 0, k == 3)
                i.then_inc(u_mm, 1)
            pe.wait_ge(wout_in, 16)
            pe.wait_ge(mg_ok, OUT_UNITS)

            pe.wait_ge(gff_in, 16 * 5)

            def router(j):
                pe.wait_ge(h2_ok, j + 1)
                if j >= 1:
                    pe.wait_ge(h2t_ok, j)
                for k in range(KD):
                    i = t_.transpose(banks(4, 2)[:, k * P:(k + 1) * P], h2[:, j % 2, k * P:(k + 1) * P], ident[:, :])
                i.then_inc(h2t_ps, 1)
                pe.wait_ge(h2t_ok, j + 1)
                if j >= 1:
                    pe.wait_ge(lg_ok, j)
                for k in range(KD):
                    t_.matmul(pb[:, 6, 0:NG + NE], h2T[:, j % 2, k, :], wr[:, k, :], start=(k == 0), stop=False)
                t_.matmul(pb[:, 6, 0:NG + NE], one_row[0:1, :], br[0:1, :], start=False, stop=True).then_inc(lg_ps, 1)

            for j in range(NTILE):
                if j >= 2:
                    pe.wait_ge(x1_ok, j - 1)
                for f in range(2):
                    for k in range(KD):
                        i = t_.matmul(pb[:, 2 * (j % 2) + f, :], gates[:, k, j * P:(j + 1) * P], wout[:, k, f * 512:(f + 1) * 512], start=(k == 0), stop=(k == KD - 1))
                i.then_inc(x1_ps, 1)
                if j >= 1:
                    router(j - 1)
            router(NTILE - 1)
            pe.wait_ge(a_ok, 1)
            A = ab[:, :, :].rearrange("p j e -> p (j e)")
            t_.matmul(pb[:, 0, 0:NE * NTILE], before[:, :], A, start=True, stop=True)
            t_.matmul(pb[:, 0, NE * NTILE:2 * NE * NTILE], ones_b[:, :], A, start=True, stop=True).then_inc(rc_ps, 1)

            pe.wait_ge(route_ok, 1)
            pe.sem_inc(y_a, 1)
            pe.sem_inc(y_d_ok, 1)
            npair = pe.value_load(npair_i[0:1, 0:1], min_val=1, max_val=MAXB // 2)

            def gather_T(b, gathers):
                pe.wait_ge(hg_in[b], gathers)
                for k in range(KD):
                    i = t_.transpose(banks(0, 2)[:, k * P:(k + 1) * P], hg[b][:, k * P:(k + 1) * P], ident[:, :])
                i.then_inc(hgt_ps, 1)

            gather_T(0, 16)
            with pe.Fori(0, npair) as i:
                for b in range(2):
                    nth = i * 2 + (b + 1)
                    pe.wait_ge(w_in0[b], i * 32 + 32)
                    pe.wait_ge(hgt_ok, nth)
                    for k in range(KD):
                        q = t_.matmul(pb[:, 2, :], hgT[b][:, k, :], wgu[b][:, k, :], start=(k == 0), stop=(k == KD - 1))
                    q.then_inc(gu_ps, 1)
                    gather_T(1 - b, i * 16 + 16 * (b + 1))
                    pe.wait_ge(mid_ok, nth)
                    for f in range(2):
                        q = t_.transpose(pb[:, 3, f * P:(f + 1) * P], mid[:, f * P:(f + 1) * P], ident[:, :])
                    q.then_inc(mt_ps, 1)
                    pe.wait_ge(mt_ok, nth)
                    pe.wait_ge(w_in1[b], i * 16 + 16)
                    pe.wait_ge(y_a, nth)
                    pe.wait_ge(y_d_ok, nth)
                    for h in range(2):
                        for f in range(2):
                            q = t_.matmul(pb[:, 4 + h, :], midT[:, f, :], wed[b][:, f, h * 512:(h + 1) * 512], start=(f == 0), stop=(f == 1))
                    q.then_inc(y_ps, 1)


_INS = ["x", "positions", "g_mix", "w_in", "g_q_lora", "w_uq", "g_kv_lora", "w_ukv", "g_qk_q", "g_qk_k",
        "w_o_mla", "w_dw", "b_dw", "g_conv_ln", "b_conv_ln", "w_conv_out", "b_gates", "w_out", "g_ffn",
        "w_group_router", "b_group_router", "w_expert_router", "b_expert_router",
        "w_e_gate", "w_e_up", "w_e_down"]
_OUTS = [((1, T, D), "float32")]


def kernel(**inputs):
    import numpy as np
    import concourse.bacc as bacc
    from concourse.bass_utils import run_bass_kernel_spmd

    nc = bacc.Bacc("TRN2", target_bir_lowering=False, num_devices=1, dynamic_dma_scratch_size=4096)
    arrays, args = {}, []
    for name in _INS:
        a = np.ascontiguousarray(inputs[name])
        arrays[f"in_{name}"] = a
        args.append(nc.dram_tensor(f"in_{name}", a.shape, mybir.dt.from_np(a.dtype), kind="ExternalInput").ap())
    for i, (shape, dtype) in enumerate(_OUTS):
        args.append(nc.dram_tensor(f"out_{i}", shape, mybir.dt.from_np(np.dtype(dtype)), kind="ExternalOutput").ap())
    build(nc, *args)
    r = run_bass_kernel_spmd(nc, [arrays], core_ids=[0])
    return r.results[0]["out_0"]
```

```python
import concourse.bass as bass
from concourse import mybir
from contextlib import ExitStack

F32 = mybir.dt.float32
F32R = mybir.dt.float32r
BF16 = mybir.dt.bfloat16
I32 = mybir.dt.int32
U32 = mybir.dt.uint32
ALU = mybir.AluOpType
ACT = mybir.ActivationFunctionType
AX = mybir.AxisListType

P = 128
D = 1024
T = 1024
NTILE = T // P
KD = D // P
HEADS, NOPE, ROPE, VD = 8, 64, 32, 64
QK = NOPE + ROPE
HALF = ROPE // 2
QL, KVL = 256, 128
DOWN = QL + KVL + ROPE
CW = 512
NC = CW // P
TAPS = 31
PAD = TAPS - 1
NG, EPG, FF = 4, 8, 256
NE = NG * EPG
EPS = 1e-6
CHUNK = 64
MASKED = -1e30
THETA = 10000.0
MAXB = 2 * T // P + NE
SLOTS = 4
NBT = MAXB + SLOTS
GLU_UNITS = 2 * NC
GATE_UNITS = 2 * D // P
IN_UNITS = GLU_UNITS + GATE_UNITS
OUT_UNITS = D // P
TAPS_PER_UNIT = 7
LN_UNIT = 20


def build(nc, x, positions, g_mix, w_in, g_q_lora, w_uq, g_kv_lora, w_ukv, g_qk_q, g_qk_k,
          w_o_mla, w_dw, b_dw, g_conv_ln, b_conv_ln, w_conv_out, b_gates, w_out, g_ffn,
          w_group_router, b_group_router, w_expert_router, b_expert_router,
          w_e_gate, w_e_up, w_e_down, out):
    K = 1024
    base = (nc.sbuf_base + 127) // 128 * 128
    at = {"top": base}

    def place(name, shape, dt, offset):
        return nc.alloc_sbuf_tensor_at(name, shape, dt, offset=offset)

    def room(nbytes):
        o = at["top"]
        at["top"] += (nbytes + 31) // 32 * 32
        assert at["top"] <= nc.sbuf_usable_end, at["top"]
        return o

    def small(name, shape, dt=F32):
        n = 2 if dt == BF16 else 4
        for s in shape[1:]:
            n *= s
        return place(name, shape, dt, room(n))

    R1 = room(64 * K)
    R2 = room(64 * K)
    R3 = room(32 * K)
    R6 = room(24 * K)
    hT = [place("hT_hi", [P, KD, T], F32R, R1), place("hT_lo", [P, KD, T], F32R, R1 + 32 * K)]
    xs = place("xs", [P, NTILE, D], F32, R2)
    diag = place("diag", [P, 2, P], F32, R2 + 32 * K)
    hp = place("hp", [P, 2, KD, P], F32, R2 + 40 * K)
    sqj = place("sqj", [P, D], F32, R2 + 48 * K)
    sq3 = place("sq3", [P, DOWN], F32, R2 + 52 * K)
    wdn_raw = place("wdn_raw", [P, KD, DOWN], F32, R6)
    wdn = [place("wdn_hi", [P, KD, DOWN], F32R, R3), place("wdn_lo", [P, KD, DOWN], F32R, R3 + 14 * K)]
    ws_raw = place("ws_raw", [P, 2, KD, P], F32, R6)
    ws = [place("ws_hi", [P, 2, KD, P], F32R, R6 + 8 * K), place("ws_lo", [P, 2, KD, P], F32R, R6 + 16 * K)]
    gates = place("gates", [P, 2 * KD, T], F32, R2)
    cv = place("cv", [P, NC, T], F32, R3)
    UW = T + PAD
    up = [place(f"up{c}", [P, UW], F32, o) for c, o in enumerate((R3 + 16 * K, R3 + 20 * K + 256, R2 + 48 * K, R2 + 56 * K))]
    sg = place("sg", [P, T], F32, R3 + 25 * K)
    QTO = room(8 * K)
    qT = place("qT", [P, 2, HEADS * P], F32, QTO)
    attnT = place("attnT", [P, 4, T], F32, R3 + 16 * K)
    kT = place("kT", [P, HEADS, T], F32, R1)
    vv = place("vv", [P, NTILE, HEADS * VD], F32, R1 + 32 * K)
    pr = place("pr", [P, 2, T], F32, R1 + 48 * K)
    pT = place("pT", [P, 2, T], F32, R1 + 56 * K)
    wuq = place("wuq", [P, 2, HEADS * QK], F32, R6)
    wukv = place("wukv", [P, HEADS * (NOPE + VD)], F32, R6 + 8 * K)
    qn = place("qn", [P, HEADS, QK], F32, R6 + 12 * K)
    kn = place("kn", [P, HEADS, QK], F32, R6 + 15 * K)
    sq2 = place("sq2", [P, HEADS, QK], F32, R6 + 18 * K)
    tmpr = place("tmpr", [P, HEADS, ROPE], F32, R6 + 21 * K)
    qdT = place("qdT", [P, 3, P], F32, R6 + 22 * K)
    lnt = [place(f"lnt{c}", [P, T], F32, o) for c, o in enumerate((QTO, QTO + 4 * K, R3 + 16 * K, R3 + 20 * K))]
    lnr = place("lnr", [P, T], F32, R3 + 25 * K)
    aT = [place("aT_hi", [P, 8, T], F32R, R1), place("aT_lo", [P, 8, T], F32R, R1 + 32 * K)]
    wout = place("wout", [P, KD, D], F32, R3)
    wout_lo = place("wout_lo", [P, KD, D], F32R, R3)
    mg = [place("mg_hi", [P, KD, T], F32R, R2 + 32 * K), place("mg_lo", [P, KD, T], F32R, R2)]
    x1 = place("x1", [P, NTILE, D], F32, R1)
    xb = place("xb", [P, 2, D], F32, R1 + 32 * K)
    h2 = place("h2", [P, 2, D], F32, R1 + 40 * K)
    h2T = place("h2T", [P, 2, KD, P], F32, R1 + 48 * K)
    sq7 = place("sq7", [P, D], F32, R1 + 56 * K)
    gffb = place("gffb", [P, D], F32, R1 + 60 * K)
    WO = (R2, R2 + 24 * K, R1 + 32 * K, R6)
    wgu = [place(f"wgu{i}", [P, KD, 2 * FF], F32, o) for i, o in enumerate(WO)]
    wed = [place(f"wed{i}", [P, 2, D], F32, o + 16 * K) for i, o in enumerate(WO)]
    hg = [place(f"hg{i}", [P, D], F32, R2 + 48 * K + 4 * K * i) for i in range(2)]
    hgT = [place(f"hgT{i}", [P, KD, P], F32, R2 + 56 * K + 4 * K * i) for i in range(2)]
    yb = [place(f"yb{i}", [P, D], F32, R3 + 4 * K * i) for i in range(2)]
    sil = place("sil", [P, FF], F32, R3 + 8 * K)
    mid = place("mid", [P, FF], F32, R3 + 9 * K)
    midT = place("midT", [P, 2, P], F32, R3 + 10 * K)

    On = small("On", [P, HEADS * VD])
    QDO = room(NTILE * DOWN * 4)
    qd = place("qd", [P, NTILE, DOWN], F32, QDO)
    wout_hi = [place(f"wout_hi{k}", [P, D], F32R, o) for k, o in enumerate(
        (R6 + 8 * K, R6 + 16 * K, R6 + 12 * K, R6 + 20 * K, QTO, QTO + 4 * K, QDO, QDO + 4 * K))]
    ident = small("ident", [P, P])
    mean_w = small("mean_w", [P, P])
    mrow = small("mrow", [1, 2, P], BF16)
    before = small("before", [P, P], BF16)
    ones_b = small("ones_b", [P, P], BF16)
    one_row = small("one_row", [1, P])
    vecs = place("vecs", [48, P], F32, R6 + 14 * K)
    V_GM, V_BG, V_BD, V_GL, V_BL, V_GQ, V_GK, V_NQ, V_NK = 0, 8, 24, 28, 32, 36, 38, 39, 40
    NV = 41
    vcol = small("vcol", [P, 48])
    dwr = place("dwr", [TAPS * NC, P], F32, R6 + 14 * K + 512)
    dwc = small("dwc", [P, TAPS * NC])
    posi = place("posi", [NTILE, P], I32, R6 + 15 * K)
    posf = place("posf", [NTILE, P], F32, R6 + 15 * K + 512)
    posc = small("posc", [P, NTILE])
    gqk = small("gqk", [P, 2, QK])
    invf = small("invf", [P, HALF])
    ang = place("ang", [P, NTILE, HALF], F32, R2 + 36 * K)
    turns = place("turns", [P, NTILE, HALF], F32, R2 + 36 * K + 512)
    sincos = small("sincos", [P, 2, NTILE, HALF])
    krr = small("krr", [P, NTILE, ROPE])
    krt = place("krt", [P, NTILE, ROPE], F32, R3 + 29 * K)
    rtab = small("rtab", [P, 2, NTILE, ROPE])
    ss1 = small("ss1", [P, NTILE])
    rs1 = small("rs1", [P, NTILE])
    ss3 = small("ss3", [P, 3, NTILE])
    ssh = small("ssh", [P, 2, HEADS])
    nmax = small("nmax", [P, 2])
    rsum = small("rsum", [P, 2, HEADS])
    rinv = small("rinv", [P, HEADS])
    wr = place("wr", [P, KD, NG + NE], F32, R6)
    br = place("br", [1, NG + NE], F32, R6 + 2 * K)
    lg = place("lg", [P, NTILE, NG], F32, R6 + 3 * K)
    le = place("le", [P, NTILE, NE], F32, R6 + 4 * K)
    pen = place("pen", [P, NTILE, NG], F32, R6 + 5 * K)
    tg = place("tg", [P, NTILE, NG], F32, R6 + 5 * K + 512)
    oh = [place(f"oh{i}", [P, NTILE, NE], F32, R3 + 12 * K + i * K) for i in range(2)]
    te = place("te", [P, NTILE, NE], F32, R3 + 14 * K)
    ab = small("ab", [P, NTILE, NE], BF16)
    s8 = [small(f"s8_{i}", [P, NTILE]) for i in range(6)]
    wt = small("wt", [P, 2, NTILE])
    pre = place("pre", [P, NTILE + 1, NE], F32, R3 + 17 * K)
    nb = small("nb", [P, NE])
    incl = small("incl", [P, NE])
    b128 = small("b128", [P, NE])
    rank = place("rank", [P, NTILE, NE], F32, R3 + 15 * K)
    cmp8 = place("cmp8", [P, NE, 8], F32, R3 + 16 * K)
    pos2 = small("pos2", [P, 2, NTILE])
    pidx = small("pidx", [P, 2, NTILE], I32)
    phi_i = small("phi_i", [P, 2, NTILE], I32)
    plo_i = small("plo_i", [P, 2, NTILE], I32)
    phi = small("phi", [P, 2, NTILE])
    plo = small("plo", [P, 2, NTILE])
    trow = small("trow", [P, NTILE])
    iop = place("iop", [P, P], F32, R6 + 6 * K)
    iob = place("iob", [P, NBT], F32, R6 + 6 * K + 512)
    ohp = place("ohp", [P, 2 * NTILE, P], F32R, R6 + 8 * K)
    ohb = place("ohb", [P, 2 * NTILE, NBT], F32, R6 + 16 * K)
    ohbt = place("ohbt", [P, 2 * NTILE, NBT], F32R, R6 + 20 * K)
    down4 = small("down4", [P, NG])
    down32 = small("down32", [P, NE])
    io8 = small("io8", [P, 8])
    io4 = small("io4", [1, MAXB // SLOTS])
    cmpb = place("cmpb", [1, NBT, NE], F32, R3 + 20 * K)
    cmp4 = small("cmp4", [1, MAXB // SLOTS])
    bexp_f = small("bexp_f", [1, NBT])
    bexp = small("bexp", [1, NBT], I32)
    ntrip_f = small("ntrip_f", [1, 1])
    ntrip_i = small("ntrip_i", [1, 2], I32)
    one32 = small("one32", [P, NE])
    stok = small("stok", [P, NBT], I32)
    swt = small("swt", [P, NBT])
    wcol = [small(f"wcol{i}", [P, 1]) for i in range(2)]
    icol = [small(f"icol{i}", [P, 1], I32) for i in range(2)]
    rcol = [small(f"rcol{i}", [P, 1], I32) for i in range(2)]
    eps = small("eps", [P, 1])
    mhalf = small("mhalf", [P, 2, HEADS])
    tick_a, tick_d, tick_p = [small(f"tick_{e}", [1, 2]) for e in "adp"]

    h2_d = nc.dram_tensor("h2_rows", (T, D), F32, kind="Internal").ap()
    first_d = nc.dram_tensor("first", (2, P), F32, kind="Internal").ap()

    pb = nc.alloc_psum_tensor("pb", [P, 8, 512], F32)

    def banks(a, n):
        return pb[:, a:a + n, :].rearrange("p b f -> p (b f)")

    ctx = ExitStack()
    with ctx:
        ctx.enter_context(nc.allow_non_contiguous_dma(reason="small per-channel vectors"))

        def sem(name):
            return ctx.enter_context(nc.semaphore(name))

        x_in = [sem(f"x_in{j}") for j in range(NTILE)]
        small_in = sem("small_in")
        late_in, gff_in = sem("late_in"), sem("gff_in")
        wdn_in, uq_in = sem("wdn_in"), sem("uq_in")
        ws_in = [sem("ws_in0"), sem("ws_in1")]
        wout_in = sem("wout_in")
        xb_in = [sem("xb_in0"), sem("xb_in1")]
        h2_out = [sem("h2_out0"), sem("h2_out1")]
        consts, ident_ok = sem("consts"), sem("ident_ok")
        vec_t, vec_c = sem("vec_t"), sem("vec_c")
        dch, ach, pch = sem("dve_chain"), sem("act_chain"), sem("pool_chain")
        s_ss, s_rs, s_xn, s_xt, s_hp, s_hi, s_lo = [sem(n) for n in
            ("sumsq", "rstd", "x_scaled", "x_transposed", "h_product", "h_hi", "h_lo")]
        dn_hi, dn_lo, dn_ps, dn_ev = [sem(n) for n in ("wdn_hi_ok", "wdn_lo_ok", "down_ps", "down_sb")]
        u_hi, u_lo, u_mm, u_ev = [sem(n) for n in ("unit_hi", "unit_lo", "unit_mm", "unit_ev")]
        u_sg = sem("glu_sigmoid")
        down_rs, head_ss, head_rs = sem("down_rstd"), sem("head_ss"), sem("head_rstd")
        conv_done = sem("conv_done")
        ss3_ok, qd_ok, sin_in, sin_ok, tab_ok = [sem(n) for n in ("ss3_ok", "qd_ok", "sin_in", "sin_ok", "tab_ok")]
        ln_mu, ln_d, ln_sq, ln_var, ln_sd, ln_y, ln_u = [sem(n) for n in ("ln_mu", "ln_d", "ln_sq", "ln_var", "ln_sd", "ln_y", "ln_u")]
        m_full, m_free = sem("misc_full"), sem("misc_free")
        qk_raw, qk_sq, qk_ok, qT_ok = [sem(n) for n in ("qk_raw", "qk_sq", "qk_ok", "qT_ok")]
        sc_ok, mx_ok, ex_ok, pt_ok, pt_a, pt_d, pv_ok = [sem(n) for n in
            ("scores", "row_max", "probs", "probs_T_ps", "probs_T_a", "probs_T_d", "pv")]
        on_ok = sem("attn_norm")
        sp_hi, sp_lo = sem("branch_hi"), sem("branch_lo")
        yab, yab_used, mg_ok = sem("branches_ps"), sem("branches_used"), sem("merged")
        mg_hi_ok, mg_lo_ok, wo_hi_ok, wo_lo_ok = [sem(n) for n in ("merged_hi", "merged_lo", "wout_hi_ok", "wout_lo_ok")]
        x1_ps, x1_ok, ss7, rs7, h2_ok, h2t_ps, h2t_ok, lg_ps, lg_ok = [sem(n) for n in
            ("x1_ps", "x1_ok", "ss7", "rs7", "h2_ok", "h2T_ps", "h2T_ok", "logits_ps", "logits_ok")]
        r_in, r_exp, a_ok, rc_ps, route_ok = [sem(n) for n in ("r_in", "r_exp", "assign", "rank_ps", "route_ok")]
        ohpb_ok, slot_ps, iota_ok = [sem(n) for n in ("slot_factors", "slot_ps", "iota_ok")]
        w_in0 = [sem(f"wgu_in{i}") for i in range(SLOTS)]
        w_in1 = [sem(f"wed_in{i}") for i in range(SLOTS)]
        ic_ok, hg_zero = sem("index_col"), sem("hg_zero")
        hg_in = [sem("hg_in0"), sem("hg_in1")]
        hgt_ps, hgt_ok, gu_ps, sil_ok, mid_ok, mt_ps, mt_ok, y_ps, y_a, y_d_ok = [sem(n) for n in
            ("hgT_ps", "hgT_ok", "gate_up", "silu", "mid", "midT_ps", "midT_ok", "y_ps", "y_sb_a", "y_sb_d")]
        y_out = [sem("y_out0"), sem("y_out1")]
        y_all = sem("y_all")
        wt_ok = sem("token_weights")
        x1_out, bexp_ok, wc_ok, stok_ok, swt_ps = [sem(n) for n in ("x1_out", "block_experts", "weight_col", "slot_tokens", "slot_weights_ps")]

        x_v = x[0].rearrange("(j p) d -> j p d", p=P)
        out_v = out[0].rearrange("(j p) d -> j p d", p=P)
        win_v = w_in[0].rearrange("(k p) c -> p k c", p=P)
        wo_v = w_o_mla[0].rearrange("(k p) c -> p k c", p=P)
        wco_v = w_conv_out[0].rearrange("(k p) c -> p k c", p=P)

        def unit_col(u):
            if u < GLU_UNITS:
                return DOWN + (CW if u % 2 == 0 else 0) + (u // 2) * P
            return DOWN + 2 * CW + (u - GLU_UNITS) * P

        PREP = ["qdT", "q0", "q1", "kv0", "kv1", "qT0", "qT1", "kT0", "kT1"]

        GU_BANK = (2, 6)
        WOUT_ORDER = (4, 5, 6, 7, 0, 1, 2, 3)
        EARLY = ((NTILE - 1) * HEADS + 4, (NTILE - 1) * HEADS + 5)

        def slots(j, h, part):
            got = [("oT", j - 1)] if (h, part) == (2, 1) and j else []
            nxt = {(0, 0): "qdT", (0, 1): "q0", (1, 0): "q1", (1, 1): "kv0", (2, 0): "kv1",
                   (4, 1): "qT0", (5, 0): "qT1", (5, 1): "kT0", (6, 0): "kT1"}
            return got + ([(nxt[h, part], j + 1)] if j + 1 < NTILE and (h, part) in nxt else [])

        order = [(k, 0) for k in PREP]
        for j in range(NTILE):
            for h in range(HEADS):
                order += slots(j, h, 0) + slots(j, h, 1)
        order.append(("oT", NTILE - 1))
        at_stage = {s: i for i, s in enumerate(order)}

        block = ctx.enter_context(nc.Block())

        @block.sync
        def _(sp):
            sp.dma_start(xs[:, 0, :], x_v[0]).then_inc(x_in[0], 16)
            sp.dma_start(xs[:, 1, :], x_v[1]).then_inc(x_in[1], 16)
            for row, src in ((V_NQ, g_qk_q), (V_NK, g_qk_k)):
                for half in range(2):
                    sp.dma_start(vecs[row:row + 1, half * NOPE:(half + 1) * NOPE], src[:, 0:NOPE]).then_inc(small_in, 16)
            sp.dma_start(dwr[:, :], w_dw[0].rearrange("t (c p) -> (t c) p", p=P)).then_inc(small_in, 16)
            sp.dma_start(posi[:, :], positions[0].rearrange("(a p) -> a p", p=P)).then_inc(small_in, 16)
            sp.dma_start(xs[:, 2, :], x_v[2]).then_inc(x_in[2], 16)
            sp.dma_start(wdn_raw[:, :, :], win_v[:, :, 0:DOWN]).then_inc(wdn_in, 16)
            for j in range(3, NTILE):
                sp.dma_start(xs[:, j, :], x_v[j]).then_inc(x_in[j], 16)
            sp.dma_start(gqk[:, 0, :], g_qk_q[0].partition_broadcast(P)).then_inc(late_in, 16)
            sp.dma_start(gqk[:, 1, :], g_qk_k[0].partition_broadcast(P)).then_inc(late_in, 16)
            sp.wait_ge(dn_hi, 1)
            sp.wait_ge(dn_lo, 1)
            for u in range(IN_UNITS):
                if u >= 2:
                    sp.wait_ge(u_hi, u - 1)
                    sp.wait_ge(u_lo, u - 1)
                sp.dma_start(ws_raw[:, u % 2, :, :], win_v[:, :, unit_col(u):unit_col(u) + P]).then_inc(ws_in[u % 2], 16)
            sp.wait_ge(u_hi, IN_UNITS)
            sp.wait_ge(u_lo, IN_UNITS)
            sp.dma_start(wuq[:, :, :], w_uq[0].rearrange("(k p) c -> p k c", p=P)).then_inc(uq_in, 16)
            sp.wait_ge(u_mm, IN_UNITS - 1)
            sp.dma_start(wukv[:, :], w_ukv[0]).then_inc(uq_in, 16)
            sp.wait_ge(m_full, at_stage["kT1", NTILE - 1] + 1)
            for c in range(OUT_UNITS):
                u = IN_UNITS + c
                if c >= 2:
                    sp.wait_ge(u_hi, u - 1)
                    sp.wait_ge(u_lo, u - 1)
                sp.dma_start(ws_raw[:, u % 2, 0:4, :], wo_v[:, :, c * P:(c + 1) * P]).then_inc(ws_in[u % 2], 16)
                sp.dma_start(ws_raw[:, u % 2, 4:8, :], wco_v[:, :, c * P:(c + 1) * P]).then_inc(ws_in[u % 2], 16)
                if c == 1:
                    sp.wait_ge(sp_hi, 4)
                    sp.wait_ge(sp_lo, 4)
                    sp.dma_start(wout[:, :, :], w_out[0].rearrange("(k p) c -> p k c", p=P)).then_inc(wout_in, 16)
            sp.wait_ge(u_mm, IN_UNITS + OUT_UNITS)
            sp.dma_start(wr[:, :, 0:NG], w_group_router[0].rearrange("(k p) c -> p k c", p=P)).then_inc(gff_in, 16)
            sp.dma_start(wr[:, :, NG:NG + NE], w_expert_router[0].rearrange("(k p) c -> p k c", p=P)).then_inc(gff_in, 16)
            sp.dma_start(br[:, 0:NG], b_group_router).then_inc(gff_in, 16)
            sp.dma_start(br[:, NG:NG + NE], b_expert_router).then_inc(gff_in, 16)
            sp.dma_start(gffb[:, :], g_ffn[0].partition_broadcast(P)).then_inc(gff_in, 16)
            for j in range(NTILE + 1):
                if j < NTILE:
                    if j >= 2:
                        sp.wait_ge(x1_ok, j - 1)
                    sp.dma_start(xb[:, j % 2, :], x_v[j]).then_inc(xb_in[j % 2], 16)
                if j >= 1:
                    sp.wait_ge(h2_ok, j)
                    sp.dma_start(h2_d[(j - 1) * P:j * P, :], h2[:, (j - 1) % 2, :]).then_inc(h2_out[(j - 1) % 2], 16)
                    sp.dma_start(out_v[j - 1], x1[:, j - 1, :]).then_inc(x1_out, 16)
            sp.wait_ge(route_ok, 1)
            ntrip = sp.value_load(ntrip_i[0:1, 0:1], min_val=2, max_val=MAXB // SLOTS)

            def load_expert(b, e, used):
                if used is not None:
                    sp.wait_ge(gu_ps, used)
                sp.dma_start(wgu[b][:, :, 0:FF], w_e_gate[0][bass.ds(e, 1), :, :].rearrange("e (k p) f -> p (e k) f", p=P)).then_inc(w_in0[b], 16)
                sp.dma_start(wgu[b][:, :, FF:2 * FF], w_e_up[0][bass.ds(e, 1), :, :].rearrange("e (k p) f -> p (e k) f", p=P)).then_inc(w_in0[b], 16)
                if used is not None:
                    sp.wait_ge(y_ps, used)
                sp.dma_start(wed[b][:, :, :], w_e_down[0][bass.ds(e, 1), :, :].rearrange("e (k p) f -> p (e k) f", p=P)).then_inc(w_in1[b], 16)

            for q in range(SLOTS):
                if q == 1:
                    sp.wait_ge(hg_in[0], 16)
                if q == 2:
                    for i in range(2):
                        sp.wait_ge(h2_out[i], 16 * NTILE // 2)
                if q == 3:
                    sp.wait_ge(stok_ok, 1)
                load_expert(q, sp.value_load(bexp[0:1, q:q + 1], min_val=0, max_val=NE - 1), None)
            sp.wait_ge(bexp_ok, 1)
            with sp.Fori(0, ntrip - 1) as i:
                for q in range(SLOTS):
                    e = sp.value_load(bexp[0:1, bass.ds(i * SLOTS + (q + SLOTS), 1)], min_val=0, max_val=NE - 1)
                    load_expert(q, e, i * SLOTS + (q + 1))
            sp.wait_ge(y_all, 2)

        @block.gpsimd
        def _(pool):
            g = nc.gpsimd
            n = [0]

            def link(ins):
                n[0] += 1
                ins.then_inc(pch, 1)
                pool.wait_ge(pch, n[0])

            link(g.memset(ident[:, :], 0.0))
            g.affine_select(out=ident[:, :], in_=ident[:, :], compare_op=ALU.not_equal, fill=1.0, base=0,
                            pattern=[[-1, P]], channel_multiplier=1).then_inc(ident_ok, 1)
            g.memset(mean_w[:, :], 1.0 / CW)
            g.memset(tick_a[:, :], 0.0)
            g.memset(eps[:, :], EPS)
            g.memset(mhalf[:, :, :], -0.5)
            g.memset(tick_p[:, :], 0.0)
            for f in range(HALF):
                g.memset(invf[:, f:f + 1], float(THETA ** (-f / HALF)))
            g.memset(ones_b[:, :], 1.0)
            g.memset(one32[:, :], 1.0)
            g.memset(one_row[:, :], 1.0)
            link(g.memset(before[:, :], 0.0))
            g.affine_select(out=before[:, :], in_=before[:, :], compare_op=ALU.is_ge, fill=1.0, base=0,
                            pattern=[[-1, P]], channel_multiplier=1)
            link(g.memset(mrow[:, :, :], 0.0))
            g.memset(mrow[:, 0, 0:CHUNK], 1.0)
            g.memset(mrow[:, 1, CHUNK:P], MASKED)
            g.iota(trow[:, :], pattern=[[P, NTILE]], base=-T, channel_multiplier=1, allow_small_or_imprecise_dtypes=True)
            g.iota(down4[:, :], pattern=[[-1, NG]], base=NG, channel_multiplier=0, allow_small_or_imprecise_dtypes=True)
            g.iota(down32[:, :], pattern=[[-1, NE]], base=NE, channel_multiplier=0, allow_small_or_imprecise_dtypes=True)
            g.iota(io8[:, :], pattern=[[P, 8]], base=0, channel_multiplier=0, allow_small_or_imprecise_dtypes=True)
            g.iota(io4[:, :], pattern=[[SLOTS, MAXB // SLOTS]], base=0, channel_multiplier=0, allow_small_or_imprecise_dtypes=True).then_inc(consts, 1)

            def rstd(dst, src, count, power):
                link(g.tensor_scalar(dst, src, 1.0 / count, EPS, ALU.mult, ALU.add))
                return g.tensor_tensor(dst, dst, power, ALU.pow)

            for j in range(NTILE):
                pool.wait_ge(s_ss, j + 1)
                rstd(rs1[:, j:j + 1], ss1[:, j:j + 1], D, mhalf[:, 0, 0:1]).then_inc(s_rs, 1)
            pool.wait_ge(ss3_ok, NTILE)
            for c, width in enumerate((QL, KVL)):
                rstd(ss3[:, c, :], ss3[:, c, :], width, mhalf[:, 0, :]).then_inc(down_rs, 1)
            for t in range(NTILE):
                pool.wait_ge(head_ss, 2 * t + 1)
                link(rstd(ssh[:, 0, :], ssh[:, 0, :], QK, mhalf[:, 0, :]))
                link(g.tensor_tensor(qn[:, :, :], qn[:, :, :], ssh[:, 0, :].unsqueeze(2).broadcast_to([P, HEADS, QK]), ALU.mult))
                rot = qn[:, :, NOPE:QK]
                if t == 0:
                    pool.wait_ge(tab_ok, 1)
                g.tensor_tensor(tmpr[:, :, 0:HALF], rot[:, :, HALF:ROPE], rtab[:, 1, t:t + 1, 0:HALF].broadcast_to([P, HEADS, HALF]), ALU.mult)
                link(g.tensor_tensor(tmpr[:, :, HALF:ROPE], rot[:, :, 0:HALF], rtab[:, 1, t:t + 1, HALF:ROPE].broadcast_to([P, HEADS, HALF]), ALU.mult))
                link(g.tensor_tensor(rot, rot, rtab[:, 0, t:t + 1, :].broadcast_to([P, HEADS, ROPE]), ALU.mult))
                g.tensor_tensor(rot, rot, tmpr[:, :, :], ALU.add).then_inc(qk_ok, 1)
                pool.wait_ge(head_ss, 2 * t + 2)
                link(rstd(ssh[:, 1, :], ssh[:, 1, :], QK, mhalf[:, 0, :]))
                g.tensor_tensor(kn[:, :, 0:NOPE], kn[:, :, 0:NOPE], ssh[:, 1, :].unsqueeze(2).broadcast_to([P, HEADS, NOPE]), ALU.mult)
                g.tensor_tensor(kn[:, :, NOPE:QK], krr[:, t:t + 1, :].broadcast_to([P, HEADS, ROPE]),
                                ssh[:, 1, :].unsqueeze(2).broadcast_to([P, HEADS, ROPE]), ALU.mult).then_inc(qk_ok, 1)
            for j in range(NTILE):
                pool.wait_ge(ss7, j + 1)
                rstd(rs1[:, j:j + 1], ss1[:, j:j + 1], D, mhalf[:, 0, 0:1]).then_inc(rs7, 1)
            g.iota(iop[:, :], pattern=[[1, P]], base=0, channel_multiplier=0, allow_small_or_imprecise_dtypes=True)
            g.iota(iob[:, :], pattern=[[1, NBT]], base=0, channel_multiplier=0, allow_small_or_imprecise_dtypes=True).then_inc(iota_ok, 1)
            pool.wait_ge(a_ok, 1)
            for b in range(2):
                g.memset(hg[b][:, :], 0.0).then_inc(hg_zero, 1)
            for b in range(2):
                pool.dma_start(first_d[b:b + 1, :].rearrange("a p -> p a"), ident[:, 0:1]).then_inc(y_out[b], 16)
            for i in range(2):
                pool.wait_ge(h2_out[i], 16 * NTILE // 2)
            pool.wait_ge(route_ok, 1)
            ntrip = pool.value_load(ntrip_i[0:1, 0:1], min_val=2, max_val=MAXB // SLOTS)

            def gather(b, count):
                pool.wait_ge(ic_ok, count)
                pool.sem_inc(pch, 1)
                g.indirect_dma_start(out=hg[b][:, :], out_offset=None, in_=h2_d,
                                     in_offset=bass.IndirectOffsetOnAxis(ap=icol[b][:, 0:1].bitcast(U32), axis=0),
                                     bounds_check=T - 1, oob_is_err=False).then_inc(hg_in[b], 16)

            def scatter(b, count, before):
                pool.wait_ge(y_a, count + 1)
                pool.sem_inc(pch, 1)
                pool.wait_ge(y_d_ok, count + 1)
                pool.sem_inc(pch, 1)
                pool.wait_ge(y_out[1 - b], before)
                pool.sem_inc(pch, 1)
                g.indirect_dma_start(out=out[0], out_offset=bass.IndirectOffsetOnAxis(ap=rcol[b][:, 0:1].bitcast(U32), axis=0),
                                     in_=yb[b][:, :], in_offset=None, compute_op=ALU.add,
                                     bounds_check=T - 1, oob_is_err=False).then_inc(y_out[b], 16)

            pool.wait_ge(hg_zero, 2)
            for k in range(SLOTS):
                gather(k % 2, k + 1)
            pool.wait_ge(x1_out, 16 * NTILE)
            with pool.Fori(0, ntrip) as i:
                for q in range(SLOTS):
                    gather(q % 2, i * SLOTS + (q + SLOTS + 1))
                    scatter(q % 2, i * SLOTS + (q + 1), i * (8 * SLOTS) + 16 * ((q + 1) // 2 + 1))
            for b in range(2):
                pool.wait_ge(hg_in[b], ntrip * (8 * SLOTS) + 8 * SLOTS)
                pool.wait_ge(y_out[b], ntrip * (8 * SLOTS) + 16)
                pool.sem_inc(y_all, 1)

        @block.scalar
        def _(act):
            a = nc.scalar

            for row, src, n in ((V_GM, g_mix, 8), (V_BG, b_gates, 16), (V_BD, b_dw, 4),
                                (V_GL, g_conv_ln, 4), (V_BL, b_conv_ln, 4), (V_GQ, g_q_lora, 2),
                                (V_GK, g_kv_lora, 1)):
                act.dma_start(vecs[row:row + n, :], src[0].rearrange("(a p) -> a p", p=P)).then_inc(small_in, 16)

            def sumsq(j):
                act.wait_ge(x_in[j], 16)
                if j:
                    act.wait_ge(s_ss, j)
                a.activation(sqj[:, :], xs[:, j, :], ACT.Square, accum_out=ss1[:, j:j + 1]).then_inc(s_ss, 1)

            def down_out(j):
                act.wait_ge(dn_ps, j + 1)
                a.activation(qd[:, j, :], pb[:, 6 + j % 2, 0:DOWN], ACT.Copy).then_inc(dn_ev, 1)
                act.wait_ge(dn_ev, j + 1)
                if j:
                    act.wait_ge(ss3_ok, j)
                for s, (lo, hi) in enumerate(((0, QL), (QL, QL + KVL), (QL + KVL, DOWN))):
                    i = a.activation(sq3[:, lo:hi], qd[:, j, lo:hi], ACT.Square, accum_out=ss3[:, s, j:j + 1])
                i.then_inc(ss3_ok, 1)

            sumsq(0)
            sumsq(1)
            act.wait_ge(wdn_in, 16)
            a.activation(wdn[0][:, :, :], wdn_raw[:, :, :], ACT.Copy).then_inc(dn_hi, 1)
            sumsq(2)
            for j in range(NTILE):
                act.wait_ge(s_hp, j + 1)
                a.activation(hT[0][:, :, j * P:(j + 1) * P], hp[:, j % 2, :, :], ACT.Copy).then_inc(s_hi, 1)
                if j + 3 < NTILE:
                    sumsq(j + 3)
                if j:
                    down_out(j - 1)
            down_out(NTILE - 1)

            def unit_hi(u):
                act.wait_ge(ws_in[u % 2], 16 * (u // 2 + 1) if u < IN_UNITS else 16 * (IN_UNITS // 2) + 32 * ((u - IN_UNITS) // 2 + 1))
                if u >= 2:
                    act.wait_ge(u_mm, u - 1)
                a.activation(ws[0][:, u % 2, :, :], ws_raw[:, u % 2, :, :], ACT.Copy).then_inc(u_hi, 1)

            unit_hi(0)
            unit_hi(1)
            for u in range(IN_UNITS):
                act.wait_ge(u_mm, u + 1)
                src = banks(2 * (u % 2) + 2, 2)
                if u < GLU_UNITS:
                    if u % 2 == 0:
                        if u >= 2:
                            act.wait_ge(u_ev, u)
                        a.activation(sg[:, :], src, ACT.Sigmoid).then_inc(u_ev, 1)
                else:
                    c = u - GLU_UNITS
                    if c == 0:
                        act.wait_ge(u_ev, GLU_UNITS)
                    if c in (12, 14):
                        act.wait_ge(conv_done, c // 2 - 3)
                    a.activation(gates[:, c, :], src, ACT.Sigmoid, bias=vcol[:, V_BG + c:V_BG + c + 1]).then_inc(u_ev, 1)
                if u + 2 < IN_UNITS:
                    unit_hi(u + 2)
                if u == 1:
                    act.wait_ge(sin_in, 1)
                    a.activation(sincos[:, :, :, :], sincos[:, :, :, :], ACT.Sin).then_inc(sin_ok, 1)
                if u == LN_UNIT:
                    for c in range(NC):
                        act.wait_ge(ln_d, c + 1)
                        a.activation(lnt[c][:, :], cv[:, c, :], ACT.Square).then_inc(ln_sq, 1)
                if u == LN_UNIT + 1:
                    act.wait_ge(ln_var, 1)
                    a.activation(lnr[:, :], banks(6, 2), ACT.Sqrt, bias=eps[:, :]).then_inc(ln_sd, 1)
                if u == LN_UNIT + 2:
                    for c in range(NC):
                        act.wait_ge(ln_y, c + 1)
                        a.activation(cv[:, c, :], cv[:, c, :], ACT.Silu, scale=vcol[:, V_GL + c:V_GL + c + 1],
                                     bias=vcol[:, V_BL + c:V_BL + c + 1]).then_inc(ln_u, 1)

            def misc(kind, t):
                s = at_stage[kind, t]
                M = pb[:, 7, :]
                if kind in ("q0", "q1"):
                    act.wait_ge(m_full, s + 1)
                    h = 4 * (kind == "q1")
                    a.activation(qn[:, h:h + 4, :], M[:, 0:4 * QK].rearrange("p (h c) -> p h c", h=4), ACT.Copy).then_inc(m_free, 1)
                    if kind == "q1":
                        act.wait_ge(m_free, s + 1)
                        if t:
                            act.wait_ge(head_ss, 2 * t)
                        a.activation(sq2[:, :, :], qn[:, :, :], ACT.Square).then_inc(qk_sq, 1)
                if kind in ("kv0", "kv1"):
                    act.wait_ge(m_full, s + 1)
                    h = 4 * (kind == "kv1")
                    kv = M.rearrange("p (h c) -> p h c", h=4)
                    a.activation(kn[:, h:h + 4, 0:NOPE], kv[:, :, 0:NOPE], ACT.Copy)
                    a.activation(vv[:, t, h * VD:(h + 4) * VD].rearrange("p (h c) -> p h c", h=4), kv[:, :, NOPE:], ACT.Copy).then_inc(m_free, 1)
                    if kind == "kv1":
                        act.wait_ge(m_free, s + 1)
                        act.wait_ge(head_ss, 2 * t + 1)
                        a.activation(sq2[:, :, 0:NOPE], kn[:, :, 0:NOPE], ACT.Square).then_inc(qk_sq, 1)
                if kind in ("qT0", "qT1"):
                    act.wait_ge(m_full, s + 1)
                    h = 4 * (kind == "qT1")
                    a.activation(qT[0:QK, t % 2, h * P:(h + 4) * P], M[0:QK, :], ACT.Copy, scale=vcol[0:QK, V_NQ:V_NQ + 1]).then_inc(m_free, 1)
                if kind == "oT":
                    act.wait_ge(m_full, s + 1)
                    a.activation(attnT[:, :, t * P:(t + 1) * P], M.rearrange("p (c t) -> p c t", c=4), ACT.Copy).then_inc(m_free, 1)

            def exps(n):
                j, h = divmod(n, HEADS)
                w = (j + 1) * P
                act.wait_ge(mx_ok, n + 1)
                if n >= 2:
                    act.wait_ge(pt_ok, n - 1)
                a.activation(pr[:, n % 2, 0:w], banks(2 * (n % 2), 2)[:, 0:w], ACT.Exp,
                             bias=nmax[:, n % 2:n % 2 + 1], accum_out=rsum[:, j % 2, h:h + 1]).then_inc(ex_ok, 1)

            for k in PREP:
                misc(k, 0)
            exps(0)
            exps(1)
            for n in range(NTILE * HEADS):
                j, h = divmod(n, HEADS)
                if j >= 4:
                    act.wait_ge(pt_ok, n + 1)
                    act.wait_ge(pv_ok, n - 1)
                    a.activation(pT[:, n % 2, 512:(j + 1) * P], banks(5, 1)[:, 0:(j + 1) * P - 512], ACT.Copy).then_inc(pt_a, 1)
                for k, t in slots(j, h, 0):
                    misc(k, t)
                if n + 2 < NTILE * HEADS:
                    exps(n + 2)
                for k, t in slots(j, h, 1):
                    misc(k, t)
                if n in EARLY:
                    unit_hi(IN_UNITS + EARLY.index(n))
            misc("oT", NTILE - 1)

            for c in range(2):
                a.activation(aT[0][:, 4 + 2 * c:6 + 2 * c, :], cv[:, 2 * c:2 * c + 2, :], ACT.Copy).then_inc(sp_hi, 1)
            act.wait_ge(m_free, len(order))
            for c in range(2):
                a.activation(aT[0][:, 2 * c:2 * c + 2, :], attnT[:, 2 * c:2 * c + 2, :], ACT.Copy).then_inc(sp_hi, 1)

            def wout_half(k):
                if k in (0, 2):
                    act.wait_ge(u_mm, IN_UNITS + OUT_UNITS - 1 + k // 2)
                a.activation(wout_hi[k][:, :], wout[:, k, :], ACT.Copy).then_inc(wo_hi_ok, 1)

            for c in range(OUT_UNITS):
                if c + 2 < OUT_UNITS:
                    unit_hi(IN_UNITS + c + 2)
                if c == 2:
                    act.wait_ge(wout_in, 16)
                if 2 <= c < 6:
                    wout_half(c + 2)
                if c == 7:
                    wout_half(0)
                    wout_half(1)
                act.wait_ge(mg_ok, c + 1)
                a.activation(mg[0][:, c, :], gates[:, c, :], ACT.Copy).then_inc(mg_hi_ok, 1)
            wout_half(2)
            wout_half(3)
            def half_two(j):
                act.wait_ge(h2t_ps, j + 1)
                if j >= 2:
                    act.wait_ge(lg_ps, j - 1)
                a.activation(h2T[:, j % 2, :, :], banks(4, 2).rearrange("p (k t) -> p k t", k=KD), ACT.Copy).then_inc(h2t_ok, 1)

            for j in range(NTILE):
                act.wait_ge(x1_ok, j + 1)
                if j:
                    act.wait_ge(ss7, j)
                a.activation(sq7[:, :], x1[:, j, :], ACT.Square, accum_out=ss1[:, j:j + 1]).then_inc(ss7, 1)
                if j >= 1:
                    half_two(j - 1)
            half_two(NTILE - 1)
            for k in range(2):
                act.wait_ge(r_in, k + 1)
                if k == 0:
                    a.activation(tg[:, :, :], tg[:, :, :], ACT.Exp).then_inc(r_exp, 1)
                else:
                    a.activation(s8[3][:, :], s8[3][:, :], ACT.Exp).then_inc(r_exp, 1)

            act.wait_ge(route_ok, 1)
            ntrip = act.value_load(ntrip_i[0:1, 0:1], min_val=2, max_val=MAXB // SLOTS)
            with act.Fori(0, ntrip) as i:
                for q in range(SLOTS):
                    nth = i * SLOTS + (q + 1)
                    act.wait_ge(gu_ps, nth)
                    a.activation(sil[:, :], pb[:, GU_BANK[q % 2], 0:FF], ACT.Silu).then_inc(sil_ok, 1)
                    act.wait_ge(y_ps, nth)
                    act.wait_ge(wc_ok, nth)
                    a.activation(yb[q % 2][:, 0:512], pb[:, 4, :], ACT.Copy, scale=wcol[q % 2][:, :]).then_inc(y_a, 1)

        @block.vector
        def _(dve):
            v = nc.vector
            n = [0]

            def link(ins):
                n[0] += 1
                ins.then_inc(dch, 1)
                dve.wait_ge(dch, n[0])

            def diagonal(j):
                dve.wait_ge(s_rs, j + 1)
                v.tensor_scalar(diag[:, j % 2, :], ident[:, :], rs1[:, j:j + 1], None, ALU.mult).then_inc(s_xn, 1)

            dve.wait_ge(ident_ok, 1)
            diagonal(0)
            dve.wait_ge(consts, 1)
            dve.wait_ge(small_in, 16 * 13)
            link(v.tensor_copy(posf[:, :], posi[:, :]))
            v.tensor_copy(posf[:, :], posf[:, :]).then_inc(vec_c, 1)
            dve.wait_ge(vec_t, 1)
            v.tensor_copy(vcol[:, 0:NV], pb[:, 6, 0:NV])
            v.tensor_copy(dwc[:, :], pb[:, 6, 64:64 + TAPS * NC])
            link(v.tensor_copy(posc[:, :], pb[:, 6, 256:256 + NTILE]))
            v.memset(vcol[NOPE:P, V_NQ:V_NQ + 2], 1.0)
            v.tensor_scalar(vcol[0:NOPE, V_NQ:V_NQ + 1], vcol[0:NOPE, V_NQ:V_NQ + 1], QK ** -0.5, None, ALU.mult)

            def lo_half(j):
                dve.wait_ge(s_hi, j + 1)
                v.tensor_tensor(hT[1][:, :, j * P:(j + 1) * P], hp[:, j % 2, :, :],
                                hT[0][:, :, j * P:(j + 1) * P].bitcast(F32), ALU.subtract).then_inc(s_lo, 1)

            diagonal(1)
            for j in range(NTILE):
                dve.wait_ge(s_xt, j + 1)
                if j >= 2:
                    dve.wait_ge(s_hi, j - 1)
                    dve.wait_ge(s_lo, j - 1)
                v.tensor_tensor(hp[:, j % 2, :, :], banks(2 * (j % 2), 2).rearrange("p (k t) -> p k t", k=KD),
                                vcol[:, V_GM:V_GM + KD].unsqueeze(2).broadcast_to([P, KD, P]), ALU.mult).then_inc(s_hp, 1)
                if j + 2 < NTILE:
                    diagonal(j + 2)
                if j == 0:
                    dve.wait_ge(dn_hi, 1)
                    v.tensor_tensor(wdn[1][:, :, :], wdn_raw[:, :, :], wdn[0][:, :, :].bitcast(F32), ALU.subtract).then_inc(dn_lo, 1)
                lo_half(j)

            def unit_lo(u):
                dve.wait_ge(u_hi, u + 1)
                if u >= 2:
                    dve.wait_ge(u_mm, u - 1)
                v.tensor_tensor(ws[1][:, u % 2, :, :], ws_raw[:, u % 2, :, :], ws[0][:, u % 2, :, :].bitcast(F32), ALU.subtract).then_inc(u_lo, 1)

            def tap(k):
                c, t = divmod(k, TAPS)
                w = dwc[:, t * NC + c:t * NC + c + 1]
                src = up[c][:, t:t + T]
                if t == 0:
                    link(v.tensor_scalar(cv[:, c, :], src, w, vcol[:, V_BD + c:V_BD + c + 1], ALU.mult, ALU.add))
                else:
                    i = v.scalar_tensor_tensor(out=cv[:, c, :], in0=src, scalar=w, in1=cv[:, c, :], op0=ALU.mult, op1=ALU.add)
                    if t < TAPS - 1:
                        link(i)
                    else:
                        i.then_inc(conv_done, 1)

            def rotary_angles():
                dve.wait_ge(late_in, 16 * 2)
                link(v.tensor_scalar(gqk[:, 0, :], gqk[:, 0, :], QK ** -0.5, None, ALU.mult))
                link(v.tensor_tensor(ang[:, :, :], posc[:, :].unsqueeze(2).broadcast_to([P, NTILE, HALF]),
                                     invf[:, :].unsqueeze(1).broadcast_to([P, NTILE, HALF]), ALU.mult))
                TWO_PI = 6.283185307179586
                link(v.tensor_scalar(turns[:, :, :], ang[:, :, :], 1.0 / TWO_PI, 12582912.0, ALU.mult, ALU.add))
                link(v.tensor_scalar(turns[:, :, :], turns[:, :, :], 12582912.0, None, ALU.subtract))
                left = TWO_PI
                for bits in (-5, -14, -23):
                    part = float(int(left / 2.0 ** bits)) * 2.0 ** bits
                    left -= part
                    link(v.scalar_tensor_tensor(out=ang[:, :, :], in0=turns[:, :, :], scalar=-part, in1=ang[:, :, :], op0=ALU.mult, op1=ALU.add))
                link(v.scalar_tensor_tensor(out=ang[:, :, :], in0=turns[:, :, :], scalar=-left, in1=ang[:, :, :], op0=ALU.mult, op1=ALU.add))
                PI = 3.1415925
                link(v.tensor_scalar(turns[:, :, :], ang[:, :, :], TWO_PI / 4, TWO_PI / 2, ALU.add, ALU.is_gt))
                link(v.scalar_tensor_tensor(out=turns[:, :, :], in0=turns[:, :, :], scalar=-TWO_PI, in1=ang[:, :, :], op0=ALU.mult, op1=ALU.add))
                link(v.tensor_scalar(turns[:, :, :], turns[:, :, :], TWO_PI / 4, PI, ALU.add, ALU.min))
                link(v.tensor_scalar(sincos[:, 1, :, :], turns[:, :, :], -PI, None, ALU.max))
                v.tensor_scalar(sincos[:, 0, :, :], ang[:, :, :], PI, -PI, ALU.min, ALU.max).then_inc(sin_in, 1)

            def rotary_tables():
                dve.wait_ge(sin_ok, 1)
                sin, cos = sincos[:, 0, :, :], sincos[:, 1, :, :]

                def gain(w, half):
                    return gqk[:, w, NOPE + half * HALF:NOPE + (half + 1) * HALF].unsqueeze(1).broadcast_to([P, NTILE, HALF])

                v.tensor_tensor(rtab[:, 0, :, 0:HALF], cos, gain(0, 0), ALU.mult)
                v.tensor_tensor(rtab[:, 0, :, HALF:ROPE], cos, gain(0, 1), ALU.mult)
                v.scalar_tensor_tensor(out=rtab[:, 1, :, 0:HALF], in0=sin, scalar=-1.0, in1=gain(0, 1), op0=ALU.mult, op1=ALU.mult)
                v.tensor_tensor(rtab[:, 1, :, HALF:ROPE], sin, gain(0, 0), ALU.mult)
                link(v.tensor_tensor(krr[:, :, :], qd[:, :, QL + KVL:DOWN], gqk[:, 1, NOPE:QK].unsqueeze(1).broadcast_to([P, NTILE, ROPE]), ALU.mult))
                v.tensor_tensor(krt[:, :, 0:HALF], krr[:, :, HALF:ROPE], sin, ALU.mult)
                link(v.tensor_tensor(krt[:, :, HALF:ROPE], krr[:, :, 0:HALF], sin, ALU.mult))
                v.tensor_tensor(krr[:, :, 0:HALF], krr[:, :, 0:HALF], cos, ALU.mult)
                link(v.tensor_tensor(krr[:, :, HALF:ROPE], krr[:, :, HALF:ROPE], cos, ALU.mult))
                v.tensor_tensor(krr[:, :, 0:HALF], krr[:, :, 0:HALF], krt[:, :, 0:HALF], ALU.subtract)
                v.tensor_tensor(krr[:, :, HALF:ROPE], krr[:, :, HALF:ROPE], krt[:, :, HALF:ROPE], ALU.add).then_inc(tab_ok, 1)

            unit_lo(0)
            unit_lo(1)
            taps_done = 0
            for u in range(IN_UNITS):
                if u == 0:
                    dve.wait_ge(down_rs, 2)
                    v.tensor_tensor(qd[:, :, 0:QL], qd[:, :, 0:QL], ss3[:, 0, :].unsqueeze(2).broadcast_to([P, NTILE, QL]), ALU.mult)
                    v.tensor_tensor(qd[:, :, QL:QL + KVL], qd[:, :, QL:QL + KVL], ss3[:, 1, :].unsqueeze(2).broadcast_to([P, NTILE, KVL]), ALU.mult).then_inc(qd_ok, 1)
                if u < GLU_UNITS and u % 2 == 1:
                    dve.wait_ge(u_mm, u + 1)
                    dve.wait_ge(u_ev, u)
                    v.memset(up[u // 2][:, 0:PAD], 0.0)
                    v.tensor_tensor(up[u // 2][:, PAD:UW], banks(2 * (u % 2) + 2, 2), sg[:, :], ALU.mult).then_inc(u_ev, 1)
                    dve.wait_ge(u_ev, u + 1)
                if u + 2 < IN_UNITS:
                    unit_lo(u + 2)
                target = min(TAPS * NC, TAPS_PER_UNIT * u)
                if u < GLU_UNITS:
                    target = min(target, TAPS * ((u + 1) // 2))
                for k in range(taps_done, target):
                    tap(k)
                taps_done = max(taps_done, target)
                if u == 1:
                    rotary_angles()
                if u == LN_UNIT - 1:
                    rotary_tables()
                if u == LN_UNIT:
                    dve.wait_ge(ln_mu, 1)
                    for c in range(NC):
                        v.tensor_tensor(cv[:, c, :], cv[:, c, :], banks(0, 2), ALU.subtract).then_inc(ln_d, 1)
                if u == LN_UNIT + 1:
                    dve.wait_ge(ln_sd, 1)
                    link(v.reciprocal(lnr[:, :], lnr[:, :]))
                    for c in range(NC):
                        dve.wait_ge(ln_sq, c + 1)
                        dve.wait_ge(ln_d, c + 1)
                        v.tensor_tensor(cv[:, c, :], cv[:, c, :], lnr[:, :], ALU.mult).then_inc(ln_y, 1)
            def misc(kind, t):
                s = at_stage[kind, t]
                M = pb[:, 7, :]
                if kind == "qdT":
                    dve.wait_ge(m_full, s + 1)
                    v.tensor_tensor(qdT[:, :, :], M[:, 0:3 * P].rearrange("p (c t) -> p c t", c=3),
                                    vcol[:, V_GQ:V_GQ + 3].unsqueeze(2).broadcast_to([P, 3, P]), ALU.mult).then_inc(m_free, 1)
                if kind == "q1":
                    dve.wait_ge(qk_sq, 2 * t + 1)
                    v.reduce_sum(ssh[:, 0, :], sq2[:, :, :], axis=AX.X).then_inc(head_ss, 1)
                if kind == "kv1":
                    dve.wait_ge(qk_sq, 2 * t + 2)
                    link(v.reduce_sum(ssh[:, 1, :], sq2[:, :, 0:NOPE], axis=AX.X))
                    v.tensor_scalar(ssh[:, 1, :], ssh[:, 1, :], ss3[:, 2, t:t + 1], None, ALU.add).then_inc(head_ss, 1)
                if kind in ("kT0", "kT1"):
                    dve.wait_ge(m_full, s + 1)
                    h = 4 * (kind == "kT1")
                    v.tensor_scalar(kT[0:QK, h:h + 4, t * P:(t + 1) * P], M[0:QK, :].rearrange("p (h t) -> p h t", h=4),
                                    vcol[0:QK, V_NK:V_NK + 1], None, ALU.mult).then_inc(m_free, 1)

            def rowmax(n):
                j, h = divmod(n, HEADS)
                dve.wait_ge(sc_ok, n + 1)
                if n >= 2:
                    dve.wait_ge(ex_ok, n - 1)
                v.tensor_reduce(out=nmax[:, n % 2:n % 2 + 1], in_=banks(2 * (n % 2), 2)[:, 0:(j + 1) * P],
                                axis=AX.X, op=ALU.max, negate=True).then_inc(mx_ok, 1)

            for k in PREP:
                misc(k, 0)
            rowmax(0)
            rowmax(1)
            for m in range(NTILE * HEADS):
                j, h = divmod(m, HEADS)
                dve.wait_ge(pt_ok, m + 1)
                if m >= 2:
                    dve.wait_ge(pv_ok, m - 1)
                v.tensor_copy(pT[:, m % 2, 0:min(512, (j + 1) * P)], banks(4, 1)[:, 0:min(512, (j + 1) * P)]).then_inc(pt_d, 1)
                for k, t in slots(j, h, 0):
                    misc(k, t)
                if m + 2 < NTILE * HEADS:
                    rowmax(m + 2)
                for k, t in slots(j, h, 1):
                    misc(k, t)
                if m in EARLY:
                    unit_lo(IN_UNITS + EARLY.index(m))
                if h + 1 == HEADS:
                    dve.wait_ge(ex_ok, m + 1)
                    link(v.reciprocal(rinv[:, :], rsum[:, j % 2, :]))
                    dve.wait_ge(pv_ok, m + 1)
                    if j:
                        dve.wait_ge(m_free, at_stage["oT", j - 1] + 1)
                    v.tensor_tensor(On[:, :].rearrange("p (h c) -> p h c", h=HEADS), pb[:, 6, :].rearrange("p (h c) -> p h c", h=HEADS),
                                    rinv[:, :].unsqueeze(2).broadcast_to([P, HEADS, VD]), ALU.mult).then_inc(on_ok, 1)

            for c in range(2):
                dve.wait_ge(sp_hi, c + 1)
                v.tensor_tensor(aT[1][:, 4 + 2 * c:6 + 2 * c, :], cv[:, 2 * c:2 * c + 2, :], aT[0][:, 4 + 2 * c:6 + 2 * c, :].bitcast(F32), ALU.subtract).then_inc(sp_lo, 1)
            for c in range(2):
                dve.wait_ge(sp_hi, c + 3)
                v.tensor_tensor(aT[1][:, 2 * c:2 * c + 2, :], attnT[:, 2 * c:2 * c + 2, :], aT[0][:, 2 * c:2 * c + 2, :].bitcast(F32), ALU.subtract).then_inc(sp_lo, 1)

            def wout_rest(k, count):
                dve.wait_ge(wo_hi_ok, count)
                v.tensor_tensor(wout_lo[:, k, :], wout[:, k, :], wout_hi[k][:, :].bitcast(F32), ALU.subtract).then_inc(wo_lo_ok, 1)

            def merged_lo(c):
                dve.wait_ge(mg_hi_ok, c + 1)
                v.tensor_tensor(mg[1][:, c, :], gates[:, c, :], mg[0][:, c, :].bitcast(F32), ALU.subtract).then_inc(mg_lo_ok, 1)

            for c in range(OUT_UNITS):
                dve.wait_ge(u_mm, IN_UNITS + c + 1)
                v.tensor_tensor(gates[:, c, :], gates[:, c, :], banks(4 * (c % 2), 2), ALU.mult)
                v.tensor_tensor(gates[:, KD + c, :], gates[:, KD + c, :], banks(4 * (c % 2) + 2, 2), ALU.mult).then_inc(yab_used, 1)
                dve.wait_ge(yab_used, c + 1)
                v.tensor_tensor(gates[:, c, :], gates[:, c, :], gates[:, KD + c, :], ALU.add).then_inc(mg_ok, 1)
                if c + 2 < OUT_UNITS:
                    unit_lo(IN_UNITS + c + 2)
                if 2 <= c < 6:
                    wout_rest(c + 2, c - 1)
                if c == 7:
                    wout_rest(0, 5)
                    wout_rest(1, 6)
                merged_lo(c)
            wout_rest(2, 7)
            wout_rest(3, 8)

            def logits_out(j):
                dve.wait_ge(lg_ps, j + 1)
                v.tensor_copy(lg[:, j, :], pb[:, 6, 0:NG])
                v.tensor_copy(le[:, j, :], pb[:, 6, NG:NG + NE]).then_inc(lg_ok, 1)

            dve.wait_ge(gff_in, 16 * 5)
            for j in range(NTILE):
                dve.wait_ge(x1_ps, j + 1)
                dve.wait_ge(xb_in[j % 2], 16 * (j // 2 + 1))
                v.tensor_tensor(x1[:, j, :], xb[:, j % 2, :], banks(2 * (j % 2), 2), ALU.add).then_inc(x1_ok, 1)
                dve.wait_ge(ss7, j + 1)
                dve.wait_ge(rs7, j + 1)
                if j >= 2:
                    dve.wait_ge(h2_out[j % 2], 16 * (j // 2))
                    dve.wait_ge(h2t_ps, j - 1)
                v.scalar_tensor_tensor(out=h2[:, j % 2, :], in0=x1[:, j, :], scalar=rs1[:, j:j + 1], in1=gffb[:, :], op0=ALU.mult, op1=ALU.mult).then_inc(h2_ok, 1)
                if j >= 2:
                    logits_out(j - 2)
            logits_out(NTILE - 2)
            logits_out(NTILE - 1)
            dve.wait_ge(lg_ok, NTILE)

            def bc(t, n):
                return t.unsqueeze(2).broadcast_to([P, NTILE, n])

            def row(t, n):
                return t.unsqueeze(1).broadcast_to([P, NTILE, n])

            link(v.reduce_max(s8[0][:, :], lg[:, :, :], axis=AX.X))
            link(v.tensor_tensor(tg[:, :, :], lg[:, :, :], bc(s8[0][:, :], NG), ALU.subtract))
            link(v.scalar_tensor_tensor(out=pen[:, :, :], in0=tg[:, :, :], scalar=0.0, in1=row(down4[:, :], NG), op0=ALU.is_ge, op1=ALU.mult))
            v.reduce_max(s8[1][:, :], pen[:, :, :], axis=AX.X).then_inc(r_in, 1)
            dve.wait_ge(r_in, 1)
            link(v.tensor_tensor(pen[:, :, :], pen[:, :, :], bc(s8[1][:, :], NG), ALU.is_equal))
            link(v.tensor_scalar(pen[:, :, :], pen[:, :, :], -1.0, -MASKED, ALU.add, ALU.mult))
            grp = le[:, :, :].rearrange("p j (g e) -> p (j g) e", g=NG)
            link(v.tensor_tensor(grp, grp, pen[:, :, :].rearrange("p j g -> p (j g)").unsqueeze(2).broadcast_to([P, NTILE * NG, EPG]), ALU.add))
            for c in range(2):
                m = s8[1 + c]
                link(v.reduce_max(m[:, :], le[:, :, :], axis=AX.X))
                link(v.tensor_tensor(te[:, :, :], le[:, :, :], bc(m[:, :], NE), ALU.is_ge))
                link(v.tensor_tensor(te[:, :, :], te[:, :, :], row(down32[:, :], NE), ALU.mult))
                link(v.reduce_max(s8[0][:, :], te[:, :, :], axis=AX.X))
                link(v.tensor_tensor(oh[c][:, :, :], te[:, :, :], bc(s8[0][:, :], NE), ALU.is_equal))
                if c == 0:
                    link(v.scalar_tensor_tensor(out=le[:, :, :], in0=oh[0][:, :, :], scalar=2 * MASKED, in1=le[:, :, :], op0=ALU.mult, op1=ALU.add))
            v.tensor_tensor(ab[:, :, :], oh[0][:, :, :], oh[1][:, :, :], ALU.add).then_inc(a_ok, 1)
            v.tensor_tensor(s8[3][:, :], s8[2][:, :], s8[1][:, :], ALU.subtract).then_inc(r_in, 1)
            dve.wait_ge(rc_ps, 1)
            v.memset(pre[:, 0, :], 0.0)
            link(v.tensor_copy(pre[:, 1:NTILE + 1, :], pb[:, 0, NE * NTILE:2 * NE * NTILE].rearrange("p (j e) -> p j e", j=NTILE)))
            for j in range(1, NTILE):
                link(v.tensor_tensor(pre[:, j + 1, :], pre[:, j + 1, :], pre[:, j, :], ALU.add))
            link(v.tensor_tensor(cmp8[:, :, :], pre[:, NTILE, :].unsqueeze(2).broadcast_to([P, NE, 8]), io8[:, :].unsqueeze(1).broadcast_to([P, NE, 8]), ALU.is_gt))
            link(v.reduce_sum(nb[:, :], cmp8[:, :, :], axis=AX.X))
            link(v.tensor_tensor_scan(incl[:, :], one32[:, :], nb[:, :], 0.0, ALU.mult, ALU.add))
            dve.wait_ge(iota_ok, 1)
            def block_experts(lo, hi):
                n = hi - lo
                link(v.tensor_tensor(cmpb[:, lo:hi, :], incl[0:1, :].unsqueeze(1).broadcast_to([1, n, NE]), iob[0:1, lo:hi].unsqueeze(2).broadcast_to([1, n, NE]), ALU.is_le))
                link(v.reduce_sum(bexp_f[:, lo:hi], cmpb[:, lo:hi, :], axis=AX.X))
                return v.tensor_scalar(bexp[:, lo:hi], bexp_f[:, lo:hi], float(NE - 1), None, ALU.min)

            v.tensor_scalar(cmp4[:, :], io4[:, :], incl[0:1, NE - 1:NE], None, ALU.is_lt)
            block_experts(0, SLOTS)
            link(v.reduce_sum(ntrip_f[:, :], cmp4[:, :], axis=AX.X))
            v.tensor_copy(ntrip_i[:, 0:1], ntrip_f[:, :])
            v.tensor_scalar(ntrip_i[:, 1:2], ntrip_f[:, :], 1.0, None, ALU.subtract).then_inc(route_ok, 1)
            v.tensor_tensor(rank[:, :, :], pb[:, 0, 0:NE * NTILE].rearrange("p (j e) -> p j e", j=NTILE), pre[:, 0:NTILE, :], ALU.add)
            link(v.tensor_tensor(b128[:, :], incl[:, :], nb[:, :], ALU.subtract))
            link(v.scalar_tensor_tensor(out=rank[:, :, :], in0=row(b128[:, :], NE), scalar=float(P), in1=rank[:, :, :], op0=ALU.mult, op1=ALU.add))
            for c in range(2):
                link(v.tensor_tensor(oh[c][:, :, :], oh[c][:, :, :], rank[:, :, :], ALU.mult))
            for c in range(2):
                i = v.reduce_sum(pos2[:, c, :], oh[c][:, :, :], axis=AX.X)
            link(i)
            link(v.tensor_copy(pidx[:, :, :], pos2[:, :, :]))
            v.tensor_single_scalar(phi_i[:, :, :], pidx[:, :, :], 7, op=ALU.logical_shift_right)
            link(v.tensor_single_scalar(plo_i[:, :, :], pidx[:, :, :], P - 1, op=ALU.bitwise_and))
            v.tensor_copy(phi[:, :, :], phi_i[:, :, :])
            link(v.tensor_copy(plo[:, :, :], plo_i[:, :, :]))
            def flat(t):
                return t.rearrange("p c j -> p (c j)").unsqueeze(2)

            def count(t, n):
                return t.unsqueeze(1).broadcast_to([P, 2 * NTILE, n])

            v.tensor_tensor(ohp[:, :, :], flat(plo[:, :, :]).broadcast_to([P, 2 * NTILE, P]), count(iop[:, :], P), ALU.is_equal)
            link(v.tensor_tensor(ohb[:, :, :], flat(phi[:, :, :]).broadcast_to([P, 2 * NTILE, NBT]), count(iob[:, :], NBT), ALU.is_equal))
            for c in range(2):
                i = v.tensor_tensor(ohbt[:, c * NTILE:(c + 1) * NTILE, :], ohb[:, c * NTILE:(c + 1) * NTILE, :], trow[:, :].unsqueeze(2).broadcast_to([P, NTILE, NBT]), ALU.mult)
            i.then_inc(ohpb_ok, 1)
            dve.wait_ge(r_exp, 1)
            link(v.reduce_sum(s8[4][:, :], tg[:, :, :], axis=AX.X))
            dve.wait_ge(r_exp, 2)
            link(v.tensor_scalar(s8[5][:, :], s8[3][:, :], 1.0, None, ALU.add))
            link(v.tensor_tensor(s8[4][:, :], s8[4][:, :], s8[5][:, :], ALU.mult))
            link(v.reciprocal(wt[:, 0, :], s8[4][:, :]))
            dve.wait_ge(slot_ps, 1)
            link(v.tensor_scalar(stok[:, :], pb[:, 6, 0:NBT], float(T), None, ALU.add))
            for b in range(2):
                v.tensor_scalar(icol[b][:, :], stok[:, b:b + 1], 0.0, None, ALU.add).then_inc(ic_ok, 1)
            link(v.tensor_tensor(wt[:, 1, :], wt[:, 0, :], s8[3][:, :], ALU.mult))
            v.tensor_tensor(ohb[:, :, :], ohb[:, :, :], flat(wt[:, :, :]).broadcast_to([P, 2 * NTILE, NBT]), ALU.mult).then_inc(wt_ok, 1)
            block_experts(SLOTS, NBT).then_inc(bexp_ok, 1)
            dve.wait_ge(swt_ps, 1)
            v.tensor_copy(swt[:, :], pb[:, 7, 0:NBT]).then_inc(stok_ok, 1)

            ntrip = dve.value_load(ntrip_i[0:1, 0:1], min_val=2, max_val=MAXB // SLOTS)

            def gathered_T(b, count, col):
                dve.wait_ge(hgt_ps, count)
                v.tensor_copy(hgT[b][:, :, :], banks(0, 2).rearrange("p (k t) -> p k t", k=KD)).then_inc(hgt_ok, 1)
                v.tensor_scalar(icol[b][:, :], stok[:, bass.ds(col, 1)], 0.0, None, ALU.add).then_inc(ic_ok, 1)

            for k in range(2):
                gathered_T(k, k + 1, k + 2)
            with dve.Fori(0, ntrip) as i:
                for q in range(SLOTS):
                    b, nth = q % 2, i * SLOTS + (q + 1)
                    dve.wait_ge(sil_ok, nth)
                    v.tensor_tensor(mid[:, :], sil[:, :], pb[:, GU_BANK[b], FF:2 * FF], ALU.mult).then_inc(mid_ok, 1)
                    dve.wait_ge(mt_ps, nth)
                    v.tensor_copy(midT[:, :, :], pb[:, 3, 0:FF].rearrange("p (f t) -> p f t", f=2)).then_inc(mt_ok, 1)
                    gathered_T(b, i * SLOTS + (q + 3), i * SLOTS + (q + SLOTS))
                    dve.wait_ge(y_out[b], i * (8 * SLOTS) + 16 * (q // 2 + 1))
                    v.tensor_scalar(rcol[b][:, :], stok[:, bass.ds(i * SLOTS + q, 1)], 0.0, None, ALU.add)
                    v.tensor_scalar(wcol[b][:, :], swt[:, bass.ds(i * SLOTS + q, 1)], 1.0, None, ALU.mult).then_inc(wc_ok, 1)
                    dve.wait_ge(wc_ok, nth)
                    dve.wait_ge(y_ps, nth)
                    v.tensor_scalar(yb[b][:, 512:1024], pb[:, 5, :], wcol[b][:, :], None, ALU.mult).then_inc(y_d_ok, 1)

        @block.tensor
        def _(pe):
            t_ = nc.tensor

            def three(out, w, m, start, stop):
                t_.matmul(out, w(0), m(0), start=start, stop=False)
                t_.matmul(out, w(0), m(1), start=False, stop=False)
                return t_.matmul(out, w(1), m(0), start=False, stop=stop)

            pe.wait_ge(ident_ok, 1)
            pe.wait_ge(consts, 1)
            pe.wait_ge(small_in, 16 * 13)
            pe.wait_ge(vec_c, 1)
            t_.transpose(pb[:, 6, 0:NV], vecs[0:NV, :], ident[0:NV, 0:NV])
            t_.transpose(pb[:, 6, 64:64 + TAPS * NC], dwr[:, :], ident[0:TAPS * NC, 0:TAPS * NC])
            t_.transpose(pb[:, 6, 256:256 + NTILE], posf[:, :], ident[0:NTILE, 0:NTILE]).then_inc(vec_t, 1)
            def scaled_T(j):
                pe.wait_ge(s_xn, j + 1)
                pe.wait_ge(x_in[j], 16)
                if j >= 2:
                    pe.wait_ge(s_hp, j - 1)
                for k in range(KD):
                    i = t_.matmul(banks(2 * (j % 2), 2)[:, k * P:(k + 1) * P], xs[:, j, k * P:(k + 1) * P], diag[:, j % 2, :], start=True, stop=True)
                i.then_inc(s_xt, 1)

            scaled_T(0)
            scaled_T(1)
            for j in range(NTILE):
                if j + 2 < NTILE:
                    scaled_T(j + 2)
                if j == 0:
                    pe.wait_ge(dn_lo, 1)
                pe.wait_ge(s_lo, j + 1)
                if j >= 2:
                    pe.wait_ge(dn_ev, j - 1)
                for k in range(KD):
                    i = three(pb[:, 6 + j % 2, 0:DOWN], lambda s: hT[s][:, k, j * P:(j + 1) * P], lambda s: wdn[s][:, k, :], k == 0, k == KD - 1)
                i.then_inc(dn_ps, 1)
            for u in range(IN_UNITS):
                    b = u % 2
                    pe.wait_ge(u_lo, u + 1)
                    if u >= 2:
                        pe.wait_ge(u_ev, u - 1)
                    for f in range(2):
                        for k in range(KD):
                            i = three(pb[:, 2 * b + 2 + f, :], lambda s: ws[s][:, b, k, :], lambda s: hT[s][:, k, f * 512:(f + 1) * 512], k == 0, k == KD - 1)
                    i.then_inc(u_mm, 1)
                    if u == LN_UNIT:
                        pe.wait_ge(conv_done, NC)
                        for f in range(2):
                            for c in range(NC):
                                i = t_.matmul(pb[:, f, :], mean_w[:, :], cv[:, c, f * 512:(f + 1) * 512], start=(c == 0), stop=(c == NC - 1))
                        i.then_inc(ln_mu, 1)
                    if u == LN_UNIT + 1:
                        for c in range(NC):
                            pe.wait_ge(ln_sq, c + 1)
                            for f in range(2):
                                i = t_.matmul(pb[:, 6 + f, :], mean_w[:, :], lnt[c][:, f * 512:(f + 1) * 512], start=(c == 0), stop=(c == NC - 1))
                        i.then_inc(ln_var, 1)

            def misc(kind, t):
                s = at_stage[kind, t]
                M = pb[:, 7, :]
                if s:
                    pe.wait_ge(m_free, s)
                if kind == "qdT":
                    pe.wait_ge(qd_ok, 1)
                    for c in range(3):
                        i = t_.transpose(M[:, c * P:(c + 1) * P], qd[:, t, c * P:(c + 1) * P], ident[:, :])
                if kind in ("q0", "q1"):
                    pe.wait_ge(uq_in, 32)
                    c0 = 4 * QK * (kind == "q1")
                    for k in range(2):
                        i = t_.matmul(M[:, 0:4 * QK], qdT[:, k, :], wuq[:, k, c0:c0 + 4 * QK], start=(k == 0), stop=(k == 1))
                if kind in ("kv0", "kv1"):
                    c0 = 512 * (kind == "kv1")
                    i = t_.matmul(M, qdT[:, 2, :], wukv[:, c0:c0 + 512], start=True, stop=True)
                if kind in ("qT0", "qT1", "kT0", "kT1"):
                    src = qn if kind[0] == "q" else kn
                    pe.wait_ge(qk_ok, 2 * t + (1 if kind[0] == "q" else 2))
                    h0 = 4 * (kind[2] == "1")
                    for h in range(4):
                        i = t_.transpose(M[0:QK, h * P:(h + 1) * P], src[:, h0 + h, :], ident[:, :])
                if kind == "oT":
                    pe.wait_ge(on_ok, t + 1)
                    for c in range(4):
                        i = t_.transpose(M[:, c * P:(c + 1) * P], On[:, c * P:(c + 1) * P], ident[:, :])
                i.then_inc(m_full, 1)

            def scores(n):
                j, h = divmod(n, HEADS)
                w = (j + 1) * P
                if h == 0:
                    pe.wait_ge(m_free, at_stage["kT1", j] + 1)
                if n >= 2:
                    pe.wait_ge(ex_ok, n - 1)
                S = banks(2 * (n % 2), 2)
                for f in range(0, w, 512):
                    e = min(w, f + 512)
                    t_.matmul(S[:, f:e], qT[0:QK, j % 2, h * P:(h + 1) * P], kT[0:QK, h, f:e], start=True, stop=(e < w))
                t_.matmul(S[:, w - P:w], mrow[0:1, 0, :], mrow[0:1, 1, :], start=False, stop=True).then_inc(sc_ok, 1)

            def probs_T(n):
                j, h = divmod(n, HEADS)
                pe.wait_ge(ex_ok, n + 1)
                if n >= 1:
                    pe.wait_ge(pt_d, n)
                    if (n - 1) // HEADS >= 4:
                        pe.wait_ge(pt_a, n - 4 * HEADS)
                for k in range(j + 1):
                    i = t_.transpose(banks(4, 2)[:, k * P:(k + 1) * P], pr[:, n % 2, k * P:(k + 1) * P], ident[:, :])
                i.then_inc(pt_ok, 1)

            def pv(n):
                j, h = divmod(n, HEADS)
                pe.wait_ge(pt_d, n + 1)
                if j >= 4:
                    pe.wait_ge(pt_a, n + 1 - 4 * HEADS)
                if h == 0 and j:
                    pe.wait_ge(on_ok, j)
                for k in range(j + 1):
                    i = t_.matmul(pb[:, 6, h * VD:(h + 1) * VD], pT[:, n % 2, k * P:(k + 1) * P], vv[:, k, h * VD:(h + 1) * VD], start=(k == 0), stop=(k == j))
                i.then_inc(pv_ok, 1)

            pe.wait_ge(ln_y, 1)
            pe.wait_ge(u_ev, IN_UNITS)
            for k in PREP:
                misc(k, 0)
            scores(0)
            scores(1)
            for n in range(NTILE * HEADS):
                j, h = divmod(n, HEADS)
                probs_T(n)
                for k, t in slots(j, h, 0):
                    misc(k, t)
                if n + 2 < NTILE * HEADS:
                    scores(n + 2)
                for k, t in slots(j, h, 1):
                    misc(k, t)
                pv(n)
            misc("oT", NTILE - 1)

            pe.wait_ge(m_free, len(order))
            for c in range(OUT_UNITS):
                u = IN_UNITS + c
                pe.wait_ge(u_lo, u + 1)
                if c >= 2:
                    pe.wait_ge(yab_used, c - 1)
                for br_ in (1, 0):
                    if c == 0:
                        pe.wait_ge(sp_lo, 4 - 2 * br_)
                    for f in range(2):
                        for k in range(4):
                            i = three(pb[:, 4 * (c % 2) + 2 * br_ + f, :], lambda s: ws[s][:, u % 2, 4 * br_ + k, :],
                                      lambda s: aT[s][:, 4 * br_ + k, f * 512:(f + 1) * 512], k == 0, k == 3)
                i.then_inc(u_mm, 1)
            pe.wait_ge(wo_lo_ok, 6)
            pe.wait_ge(mg_lo_ok, OUT_UNITS)
            wout_pair = (lambda k: wout_hi[k][:, :], lambda k: wout_lo[:, k, :])

            def h2_T(j):
                pe.wait_ge(h2_ok, j + 1)
                if j >= 1:
                    pe.wait_ge(h2t_ok, j)
                for k in range(KD):
                    i = t_.transpose(banks(4, 2)[:, k * P:(k + 1) * P], h2[:, j % 2, k * P:(k + 1) * P], ident[:, :])
                i.then_inc(h2t_ps, 1)

            def logits(j):
                pe.wait_ge(h2t_ok, j + 1)
                if j >= 1:
                    pe.wait_ge(lg_ok, j)
                for k in range(KD):
                    t_.matmul(pb[:, 6, 0:NG + NE], h2T[:, j % 2, k, :], wr[:, k, :], start=(k == 0), stop=False)
                t_.matmul(pb[:, 6, 0:NG + NE], one_row[0:1, :], br[0:1, :], start=False, stop=True).then_inc(lg_ps, 1)

            for j in range(NTILE):
                if j >= 2:
                    pe.wait_ge(x1_ok, j - 1)
                for f in range(2):
                    for n, k in enumerate(WOUT_ORDER):
                        if j == 0 and f == 0 and k in (2, 3):
                            pe.wait_ge(wo_lo_ok, 5 + k)
                        i = three(pb[:, 2 * (j % 2) + f, :], lambda s: mg[s][:, k, j * P:(j + 1) * P], lambda s: wout_pair[s](k)[:, f * 512:(f + 1) * 512], n == 0, n == KD - 1)
                if j == 0:
                    pe.wait_ge(gff_in, 16 * 5)
                i.then_inc(x1_ps, 1)
                if j >= 1:
                    h2_T(j - 1)
                if j >= 2:
                    logits(j - 2)
            logits(NTILE - 2)
            h2_T(NTILE - 1)
            logits(NTILE - 1)
            pe.wait_ge(a_ok, 1)
            A = ab[:, :, :].rearrange("p j e -> p (j e)")
            t_.matmul(pb[:, 0, 0:NE * NTILE], before[:, :], A, start=True, stop=True)
            t_.matmul(pb[:, 0, NE * NTILE:2 * NE * NTILE], ones_b[:, :], A, start=True, stop=True).then_inc(rc_ps, 1)

            pe.wait_ge(ohpb_ok, 1)
            for m in range(2 * NTILE):
                i = t_.matmul(pb[:, 6, 0:NBT], ohp[:, m, :], ohbt[:, m, :], start=(m == 0), stop=(m == 2 * NTILE - 1))
            i.then_inc(slot_ps, 1)
            pe.wait_ge(wt_ok, 1)
            for m in range(2 * NTILE):
                i = t_.matmul(pb[:, 7, 0:NBT], ohp[:, m, :].bitcast(F32), ohb[:, m, :], start=(m == 0), stop=(m == 2 * NTILE - 1))
            i.then_inc(swt_ps, 1)

            pe.wait_ge(route_ok, 1)
            pe.sem_inc(y_a, 1)
            pe.sem_inc(y_d_ok, 1)
            last = pe.value_load(ntrip_i[0:1, 1:2], min_val=1, max_val=MAXB // SLOTS - 1)

            def gather_T(b, gathers):
                pe.wait_ge(hg_in[b], gathers)
                for k in range(KD):
                    i = t_.transpose(banks(0, 2)[:, k * P:(k + 1) * P], hg[b][:, k * P:(k + 1) * P], ident[:, :])
                i.then_inc(hgt_ps, 1)

            def gate_up(q, i, hgts):
                pe.wait_ge(w_in0[q], i * 32 + 32)
                pe.wait_ge(hgt_ok, hgts)
                for k in range(KD):
                    m = t_.matmul(pb[:, GU_BANK[q % 2], :], hgT[q % 2][:, k, :], wgu[q][:, k, :], start=(k == 0), stop=(k == KD - 1))
                m.then_inc(gu_ps, 1)

            def finish(q, i):
                nth = i * SLOTS + (q + 1)
                pe.wait_ge(mid_ok, nth)
                for f in range(2):
                    m = t_.transpose(pb[:, 3, f * P:(f + 1) * P], mid[:, f * P:(f + 1) * P], ident[:, :])
                m.then_inc(mt_ps, 1)
                gather_T(q % 2, i * (8 * SLOTS) + 16 * (q // 2 + 2))
                pe.wait_ge(mt_ok, nth)
                pe.wait_ge(w_in1[q], i * 16 + 16)
                pe.wait_ge(y_a, nth)
                pe.wait_ge(y_d_ok, nth)
                for h in range(2):
                    for f in range(2):
                        m = t_.matmul(pb[:, 4 + h, :], midT[:, f, :], wed[q][:, f, h * 512:(h + 1) * 512], start=(f == 0), stop=(f == 1))
                m.then_inc(y_ps, 1)

            for k in range(2):
                if k:
                    pe.wait_ge(hgt_ok, k)
                gather_T(k, 16)
            gate_up(0, 0, 1)
            with pe.Fori(0, last) as i:
                for q in range(SLOTS):
                    gate_up((q + 1) % SLOTS, i + (q + 1) // SLOTS, i * SLOTS + (q + 2))
                    finish(q, i)
            for q in range(SLOTS):
                if q + 1 < SLOTS:
                    gate_up(q + 1, last, last * SLOTS + (q + 2))
                finish(q, last)


_INS = ["x", "positions", "g_mix", "w_in", "g_q_lora", "w_uq", "g_kv_lora", "w_ukv", "g_qk_q", "g_qk_k",
        "w_o_mla", "w_dw", "b_dw", "g_conv_ln", "b_conv_ln", "w_conv_out", "b_gates", "w_out", "g_ffn",
        "w_group_router", "b_group_router", "w_expert_router", "b_expert_router",
        "w_e_gate", "w_e_up", "w_e_down"]
_OUTS = [((1, T, D), "float32")]


def kernel(**inputs):
    import numpy as np
    import concourse.bacc as bacc
    from concourse.bass_utils import run_bass_kernel_spmd

    nc = bacc.Bacc("TRN2", target_bir_lowering=False, num_devices=1, dynamic_dma_scratch_size=4096)
    arrays, args = {}, []
    for name in _INS:
        a = np.ascontiguousarray(inputs[name])
        arrays[f"in_{name}"] = a
        args.append(nc.dram_tensor(f"in_{name}", a.shape, mybir.dt.from_np(a.dtype), kind="ExternalInput").ap())
    for i, (shape, dtype) in enumerate(_OUTS):
        args.append(nc.dram_tensor(f"out_{i}", shape, mybir.dt.from_np(np.dtype(dtype)), kind="ExternalOutput").ap())
    build(nc, *args)
    r = run_bass_kernel_spmd(nc, [arrays], core_ids=[0])
    return r.results[0]["out_0"]
```

```python
import concourse.bass as bass
from concourse import mybir
from contextlib import ExitStack

F32 = mybir.dt.float32
F32R = mybir.dt.float32r
BF16 = mybir.dt.bfloat16
I32 = mybir.dt.int32
U32 = mybir.dt.uint32
ALU = mybir.AluOpType
ACT = mybir.ActivationFunctionType
AX = mybir.AxisListType

P = 128
D = 1024
T = 1024
NTILE = T // P
KD = D // P
HEADS, NOPE, ROPE, VD = 8, 64, 32, 64
QK = NOPE + ROPE
HALF = ROPE // 2
QL, KVL = 256, 128
DOWN = QL + KVL + ROPE
CW = 512
NC = CW // P
TAPS = 31
PAD = TAPS - 1
NG, EPG, FF = 4, 8, 256
NE = NG * EPG
EPS = 1e-6
CHUNK = 64
MASKED = -1e30
THETA = 10000.0
MAXB = 2 * T // P + NE
SLOTS = 4
NBT = MAXB + SLOTS
GLU_UNITS = 2 * NC
GATE_UNITS = 2 * D // P
IN_UNITS = GLU_UNITS + GATE_UNITS
OUT_UNITS = D // P
TAPS_PER_UNIT = 7
LO_SPLIT = 5
LN_UNIT = 20


def build(nc, x, positions, g_mix, w_in, g_q_lora, w_uq, g_kv_lora, w_ukv, g_qk_q, g_qk_k,
          w_o_mla, w_dw, b_dw, g_conv_ln, b_conv_ln, w_conv_out, b_gates, w_out, g_ffn,
          w_group_router, b_group_router, w_expert_router, b_expert_router,
          w_e_gate, w_e_up, w_e_down, out):
    K = 1024
    base = (nc.sbuf_base + 127) // 128 * 128
    at = {"top": base}

    def place(name, shape, dt, offset):
        return nc.alloc_sbuf_tensor_at(name, shape, dt, offset=offset)

    def room(nbytes):
        o = at["top"]
        at["top"] += (nbytes + 31) // 32 * 32
        assert at["top"] <= nc.sbuf_usable_end, at["top"]
        return o

    def small(name, shape, dt=F32):
        n = 2 if dt == BF16 else 4
        for s in shape[1:]:
            n *= s
        return place(name, shape, dt, room(n))

    R1 = room(64 * K)
    R2 = room(64 * K)
    R3 = room(32 * K)
    R6 = room(24 * K)
    hT = [place("hT_hi", [P, KD, T], F32R, R1), place("hT_lo", [P, KD, T], F32R, R1 + 32 * K)]
    xs = place("xs", [P, NTILE, D], F32, R2)
    diag = place("diag", [P, 2, P], F32, R2 + 32 * K)
    hp = place("hp", [P, 2, KD, P], F32, R2 + 40 * K)
    sqj = place("sqj", [P, D], F32, R2 + 48 * K)
    sq3 = place("sq3", [P, DOWN], F32, R2 + 52 * K)
    wdn_raw = place("wdn_raw", [P, KD, DOWN], F32, R6)
    wdn = [place("wdn_hi", [P, KD, DOWN], F32R, R3), place("wdn_lo", [P, KD, DOWN], F32R, R3 + 14 * K)]
    ws_raw = place("ws_raw", [P, 2, KD, P], F32, R6)
    ws = [place("ws_hi", [P, 2, KD, P], F32R, R6 + 8 * K), place("ws_lo", [P, 2, KD, P], F32R, R6 + 16 * K)]
    gates = place("gates", [P, 2 * KD, T], F32, R2)
    cv = place("cv", [P, NC, T], F32, R3)
    UW = T + PAD
    up = [place(f"up{c}", [P, UW], F32, o) for c, o in enumerate((R3 + 16 * K, R3 + 20 * K + 256, R2 + 48 * K, R2 + 56 * K))]
    sg = place("sg", [P, T], F32, R3 + 25 * K)
    QTO = room(8 * K)
    qT = place("qT", [P, 2, HEADS * P], F32, QTO)
    attnT = place("attnT", [P, 4, T], F32, R3 + 16 * K)
    kT = place("kT", [P, HEADS, T], F32, R1)
    vv = place("vv", [P, NTILE, HEADS * VD], F32, R1 + 32 * K)
    pr = place("pr", [P, 2, T], F32, R1 + 48 * K)
    pT = place("pT", [P, 2, T], F32, R1 + 56 * K)
    wuq = place("wuq", [P, 2, HEADS * QK], F32, R6)
    wukv = place("wukv", [P, HEADS * (NOPE + VD)], F32, R6 + 8 * K)
    qn = place("qn", [P, HEADS, QK], F32, R6 + 16 * K)
    kn = place("kn", [P, HEADS, QK], F32, R6 + 12 * K)
    sq2 = place("sq2", [P, HEADS, QK], F32, R6 + 20 * K)
    kn_first = place("kn_first", [P, HEADS, QK], F32, R3 + 16 * K)
    vv_first = place("vv_first", [P, HEADS * VD], F32, R3 + 20 * K)
    sq2_first = place("sq2_first", [P, HEADS, QK], F32, QTO + 4 * K)
    tmpr = place("tmpr", [P, HEADS, ROPE], F32, R6 + 19 * K)
    qdT = place("qdT", [P, 3, P], F32, R6 + 6 * K)
    lnt = [place(f"lnt{c}", [P, T], F32, o) for c, o in enumerate((QTO, QTO + 4 * K, R3 + 16 * K, R3 + 20 * K))]
    lnr = place("lnr", [P, T], F32, R3 + 25 * K)
    aT = [place("aT_hi", [P, 8, T], F32R, R1), place("aT_lo", [P, 8, T], F32R, R1 + 32 * K)]
    wout = place("wout", [P, KD, D], F32, R3)
    wout_lo = place("wout_lo", [P, KD, D], F32R, R3)
    mg = [place("mg_hi", [P, KD, T], F32R, R2 + 32 * K), place("mg_lo", [P, KD, T], F32R, R2)]
    x1 = place("x1", [P, NTILE, D], F32, R1)
    xb = place("xb", [P, 2, D], F32, R1 + 32 * K)
    h2 = place("h2", [P, 2, D], F32, R1 + 40 * K)
    h2T = place("h2T", [P, 2, KD, P], F32, R1 + 48 * K)
    sq7 = place("sq7", [P, D], F32, R1 + 56 * K)
    gffb = place("gffb", [P, D], F32, R1 + 60 * K)
    WO = (R2, R2 + 24 * K, R1 + 32 * K, R6)
    wgu = [place(f"wgu{i}", [P, KD, 2 * FF], F32, o) for i, o in enumerate(WO)]
    wed = [place(f"wed{i}", [P, 2, D], F32, o + 16 * K) for i, o in enumerate(WO)]
    hg = [place(f"hg{i}", [P, D], F32, R2 + 48 * K + 4 * K * i) for i in range(2)]
    hgT = [place(f"hgT{i}", [P, KD, P], F32, R2 + 56 * K + 4 * K * i) for i in range(2)]
    yb = [place(f"yb{i}", [P, D], F32, R3 + 4 * K * i) for i in range(2)]
    sil = place("sil", [P, FF], F32, R3 + 8 * K)
    mid = place("mid", [P, FF], F32, R3 + 9 * K)
    midT = place("midT", [P, 2, P], F32, R3 + 10 * K)

    On = small("On", [P, HEADS * VD])
    QDO = room(NTILE * DOWN * 4)
    qd = place("qd", [P, NTILE, DOWN], F32, QDO)
    wout_hi = [place(f"wout_hi{k}", [P, D], F32R, o) for k, o in enumerate(
        (R6 + 8 * K, R6 + 16 * K, R6 + 12 * K, R6 + 20 * K, QTO, QTO + 4 * K, QDO, QDO + 4 * K))]
    ident = small("ident", [P, P])
    mean_w = small("mean_w", [P, P])
    mrow = small("mrow", [1, 2, P], BF16)
    before = small("before", [P, P], BF16)
    ones_b = small("ones_b", [P, P], BF16)
    one_row = small("one_row", [1, P])
    vecs = place("vecs", [48, P], F32, R6 + 14 * K)
    V_GM, V_BG, V_BD, V_GL, V_BL, V_GQ, V_GK, V_NQ, V_NK = 0, 8, 24, 28, 32, 36, 38, 39, 40
    NV = 41
    vcol = small("vcol", [P, 48])
    dwr = place("dwr", [TAPS * NC, P], F32, R6 + 14 * K + 512)
    dwc = small("dwc", [P, TAPS * NC])
    posi = place("posi", [NTILE, P], I32, R6 + 15 * K)
    posf = place("posf", [NTILE, P], F32, R6 + 15 * K + 512)
    posc = small("posc", [P, NTILE])
    gqk = small("gqk", [P, 2, QK])
    invf = small("invf", [P, HALF])
    ang = place("ang", [P, NTILE, HALF], F32, R2 + 36 * K)
    turns = place("turns", [P, NTILE, HALF], F32, R2 + 36 * K + 512)
    sincos = small("sincos", [P, 2, NTILE, HALF])
    krr = small("krr", [P, NTILE, ROPE])
    krt = place("krt", [P, NTILE, ROPE], F32, R3 + 29 * K)
    rtab = small("rtab", [P, 2, NTILE, ROPE])
    ss1 = small("ss1", [P, NTILE])
    rs1 = small("rs1", [P, NTILE])
    ss3 = small("ss3", [P, 3, NTILE])
    ssh = small("ssh", [P, 2, HEADS])
    nmax = small("nmax", [P, 2])
    rsum = small("rsum", [P, 2, HEADS])
    rinv = small("rinv", [P, HEADS])
    wr = place("wr", [P, KD, NG + NE], F32, R6)
    br = place("br", [1, NG + NE], F32, R6 + 2 * K)
    lg = place("lg", [P, NTILE, NG], F32, R6 + 3 * K)
    le = place("le", [P, NTILE, NE], F32, R6 + 4 * K)
    pen = place("pen", [P, NG], F32, R6 + 3 * K + 128)
    tg = place("tg", [P, NTILE, NG], F32, R6 + 3 * K + 256)
    te = place("te", [P, NE], F32, R6 + 3 * K + 384)
    ab = small("ab", [P, NTILE + 1, NE], BF16)
    oh = [place(f"oh{i}", [P, NTILE, NE], F32, R6 + o * K) for i, o in enumerate((5, 7))]
    first = small("first_of", [P, NTILE])
    logit = [small(f"logit{c}", [P, NTILE]) for c in range(2)]
    second = small("second", [P, NTILE])
    denom, onep = small("denom", [P, NTILE]), small("onep", [P, NTILE])
    wt = small("wt", [P, 2, NTILE])
    nb = small("nb", [P, NE])
    incl = small("incl", [P, NE])
    b128 = small("b128", [P, NE])
    rank = place("rank", [P, NTILE, NE], F32, R3 + 15 * K)
    cmp8 = place("cmp8", [P, NE, 8], F32, R3 + 16 * K)
    pos2 = small("pos2", [P, 2, NTILE])
    pidx = small("pidx", [P, 2, NTILE], I32)
    phi_i = small("phi_i", [P, 2, NTILE], I32)
    plo_i = small("plo_i", [P, 2, NTILE], I32)
    phi = small("phi", [P, 2, NTILE])
    plo = small("plo", [P, 2, NTILE])
    trow = small("trow", [P, NTILE])
    iop = place("iop", [P, P], F32, R6 + 6 * K)
    iob = place("iob", [P, NBT], F32, R6 + 6 * K + 512)
    ohp = place("ohp", [P, 2 * NTILE, P], F32R, R6 + 8 * K)
    ohb = place("ohb", [P, 2 * NTILE, NBT], F32, R6 + 16 * K)
    ohbt = place("ohbt", [P, 2 * NTILE, NBT], F32R, R6 + 20 * K)
    down4 = small("down4", [P, NG])
    down32 = small("down32", [P, NE])
    io8 = small("io8", [P, 8])
    io4 = small("io4", [1, MAXB // SLOTS])
    cmpb = place("cmpb", [1, NBT, NE], F32, R3 + 20 * K)
    cmp4 = small("cmp4", [1, MAXB // SLOTS])
    bexp_f = small("bexp_f", [1, NBT])
    bexp = small("bexp", [1, NBT], I32)
    ntrip_f = small("ntrip_f", [1, 1])
    ntrip_i = small("ntrip_i", [1, 2], I32)
    one32 = small("one32", [P, NE])
    stok = small("stok", [P, NBT], I32)
    swt = small("swt", [P, NBT])
    wcol = [small(f"wcol{i}", [P, 1]) for i in range(2)]
    icol = [small(f"icol{i}", [P, 1], I32) for i in range(2)]
    rcol = [small(f"rcol{i}", [P, 1], I32) for i in range(2)]
    eps = small("eps", [P, 1])
    mhalf = small("mhalf", [P, 2, HEADS])

    h2_d = nc.dram_tensor("h2_rows", (T, D), F32, kind="Internal").ap()
    first_d = nc.dram_tensor("first", (2, P), F32, kind="Internal").ap()

    pb = nc.alloc_psum_tensor("pb", [P, 8, 512], F32)

    def banks(a, n):
        return pb[:, a:a + n, :].rearrange("p b f -> p (b f)")

    ctx = ExitStack()
    with ctx:
        ctx.enter_context(nc.allow_non_contiguous_dma(reason="small per-channel vectors"))

        def sem(name):
            return ctx.enter_context(nc.semaphore(name))

        x_in = [sem(f"x_in{j}") for j in range(NTILE)]
        small_in = sem("small_in")
        late_in, gff_in = sem("late_in"), sem("gff_in")
        wdn_in, uq_in, ukv_in = sem("wdn_in"), sem("uq_in"), sem("ukv_in")
        ws_in = [sem("ws_in0"), sem("ws_in1")]
        wout_in = sem("wout_in")
        xb_in = [sem("xb_in0"), sem("xb_in1")]
        h2_out = [sem("h2_out0"), sem("h2_out1")]
        consts, ident_ok = sem("consts"), sem("ident_ok")
        vec_t, vec_c = sem("vec_t"), sem("vec_c")
        dch, pch = sem("dve_chain"), sem("pool_chain")
        s_ss, s_rs, s_xn, s_xt, s_hp, s_hi, s_lo = [sem(n) for n in
            ("sumsq", "rstd", "x_scaled", "x_transposed", "h_product", "h_hi", "h_lo")]
        dn_hi, dn_lo, dn_ps, dn_ev = [sem(n) for n in ("wdn_hi_ok", "wdn_lo_ok", "down_ps", "down_sb")]
        u_hi, u_lo, u_mm, u_ev = [sem(n) for n in ("unit_hi", "unit_lo", "unit_mm", "unit_ev")]
        down_rs, head_ss, head_rs = sem("down_rstd"), sem("head_ss"), sem("head_rstd")
        conv_done = sem("conv_done")
        ss3_ok, qd_ok, sin_in, sin_ok, tab_ok = [sem(n) for n in ("ss3_ok", "qd_ok", "sin_in", "sin_ok", "tab_ok")]
        ln_mu, ln_d, ln_sq, ln_var, ln_sd, ln_y, ln_u = [sem(n) for n in ("ln_mu", "ln_d", "ln_sq", "ln_var", "ln_sd", "ln_y", "ln_u")]
        m_full, m_free = sem("misc_full"), sem("misc_free")
        qk_sq, qk_ok = sem("qk_squares"), sem("qk_normed")
        sc_ok, mx_ok, ex_ok, pt_ok, pt_a, pt_d, pv_ok = [sem(n) for n in
            ("scores", "row_max", "probs", "probs_T_ps", "probs_T_a", "probs_T_d", "pv")]
        on_ok = sem("attn_norm")
        sp_hi, sp_lo = sem("branch_hi"), sem("branch_lo")
        yab_used, mg_ok = sem("branches_used"), sem("merged")
        mg_hi_ok, mg_lo_ok, wo_hi_ok, wo_lo_ok = [sem(n) for n in ("merged_hi", "merged_lo", "wout_hi_ok", "wout_lo_ok")]
        x1_ps, x1_ok, ss7, rs7, h2_ok, h2t_ps, h2t_ok, lg_ps, lg_ok = [sem(n) for n in
            ("x1_ps", "x1_ok", "ss7", "rs7", "h2_ok", "h2T_ps", "h2T_ok", "logits_ps", "logits_ok")]
        r_in, r_exp, a_ok, rc_ps, route_ok = [sem(n) for n in ("r_in", "r_exp", "assign", "rank_ps", "route_ok")]
        ohpb_ok, slot_ps, iota_ok = [sem(n) for n in ("slot_factors", "slot_ps", "iota_ok")]
        w_in0 = [sem(f"wgu_in{i}") for i in range(SLOTS)]
        w_in1 = [sem(f"wed_in{i}") for i in range(SLOTS)]
        ic_ok, hg_zero = sem("index_col"), sem("hg_zero")
        hg_in = [sem("hg_in0"), sem("hg_in1")]
        hgt_ps, hgt_ok, gu_ps, sil_ok, mid_ok, mt_ps, mt_ok, y_ps, y_a, y_d_ok = [sem(n) for n in
            ("hgT_ps", "hgT_ok", "gate_up", "silu", "mid", "midT_ps", "midT_ok", "y_ps", "y_sb_a", "y_sb_d")]
        y_out = [sem("y_out0"), sem("y_out1")]
        y_all = sem("y_all")
        wt_ok = sem("token_weights")
        x1_out, bexp_ok, wc_ok, stok_ok, swt_ps = [sem(n) for n in ("x1_out", "block_experts", "weight_col", "slot_tokens", "slot_weights_ps")]

        x_v = x[0].rearrange("(j p) d -> j p d", p=P)
        out_v = out[0].rearrange("(j p) d -> j p d", p=P)
        win_v = w_in[0].rearrange("(k p) c -> p k c", p=P)
        wo_v = w_o_mla[0].rearrange("(k p) c -> p k c", p=P)
        wco_v = w_conv_out[0].rearrange("(k p) c -> p k c", p=P)

        VALUE_COL, GATE_COL, LOGIT_COL = DOWN, DOWN + CW, DOWN + 2 * CW

        PREP = ["qdT", "q0", "q1", "kv0", "kv1", "qT0", "kT0", "qT1", "kT1"]

        GU_BANK = (2, 6)
        WOUT_ORDER = (4, 5, 6, 0, 1, 2, 7, 3)
        EARLY = ((NTILE - 1) * HEADS + 4, (NTILE - 1) * HEADS + 5)

        def slots(j, h, part):
            got = [("oT", j - 1)] if (h, part) == (2, 1) and j else []
            nxt = {(0, 0): "qdT", (0, 1): "q0", (1, 0): "q1", (1, 1): "kv0", (2, 0): "kv1", (4, 1): "qT0", (5, 1): "kT0", (6, 1): "qT1", (7, 1): "kT1"}
            return got + ([(nxt[h, part], j + 1)] if j + 1 < NTILE and (h, part) in nxt else [])

        order = [(k, 0) for k in PREP]
        for j in range(NTILE):
            for h in range(HEADS):
                order += slots(j, h, 0) + slots(j, h, 1)
        order.append(("oT", NTILE - 1))
        at_stage = {s: i for i, s in enumerate(order)}

        SMALL_VECS = ((V_GM, g_mix, 8), (V_BG, b_gates, 16), (V_BD, b_dw, 4), (V_GL, g_conv_ln, 4),
                      (V_BL, b_conv_ln, 4), (V_GQ, g_q_lora, 2), (V_GK, g_kv_lora, 1))

        block = ctx.enter_context(nc.Block())

        @block.sync
        def _(sp):
            sp.dma_start(xs[:, 0, :], x_v[0]).then_inc(x_in[0], 16)
            sp.dma_start(xs[:, 1, :], x_v[1]).then_inc(x_in[1], 16)
            for row, src, n in SMALL_VECS[4:]:
                sp.dma_start(vecs[row:row + n, :], src[0].rearrange("(a p) -> a p", p=P)).then_inc(small_in, 16)
            sp.dma_start(wdn_raw[:, :, :], win_v[:, :, 0:DOWN]).then_inc(wdn_in, 16)
            for row, src in ((V_NQ, g_qk_q), (V_NK, g_qk_k)):
                for half in range(2):
                    sp.dma_start(vecs[row:row + 1, half * NOPE:(half + 1) * NOPE], src[:, 0:NOPE]).then_inc(small_in, 16)
            sp.dma_start(dwr[:, :], w_dw[0].rearrange("t (c p) -> (t c) p", p=P)).then_inc(small_in, 16)
            sp.dma_start(posi[:, :], positions[0].rearrange("(a p) -> a p", p=P)).then_inc(small_in, 16)
            sp.dma_start(xs[:, 2, :], x_v[2]).then_inc(x_in[2], 16)
            for j in range(3, NTILE):
                sp.dma_start(xs[:, j, :], x_v[j]).then_inc(x_in[j], 16)
            sp.dma_start(gqk[:, 0, :], g_qk_q[0].partition_broadcast(P)).then_inc(late_in, 16)
            sp.dma_start(gqk[:, 1, :], g_qk_k[0].partition_broadcast(P)).then_inc(late_in, 16)
            sp.wait_ge(dn_hi, 1)
            sp.wait_ge(dn_lo, 2)
            def load_unit(b, col):
                sp.dma_start(ws_raw[:, b, :, :], win_v[:, :, bass.ds(col, P)]).then_inc(ws_in[b], 16)

            load_unit(0, GATE_COL)
            load_unit(1, VALUE_COL)
            with sp.Fori(1, NC) as i:
                for b, col in enumerate((GATE_COL, VALUE_COL)):
                    sp.wait_ge(u_hi, i * 2 + (b - 1))
                    sp.wait_ge(u_lo, i * 2 + (b - 1))
                    load_unit(b, i * P + col)
            with sp.Fori(0, GATE_UNITS // 2) as i:
                for b in range(2):
                    sp.wait_ge(u_hi, i * 2 + (GLU_UNITS + b - 1))
                    sp.wait_ge(u_lo, i * 2 + (GLU_UNITS + b - 1))
                    load_unit(b, i * (2 * P) + (LOGIT_COL + b * P))
            sp.wait_ge(u_hi, IN_UNITS)
            sp.wait_ge(u_lo, IN_UNITS)
            sp.dma_start(wuq[:, :, :], w_uq[0].rearrange("(k p) c -> p k c", p=P)).then_inc(uq_in, 16)
            sp.wait_ge(u_mm, IN_UNITS - 1)
            sp.dma_start(wukv[:, :], w_ukv[0]).then_inc(ukv_in, 16)
            sp.wait_ge(m_full, at_stage["kT1", NTILE - 1] + 1)
            for c in range(OUT_UNITS):
                u = IN_UNITS + c
                if c >= 2:
                    sp.wait_ge(u_hi, u - 1)
                    sp.wait_ge(u_lo, u - 1)
                sp.dma_start(ws_raw[:, u % 2, 0:4, :], wo_v[:, :, c * P:(c + 1) * P]).then_inc(ws_in[u % 2], 16)
                sp.dma_start(ws_raw[:, u % 2, 4:8, :], wco_v[:, :, c * P:(c + 1) * P]).then_inc(ws_in[u % 2], 16)
                if c == 1:
                    sp.wait_ge(sp_hi, 4)
                    sp.wait_ge(sp_lo, 4)
                    sp.dma_start(wout[:, :, :], w_out[0].rearrange("(k p) c -> p k c", p=P)).then_inc(wout_in, 16)
            sp.wait_ge(u_mm, IN_UNITS + OUT_UNITS)
            sp.dma_start(wr[:, :, 0:NG], w_group_router[0].rearrange("(k p) c -> p k c", p=P)).then_inc(gff_in, 16)
            sp.dma_start(wr[:, :, NG:NG + NE], w_expert_router[0].rearrange("(k p) c -> p k c", p=P)).then_inc(gff_in, 16)
            sp.dma_start(br[:, 0:NG], b_group_router).then_inc(gff_in, 16)
            sp.dma_start(br[:, NG:NG + NE], b_expert_router).then_inc(gff_in, 16)
            sp.dma_start(gffb[:, :], g_ffn[0].partition_broadcast(P)).then_inc(gff_in, 16)
            for j in range(NTILE + 1):
                if j < NTILE:
                    if j >= 2:
                        sp.wait_ge(x1_ok, j - 1)
                    sp.dma_start(xb[:, j % 2, :], x_v[j]).then_inc(xb_in[j % 2], 16)
                if j >= 1:
                    sp.wait_ge(h2_ok, j)
                    sp.dma_start(h2_d[(j - 1) * P:j * P, :], h2[:, (j - 1) % 2, :]).then_inc(h2_out[(j - 1) % 2], 16)
                    sp.dma_start(out_v[j - 1], x1[:, j - 1, :]).then_inc(x1_out, 16)
            sp.wait_ge(route_ok, 1)
            ntrip = sp.value_load(ntrip_i[0:1, 0:1], min_val=2, max_val=MAXB // SLOTS)

            def load_expert(b, e, used):
                if used is not None:
                    sp.wait_ge(gu_ps, used)
                sp.dma_start(wgu[b][:, :, 0:FF], w_e_gate[0][bass.ds(e, 1), :, :].rearrange("e (k p) f -> p (e k) f", p=P)).then_inc(w_in0[b], 16)
                sp.dma_start(wgu[b][:, :, FF:2 * FF], w_e_up[0][bass.ds(e, 1), :, :].rearrange("e (k p) f -> p (e k) f", p=P)).then_inc(w_in0[b], 16)
                if used is not None:
                    sp.wait_ge(y_ps, used)
                sp.dma_start(wed[b][:, :, :], w_e_down[0][bass.ds(e, 1), :, :].rearrange("e (k p) f -> p (e k) f", p=P)).then_inc(w_in1[b], 16)

            for q in range(SLOTS):
                if q == 2:
                    sp.wait_ge(hg_in[0], 16)
                    for i in range(2):
                        sp.wait_ge(h2_out[i], 16 * NTILE // 2)
                if q == 3:
                    sp.wait_ge(stok_ok, 1)
                load_expert(q, sp.value_load(bexp[0:1, q:q + 1], min_val=0, max_val=NE - 1), None)
            sp.wait_ge(bexp_ok, 1)
            with sp.Fori(0, ntrip - 1) as i:
                for q in range(SLOTS):
                    e = sp.value_load(bexp[0:1, bass.ds(i * SLOTS + (q + SLOTS), 1)], min_val=0, max_val=NE - 1)
                    load_expert(q, e, i * SLOTS + (q + 1))
            sp.wait_ge(y_all, 2)

        @block.gpsimd
        def _(pool):
            g = nc.gpsimd
            n = [0]

            def link(ins):
                n[0] += 1
                ins.then_inc(pch, 1)
                pool.wait_ge(pch, n[0])

            link(g.memset(ident[:, :], 0.0))
            g.affine_select(out=ident[:, :], in_=ident[:, :], compare_op=ALU.not_equal, fill=1.0, base=0,
                            pattern=[[-1, P]], channel_multiplier=1).then_inc(ident_ok, 1)
            g.memset(mean_w[:, :], 1.0 / CW)
            g.memset(eps[:, :], EPS)
            g.memset(mhalf[:, :, :], -0.5)
            for f in range(HALF):
                g.memset(invf[:, f:f + 1], float(THETA ** (-f / HALF)))
            g.memset(ones_b[:, :], 1.0)
            g.memset(one32[:, :], 1.0)
            g.memset(ab[:, NTILE, :], 0.0)
            g.memset(one_row[:, :], 1.0)
            link(g.memset(before[:, :], 0.0))
            g.affine_select(out=before[:, :], in_=before[:, :], compare_op=ALU.is_ge, fill=1.0, base=0,
                            pattern=[[-1, P]], channel_multiplier=1)
            link(g.memset(mrow[:, :, :], 0.0))
            g.memset(mrow[:, 0, 0:CHUNK], 1.0)
            g.memset(mrow[:, 1, CHUNK:P], MASKED)
            g.iota(trow[:, :], pattern=[[P, NTILE]], base=-T, channel_multiplier=1, allow_small_or_imprecise_dtypes=True)
            g.iota(down4[:, :], pattern=[[-1, NG]], base=NG, channel_multiplier=0, allow_small_or_imprecise_dtypes=True)
            g.iota(down32[:, :], pattern=[[-1, NE]], base=NE, channel_multiplier=0, allow_small_or_imprecise_dtypes=True)
            g.iota(io8[:, :], pattern=[[P, 8]], base=0, channel_multiplier=0, allow_small_or_imprecise_dtypes=True)
            g.iota(io4[:, :], pattern=[[SLOTS, MAXB // SLOTS]], base=0, channel_multiplier=0, allow_small_or_imprecise_dtypes=True).then_inc(consts, 1)

            def rstd(dst, src, count, power):
                link(g.tensor_scalar(dst, src, 1.0 / count, EPS, ALU.mult, ALU.add))
                return g.tensor_tensor(dst, dst, power, ALU.pow)

            for j in range(NTILE):
                pool.wait_ge(s_ss, j + 1)
                rstd(rs1[:, j:j + 1], ss1[:, j:j + 1], D, mhalf[:, 0, 0:1]).then_inc(s_rs, 1)
                if j == 2:
                    pool.wait_ge(dn_hi, 1)
                    g.tensor_tensor(wdn[1][:, LO_SPLIT:KD, :], wdn_raw[:, LO_SPLIT:KD, :], wdn[0][:, LO_SPLIT:KD, :].bitcast(F32), ALU.subtract).then_inc(dn_lo, 1)
            pool.wait_ge(ss3_ok, NTILE)
            for c, width in enumerate((QL, KVL)):
                rstd(ss3[:, c, :], ss3[:, c, :], width, mhalf[:, 0, :]).then_inc(down_rs, 1)
            for t in range(NTILE):
                pool.wait_ge(head_ss, 2 * t + 1)
                link(rstd(ssh[:, 0, :], ssh[:, 0, :], QK, mhalf[:, 0, :]))
                link(g.tensor_tensor(qn[:, :, :], qn[:, :, :], ssh[:, 0, :].unsqueeze(2).broadcast_to([P, HEADS, QK]), ALU.mult))
                rot = qn[:, :, NOPE:QK]
                if t == 0:
                    pool.wait_ge(tab_ok, 1)
                g.tensor_tensor(tmpr[:, :, 0:HALF], rot[:, :, HALF:ROPE], rtab[:, 1, t:t + 1, 0:HALF].broadcast_to([P, HEADS, HALF]), ALU.mult)
                link(g.tensor_tensor(tmpr[:, :, HALF:ROPE], rot[:, :, 0:HALF], rtab[:, 1, t:t + 1, HALF:ROPE].broadcast_to([P, HEADS, HALF]), ALU.mult))
                link(g.tensor_tensor(rot, rot, rtab[:, 0, t:t + 1, :].broadcast_to([P, HEADS, ROPE]), ALU.mult))
                g.tensor_tensor(rot, rot, tmpr[:, :, :], ALU.add).then_inc(qk_ok, 1)
                pool.wait_ge(head_ss, 2 * t + 2)
                link(rstd(ssh[:, 1, :], ssh[:, 1, :], QK, mhalf[:, 0, :]))
                k = kn if t else kn_first
                g.tensor_tensor(k[:, :, 0:NOPE], k[:, :, 0:NOPE], ssh[:, 1, :].unsqueeze(2).broadcast_to([P, HEADS, NOPE]), ALU.mult)
                g.tensor_tensor(k[:, :, NOPE:QK], krr[:, t:t + 1, :].broadcast_to([P, HEADS, ROPE]),
                                ssh[:, 1, :].unsqueeze(2).broadcast_to([P, HEADS, ROPE]), ALU.mult).then_inc(qk_ok, 1)
            for j in range(NTILE):
                pool.wait_ge(ss7, j + 1)
                rstd(rs1[:, j:j + 1], ss1[:, j:j + 1], D, mhalf[:, 0, 0:1]).then_inc(rs7, 1)
            g.iota(iop[:, :], pattern=[[1, P]], base=0, channel_multiplier=0, allow_small_or_imprecise_dtypes=True)
            g.iota(iob[:, :], pattern=[[1, NBT]], base=0, channel_multiplier=0, allow_small_or_imprecise_dtypes=True).then_inc(iota_ok, 1)
            pool.wait_ge(a_ok, NTILE)
            for b in range(2):
                g.memset(hg[b][:, :], 0.0).then_inc(hg_zero, 1)
            for b in range(2):
                pool.dma_start(first_d[b:b + 1, :].rearrange("a p -> p a"), ident[:, 0:1]).then_inc(y_out[b], 16)
            for i in range(2):
                pool.wait_ge(h2_out[i], 16 * NTILE // 2)
            pool.wait_ge(route_ok, 1)
            ntrip = pool.value_load(ntrip_i[0:1, 0:1], min_val=2, max_val=MAXB // SLOTS)

            def gather(b, count):
                pool.wait_ge(ic_ok, count)
                pool.sem_inc(pch, 1)
                g.indirect_dma_start(out=hg[b][:, :], out_offset=None, in_=h2_d,
                                     in_offset=bass.IndirectOffsetOnAxis(ap=icol[b][:, 0:1].bitcast(U32), axis=0),
                                     bounds_check=T - 1, oob_is_err=False).then_inc(hg_in[b], 16)

            def scatter(b, count, before):
                pool.wait_ge(y_a, count + 1)
                pool.sem_inc(pch, 1)
                pool.wait_ge(y_d_ok, count + 1)
                pool.sem_inc(pch, 1)
                pool.wait_ge(y_out[1 - b], before)
                pool.sem_inc(pch, 1)
                g.indirect_dma_start(out=out[0], out_offset=bass.IndirectOffsetOnAxis(ap=rcol[b][:, 0:1].bitcast(U32), axis=0),
                                     in_=yb[b][:, :], in_offset=None, compute_op=ALU.add,
                                     bounds_check=T - 1, oob_is_err=False).then_inc(y_out[b], 16)

            pool.wait_ge(hg_zero, 2)
            for k in range(SLOTS):
                gather(k % 2, k + 1)
            pool.wait_ge(x1_out, 16 * NTILE)
            with pool.Fori(0, ntrip) as i:
                for q in range(SLOTS):
                    gather(q % 2, i * SLOTS + (q + SLOTS + 1))
                    scatter(q % 2, i * SLOTS + (q + 1), i * (8 * SLOTS) + 16 * ((q + 1) // 2 + 1))
            for b in range(2):
                pool.wait_ge(hg_in[b], ntrip * (8 * SLOTS) + 8 * SLOTS)
                pool.wait_ge(y_out[b], ntrip * (8 * SLOTS) + 16)
                pool.sem_inc(y_all, 1)

        @block.scalar
        def _(act):
            a = nc.scalar

            for row, src, n in SMALL_VECS[:4]:
                act.dma_start(vecs[row:row + n, :], src[0].rearrange("(a p) -> a p", p=P)).then_inc(small_in, 16)

            def sumsq(j):
                act.wait_ge(x_in[j], 16)
                if j:
                    act.wait_ge(s_ss, j)
                a.activation(sqj[:, :], xs[:, j, :], ACT.Square, accum_out=ss1[:, j:j + 1]).then_inc(s_ss, 1)

            def down_out(j):
                act.wait_ge(dn_ps, j + 1)
                a.activation(qd[:, j, :], pb[:, 6 + j % 2, 0:DOWN], ACT.Copy).then_inc(dn_ev, 1)
                act.wait_ge(dn_ev, j + 1)
                if j:
                    act.wait_ge(ss3_ok, j)
                for s, (lo, hi) in enumerate(((0, QL), (QL, QL + KVL), (QL + KVL, DOWN))):
                    i = a.activation(sq3[:, lo:hi], qd[:, j, lo:hi], ACT.Square, accum_out=ss3[:, s, j:j + 1])
                i.then_inc(ss3_ok, 1)

            sumsq(0)
            sumsq(1)
            sumsq(2)
            for j in range(NTILE):
                act.wait_ge(s_hp, j + 1)
                a.activation(hT[0][:, :, j * P:(j + 1) * P], hp[:, j % 2, :, :], ACT.Copy).then_inc(s_hi, 1)
                if j == 0:
                    act.wait_ge(wdn_in, 16)
                    a.activation(wdn[0][:, :, :], wdn_raw[:, :, :], ACT.Copy).then_inc(dn_hi, 1)
                if j + 3 < NTILE:
                    sumsq(j + 3)
                if j:
                    down_out(j - 1)

            def unit_hi(u):
                act.wait_ge(ws_in[u % 2], 16 * (u // 2 + 1) if u < IN_UNITS else 16 * (IN_UNITS // 2) + 32 * ((u - IN_UNITS) // 2 + 1))
                if u >= 2:
                    act.wait_ge(u_mm, u - 1)
                a.activation(ws[0][:, u % 2, :, :], ws_raw[:, u % 2, :, :], ACT.Copy).then_inc(u_hi, 1)

            def misc(kind, t):
                s = at_stage[kind, t]
                M = pb[:, 7, :]
                if kind in ("q0", "q1"):
                    act.wait_ge(m_full, s + 1)
                    h = 4 * (kind == "q1")
                    a.activation(qn[:, h:h + 4, :], M[:, 0:4 * QK].rearrange("p (h c) -> p h c", h=4), ACT.Copy).then_inc(m_free, 1)
                    if kind == "q1":
                        act.wait_ge(m_free, s + 1)
                        if t:
                            act.wait_ge(head_ss, 2 * t)
                        a.activation((sq2 if t else sq2_first)[:, :, :], qn[:, :, :], ACT.Square).then_inc(qk_sq, 1)
                if kind in ("kv0", "kv1"):
                    act.wait_ge(m_full, s + 1)
                    h = 4 * (kind == "kv1")
                    kv = M.rearrange("p (h c) -> p h c", h=4)
                    k, vt = (kn, vv[:, t, :]) if t else (kn_first, vv_first[:, :])
                    a.activation(k[:, h:h + 4, 0:NOPE], kv[:, :, 0:NOPE], ACT.Copy)
                    a.activation(vt[:, h * VD:(h + 4) * VD].rearrange("p (h c) -> p h c", h=4), kv[:, :, NOPE:], ACT.Copy).then_inc(m_free, 1)
                    if kind == "kv1":
                        act.wait_ge(m_free, s + 1)
                        act.wait_ge(head_ss, 2 * t + 1)
                        a.activation((sq2 if t else sq2_first)[:, :, 0:NOPE], k[:, :, 0:NOPE], ACT.Square).then_inc(qk_sq, 1)
                if kind in ("qT0", "qT1"):
                    act.wait_ge(m_full, s + 1)
                    h = 4 * (kind == "qT1")
                    a.activation(qT[0:QK, t % 2, h * P:(h + 4) * P], M[0:QK, :], ACT.Copy, scale=vcol[0:QK, V_NQ:V_NQ + 1]).then_inc(m_free, 1)
                if kind == "oT":
                    act.wait_ge(m_full, s + 1)
                    a.activation(attnT[:, :, t * P:(t + 1) * P], M.rearrange("p (c t) -> p c t", c=4), ACT.Copy).then_inc(m_free, 1)

            unit_hi(0)
            unit_hi(1)
            down_out(NTILE - 1)
            for u in range(IN_UNITS):
                act.wait_ge(u_mm, u + 1)
                src = banks(2 * (u % 2) + 2, 2)
                if u < GLU_UNITS:
                    if u % 2 == 0:
                        if u >= 2:
                            act.wait_ge(u_ev, u)
                        a.activation(sg[:, :], src, ACT.Sigmoid).then_inc(u_ev, 1)
                else:
                    c = u - GLU_UNITS
                    if c == 0:
                        act.wait_ge(u_ev, GLU_UNITS)
                    if c in (12, 14):
                        act.wait_ge(conv_done, c // 2 - 3)
                    a.activation(gates[:, c, :], src, ACT.Sigmoid, bias=vcol[:, V_BG + c:V_BG + c + 1]).then_inc(u_ev, 1)
                if u + 2 < IN_UNITS:
                    unit_hi(u + 2)
                if u == 1:
                    act.wait_ge(sin_in, 1)
                    a.activation(sincos[:, :, :, :], sincos[:, :, :, :], ACT.Sin).then_inc(sin_ok, 1)
                if u == LN_UNIT:
                    for c in range(NC):
                        act.wait_ge(ln_d, c + 1)
                        a.activation(lnt[c][:, :], cv[:, c, :], ACT.Square).then_inc(ln_sq, 1)
                if u == LN_UNIT + 1:
                    act.wait_ge(ln_var, 1)
                    a.activation(lnr[:, :], banks(6, 2), ACT.Sqrt, bias=eps[:, :]).then_inc(ln_sd, 1)
                if u == LN_UNIT + 2:
                    for c in range(NC):
                        act.wait_ge(ln_y, c + 1)
                        a.activation(cv[:, c, :], cv[:, c, :], ACT.Silu, scale=vcol[:, V_GL + c:V_GL + c + 1],
                                     bias=vcol[:, V_BL + c:V_BL + c + 1]).then_inc(ln_u, 1)
                    for k in PREP[1:5]:
                        misc(k, 0)

            def exps(n):
                j, h = divmod(n, HEADS)
                w = (j + 1) * P
                act.wait_ge(mx_ok, n + 1)
                if n >= 2:
                    act.wait_ge(pt_ok, n - 1)
                a.activation(pr[:, n % 2, 0:w], banks(2 * (n % 2), 2)[:, 0:w], ACT.Exp,
                             bias=nmax[:, n % 2:n % 2 + 1], accum_out=rsum[:, j % 2, h:h + 1]).then_inc(ex_ok, 1)

            act.wait_ge(u_mm, IN_UNITS)
            a.activation(vv[:, 0, :], vv_first[:, :], ACT.Copy)
            for k in PREP[5:]:
                misc(k, 0)
            exps(0)
            exps(1)
            for n in range(NTILE * HEADS):
                j, h = divmod(n, HEADS)
                if j >= 4:
                    act.wait_ge(pt_ok, n + 1)
                    act.wait_ge(pv_ok, n - 1)
                    a.activation(pT[:, n % 2, 512:(j + 1) * P], banks(5, 1)[:, 0:(j + 1) * P - 512], ACT.Copy).then_inc(pt_a, 1)
                for k, t in slots(j, h, 0):
                    misc(k, t)
                if n + 2 < NTILE * HEADS:
                    exps(n + 2)
                for k, t in slots(j, h, 1):
                    misc(k, t)
                if n in EARLY:
                    unit_hi(IN_UNITS + EARLY.index(n))
                if n >= NTILE * HEADS - 2:
                    c = n - (NTILE * HEADS - 2)
                    act.wait_ge(sc_ok, NTILE * HEADS)
                    a.activation(aT[0][:, 4 + 2 * c:6 + 2 * c, :], cv[:, 2 * c:2 * c + 2, :], ACT.Copy).then_inc(sp_hi, 1)
            misc("oT", NTILE - 1)

            act.wait_ge(m_free, len(order))
            for c in range(2):
                a.activation(aT[0][:, 2 * c:2 * c + 2, :], attnT[:, 2 * c:2 * c + 2, :], ACT.Copy).then_inc(sp_hi, 1)

            def wout_half(k):
                if k in (0, 2):
                    act.wait_ge(u_mm, IN_UNITS + OUT_UNITS - 1 + k // 2)
                a.activation(wout_hi[k][:, :], wout[:, k, :], ACT.Copy).then_inc(wo_hi_ok, 1)

            for c in range(OUT_UNITS):
                if c + 2 < OUT_UNITS:
                    unit_hi(IN_UNITS + c + 2)
                if c == 2:
                    act.wait_ge(wout_in, 16)
                if 2 <= c < 6:
                    wout_half(c + 2)
                act.wait_ge(mg_ok, c + 1)
                a.activation(mg[0][:, c, :], gates[:, c, :], ACT.Copy).then_inc(mg_hi_ok, 1)
                if c == 6:
                    wout_half(0)
                    wout_half(1)
            wout_half(2)
            wout_half(3)
            def half_two(j):
                act.wait_ge(h2t_ps, j + 1)
                if j >= 2:
                    act.wait_ge(lg_ps, j - 1)
                a.activation(h2T[:, j % 2, :, :], banks(4, 2).rearrange("p (k t) -> p k t", k=KD), ACT.Copy).then_inc(h2t_ok, 1)

            for j in range(NTILE):
                act.wait_ge(x1_ok, j + 1)
                if j:
                    act.wait_ge(ss7, j)
                a.activation(sq7[:, :], x1[:, j, :], ACT.Square, accum_out=ss1[:, j:j + 1]).then_inc(ss7, 1)
                if j >= 1:
                    half_two(j - 1)
            half_two(NTILE - 1)
            act.wait_ge(r_in, 1)
            a.activation(tg[:, :, :], tg[:, :, :], ACT.Exp).then_inc(r_exp, 1)
            a.activation(second[:, :], second[:, :], ACT.Exp).then_inc(r_exp, 1)

            act.wait_ge(route_ok, 1)
            ntrip = act.value_load(ntrip_i[0:1, 0:1], min_val=2, max_val=MAXB // SLOTS)
            with act.Fori(0, ntrip) as i:
                for q in range(SLOTS):
                    nth = i * SLOTS + (q + 1)
                    act.wait_ge(gu_ps, nth)
                    a.activation(sil[:, :], pb[:, GU_BANK[q % 2], 0:FF], ACT.Silu).then_inc(sil_ok, 1)
                    act.wait_ge(y_ps, nth)
                    act.wait_ge(wc_ok, nth)
                    a.activation(yb[q % 2][:, 0:512], pb[:, 4, :], ACT.Copy, scale=wcol[q % 2][:, :]).then_inc(y_a, 1)

        @block.vector
        def _(dve):
            v = nc.vector
            n = [0]

            def link(ins):
                n[0] += 1
                ins.then_inc(dch, 1)
                dve.wait_ge(dch, n[0])

            def diagonal(j):
                dve.wait_ge(s_rs, j + 1)
                v.tensor_scalar(diag[:, j % 2, :], ident[:, :], rs1[:, j:j + 1], None, ALU.mult).then_inc(s_xn, 1)

            dve.wait_ge(ident_ok, 1)
            diagonal(0)
            diagonal(1)
            dve.wait_ge(consts, 1)
            dve.wait_ge(small_in, 16 * 13)
            link(v.tensor_copy(posf[:, :], posi[:, :]))
            v.tensor_copy(posf[:, :], posf[:, :]).then_inc(vec_c, 1)
            dve.wait_ge(vec_t, 1)
            v.tensor_copy(vcol[:, 0:NV], pb[:, 6, 0:NV])
            v.tensor_copy(dwc[:, :], pb[:, 6, 64:64 + TAPS * NC])
            link(v.tensor_copy(posc[:, :], pb[:, 6, 256:256 + NTILE]))
            v.memset(vcol[NOPE:P, V_NQ:V_NQ + 2], 1.0)
            v.tensor_scalar(vcol[0:NOPE, V_NQ:V_NQ + 1], vcol[0:NOPE, V_NQ:V_NQ + 1], QK ** -0.5, None, ALU.mult)

            def lo_half(j):
                dve.wait_ge(s_hi, j + 1)
                v.tensor_tensor(hT[1][:, :, j * P:(j + 1) * P], hp[:, j % 2, :, :],
                                hT[0][:, :, j * P:(j + 1) * P].bitcast(F32), ALU.subtract).then_inc(s_lo, 1)

            for j in range(NTILE):
                dve.wait_ge(s_xt, j + 1)
                if j >= 2:
                    dve.wait_ge(s_hi, j - 1)
                    dve.wait_ge(s_lo, j - 1)
                v.tensor_tensor(hp[:, j % 2, :, :], banks(2 * (j % 2), 2).rearrange("p (k t) -> p k t", k=KD),
                                vcol[:, V_GM:V_GM + KD].unsqueeze(2).broadcast_to([P, KD, P]), ALU.mult).then_inc(s_hp, 1)
                if j + 2 < NTILE:
                    diagonal(j + 2)
                lo_half(j)
                if j == 0:
                    dve.wait_ge(dn_hi, 1)
                    v.tensor_tensor(wdn[1][:, 0:LO_SPLIT, :], wdn_raw[:, 0:LO_SPLIT, :], wdn[0][:, 0:LO_SPLIT, :].bitcast(F32), ALU.subtract).then_inc(dn_lo, 1)

            def unit_lo(u):
                dve.wait_ge(u_hi, u + 1)
                if u >= 2:
                    dve.wait_ge(u_mm, u - 1)
                v.tensor_tensor(ws[1][:, u % 2, :, :], ws_raw[:, u % 2, :, :], ws[0][:, u % 2, :, :].bitcast(F32), ALU.subtract).then_inc(u_lo, 1)

            def tap(k):
                c, t = divmod(k, TAPS)
                w = dwc[:, t * NC + c:t * NC + c + 1]
                src = up[c][:, t:t + T]
                if t == 0:
                    link(v.tensor_scalar(cv[:, c, :], src, w, vcol[:, V_BD + c:V_BD + c + 1], ALU.mult, ALU.add))
                else:
                    i = v.scalar_tensor_tensor(out=cv[:, c, :], in0=src, scalar=w, in1=cv[:, c, :], op0=ALU.mult, op1=ALU.add)
                    if t < TAPS - 1:
                        link(i)
                    else:
                        i.then_inc(conv_done, 1)

            def rotary_angles():
                dve.wait_ge(late_in, 16 * 2)
                link(v.tensor_scalar(gqk[:, 0, :], gqk[:, 0, :], QK ** -0.5, None, ALU.mult))
                link(v.tensor_tensor(ang[:, :, :], posc[:, :].unsqueeze(2).broadcast_to([P, NTILE, HALF]),
                                     invf[:, :].unsqueeze(1).broadcast_to([P, NTILE, HALF]), ALU.mult))
                TWO_PI = 6.283185307179586
                link(v.tensor_scalar(turns[:, :, :], ang[:, :, :], 1.0 / TWO_PI, 12582912.0, ALU.mult, ALU.add))
                link(v.tensor_scalar(turns[:, :, :], turns[:, :, :], 12582912.0, None, ALU.subtract))
                left = TWO_PI
                for bits in (-5, -14, -23):
                    part = float(int(left / 2.0 ** bits)) * 2.0 ** bits
                    left -= part
                    link(v.scalar_tensor_tensor(out=ang[:, :, :], in0=turns[:, :, :], scalar=-part, in1=ang[:, :, :], op0=ALU.mult, op1=ALU.add))
                link(v.scalar_tensor_tensor(out=ang[:, :, :], in0=turns[:, :, :], scalar=-left, in1=ang[:, :, :], op0=ALU.mult, op1=ALU.add))
                PI = 3.1415925
                link(v.tensor_scalar(turns[:, :, :], ang[:, :, :], TWO_PI / 4, TWO_PI / 2, ALU.add, ALU.is_gt))
                link(v.scalar_tensor_tensor(out=turns[:, :, :], in0=turns[:, :, :], scalar=-TWO_PI, in1=ang[:, :, :], op0=ALU.mult, op1=ALU.add))
                link(v.tensor_scalar(turns[:, :, :], turns[:, :, :], TWO_PI / 4, PI, ALU.add, ALU.min))
                link(v.tensor_scalar(sincos[:, 1, :, :], turns[:, :, :], -PI, None, ALU.max))
                v.tensor_scalar(sincos[:, 0, :, :], ang[:, :, :], PI, -PI, ALU.min, ALU.max).then_inc(sin_in, 1)

            def rotary_tables():
                dve.wait_ge(sin_ok, 1)
                sin, cos = sincos[:, 0, :, :], sincos[:, 1, :, :]

                def gain(w, half):
                    return gqk[:, w, NOPE + half * HALF:NOPE + (half + 1) * HALF].unsqueeze(1).broadcast_to([P, NTILE, HALF])

                v.tensor_tensor(rtab[:, 0, :, 0:HALF], cos, gain(0, 0), ALU.mult)
                v.tensor_tensor(rtab[:, 0, :, HALF:ROPE], cos, gain(0, 1), ALU.mult)
                v.scalar_tensor_tensor(out=rtab[:, 1, :, 0:HALF], in0=sin, scalar=-1.0, in1=gain(0, 1), op0=ALU.mult, op1=ALU.mult)
                v.tensor_tensor(rtab[:, 1, :, HALF:ROPE], sin, gain(0, 0), ALU.mult)
                link(v.tensor_tensor(krr[:, :, :], qd[:, :, QL + KVL:DOWN], gqk[:, 1, NOPE:QK].unsqueeze(1).broadcast_to([P, NTILE, ROPE]), ALU.mult))
                v.tensor_tensor(krt[:, :, 0:HALF], krr[:, :, HALF:ROPE], sin, ALU.mult)
                link(v.tensor_tensor(krt[:, :, HALF:ROPE], krr[:, :, 0:HALF], sin, ALU.mult))
                v.tensor_tensor(krr[:, :, 0:HALF], krr[:, :, 0:HALF], cos, ALU.mult)
                link(v.tensor_tensor(krr[:, :, HALF:ROPE], krr[:, :, HALF:ROPE], cos, ALU.mult))
                v.tensor_tensor(krr[:, :, 0:HALF], krr[:, :, 0:HALF], krt[:, :, 0:HALF], ALU.subtract)
                v.tensor_tensor(krr[:, :, HALF:ROPE], krr[:, :, HALF:ROPE], krt[:, :, HALF:ROPE], ALU.add).then_inc(tab_ok, 1)

            def misc(kind, t):
                s = at_stage[kind, t]
                M = pb[:, 7, :]
                if kind == "qdT":
                    dve.wait_ge(m_full, s + 1)
                    v.tensor_tensor(qdT[:, :, :], M[:, 0:3 * P].rearrange("p (c t) -> p c t", c=3),
                                    vcol[:, V_GQ:V_GQ + 3].unsqueeze(2).broadcast_to([P, 3, P]), ALU.mult).then_inc(m_free, 1)
                if kind == "q1":
                    dve.wait_ge(qk_sq, 2 * t + 1)
                    v.reduce_sum(ssh[:, 0, :], (sq2 if t else sq2_first)[:, :, :], axis=AX.X).then_inc(head_ss, 1)
                if kind == "kv1":
                    dve.wait_ge(qk_sq, 2 * t + 2)
                    link(v.reduce_sum(ssh[:, 1, :], (sq2 if t else sq2_first)[:, :, 0:NOPE], axis=AX.X))
                    v.tensor_scalar(ssh[:, 1, :], ssh[:, 1, :], ss3[:, 2, t:t + 1], None, ALU.add).then_inc(head_ss, 1)
                if kind in ("kT0", "kT1"):
                    dve.wait_ge(m_full, s + 1)
                    h = 4 * (kind == "kT1")
                    v.tensor_scalar(kT[0:QK, h:h + 4, t * P:(t + 1) * P], M[0:QK, :].rearrange("p (h t) -> p h t", h=4),
                                    vcol[0:QK, V_NK:V_NK + 1], None, ALU.mult).then_inc(m_free, 1)

            unit_lo(0)
            unit_lo(1)
            taps_done = 0
            for u in range(IN_UNITS):
                if u == 0:
                    dve.wait_ge(down_rs, 2)
                    v.tensor_tensor(qd[:, :, 0:QL], qd[:, :, 0:QL], ss3[:, 0, :].unsqueeze(2).broadcast_to([P, NTILE, QL]), ALU.mult)
                    v.tensor_tensor(qd[:, :, QL:QL + KVL], qd[:, :, QL:QL + KVL], ss3[:, 1, :].unsqueeze(2).broadcast_to([P, NTILE, KVL]), ALU.mult).then_inc(qd_ok, 1)
                if u < GLU_UNITS and u % 2 == 1:
                    dve.wait_ge(u_mm, u + 1)
                    dve.wait_ge(u_ev, u)
                    v.memset(up[u // 2][:, 0:PAD], 0.0)
                    v.tensor_tensor(up[u // 2][:, PAD:UW], banks(2 * (u % 2) + 2, 2), sg[:, :], ALU.mult).then_inc(u_ev, 1)
                    dve.wait_ge(u_ev, u + 1)
                if u + 2 < IN_UNITS:
                    unit_lo(u + 2)
                target = min(TAPS * NC, TAPS_PER_UNIT * u)
                if u < GLU_UNITS:
                    target = min(target, TAPS * ((u + 1) // 2))
                for k in range(taps_done, target):
                    tap(k)
                taps_done = max(taps_done, target)
                if u == 1:
                    rotary_angles()
                if u == LN_UNIT - 1:
                    rotary_tables()
                if u == IN_UNITS - 2:
                    for k in ("qdT", "q1", "kv1"):
                        misc(k, 0)
                if u == LN_UNIT:
                    dve.wait_ge(ln_mu, 1)
                    for c in range(NC):
                        v.tensor_tensor(cv[:, c, :], cv[:, c, :], banks(0, 2), ALU.subtract).then_inc(ln_d, 1)
                if u == LN_UNIT + 1:
                    dve.wait_ge(ln_sd, 1)
                    link(v.reciprocal(lnr[:, :], lnr[:, :]))
                    for c in range(NC):
                        dve.wait_ge(ln_sq, c + 1)
                        dve.wait_ge(ln_d, c + 1)
                        v.tensor_tensor(cv[:, c, :], cv[:, c, :], lnr[:, :], ALU.mult).then_inc(ln_y, 1)
            def rowmax(n):
                j, h = divmod(n, HEADS)
                dve.wait_ge(sc_ok, n + 1)
                if n >= 2:
                    dve.wait_ge(ex_ok, n - 1)
                v.tensor_reduce(out=nmax[:, n % 2:n % 2 + 1], in_=banks(2 * (n % 2), 2)[:, 0:(j + 1) * P],
                                axis=AX.X, op=ALU.max, negate=True).then_inc(mx_ok, 1)

            def conv_lo(c):
                dve.wait_ge(sp_hi, c + 1)
                v.tensor_tensor(aT[1][:, 4 + 2 * c:6 + 2 * c, :], cv[:, 2 * c:2 * c + 2, :], aT[0][:, 4 + 2 * c:6 + 2 * c, :].bitcast(F32), ALU.subtract).then_inc(sp_lo, 1)

            for k in PREP[5:]:
                misc(k, 0)
            rowmax(0)
            rowmax(1)
            for m in range(NTILE * HEADS):
                j, h = divmod(m, HEADS)
                dve.wait_ge(pt_ok, m + 1)
                if m >= 2:
                    dve.wait_ge(pv_ok, m - 1)
                v.tensor_copy(pT[:, m % 2, 0:min(512, (j + 1) * P)], banks(4, 1)[:, 0:min(512, (j + 1) * P)]).then_inc(pt_d, 1)
                for k, t in slots(j, h, 0):
                    misc(k, t)
                if m + 2 < NTILE * HEADS:
                    rowmax(m + 2)
                for k, t in slots(j, h, 1):
                    misc(k, t)
                if m in EARLY:
                    unit_lo(IN_UNITS + EARLY.index(m))
                if m + 1 == NTILE * HEADS:
                    conv_lo(0)
                if h + 1 == HEADS:
                    dve.wait_ge(ex_ok, m + 1)
                    link(v.reciprocal(rinv[:, :], rsum[:, j % 2, :]))
                    dve.wait_ge(pv_ok, m + 1)
                    if j:
                        dve.wait_ge(m_free, at_stage["oT", j - 1] + 1)
                    v.tensor_tensor(On[:, :].rearrange("p (h c) -> p h c", h=HEADS), pb[:, 6, :].rearrange("p (h c) -> p h c", h=HEADS),
                                    rinv[:, :].unsqueeze(2).broadcast_to([P, HEADS, VD]), ALU.mult).then_inc(on_ok, 1)

            conv_lo(1)
            for c in range(2):
                dve.wait_ge(sp_hi, c + 3)
                v.tensor_tensor(aT[1][:, 2 * c:2 * c + 2, :], attnT[:, 2 * c:2 * c + 2, :], aT[0][:, 2 * c:2 * c + 2, :].bitcast(F32), ALU.subtract).then_inc(sp_lo, 1)

            def wout_rest(k, count):
                dve.wait_ge(wo_hi_ok, count)
                v.tensor_tensor(wout_lo[:, k, :], wout[:, k, :], wout_hi[k][:, :].bitcast(F32), ALU.subtract).then_inc(wo_lo_ok, 1)

            def merged_lo(c):
                dve.wait_ge(mg_hi_ok, c + 1)
                v.tensor_tensor(mg[1][:, c, :], gates[:, c, :], mg[0][:, c, :].bitcast(F32), ALU.subtract).then_inc(mg_lo_ok, 1)

            for c in range(OUT_UNITS):
                dve.wait_ge(u_mm, IN_UNITS + c + 1)
                v.tensor_tensor(gates[:, c, :], gates[:, c, :], banks(4 * (c % 2), 2), ALU.mult)
                v.tensor_tensor(gates[:, KD + c, :], gates[:, KD + c, :], banks(4 * (c % 2) + 2, 2), ALU.mult).then_inc(yab_used, 1)
                dve.wait_ge(yab_used, c + 1)
                v.tensor_tensor(gates[:, c, :], gates[:, c, :], gates[:, KD + c, :], ALU.add).then_inc(mg_ok, 1)
                if c + 2 < OUT_UNITS:
                    unit_lo(IN_UNITS + c + 2)
                if 2 <= c < 6:
                    wout_rest(c + 2, c - 1)
                merged_lo(c)
                if c == 6:
                    wout_rest(0, 5)
                    wout_rest(1, 6)
            wout_rest(2, 7)
            wout_rest(3, 8)

            def logits_out(j):
                dve.wait_ge(lg_ps, j + 1)
                v.tensor_copy(lg[:, j, :], pb[:, 6, 0:NG])
                v.tensor_copy(le[:, j, :], pb[:, 6, NG:NG + NE]).then_inc(lg_ok, 1)

            def route(j):
                dve.wait_ge(lg_ok, j + 1)
                col, L = slice(j, j + 1), le[:, j, :]
                link(v.reduce_max(first[:, col], lg[:, j, :], axis=AX.X))
                link(v.tensor_scalar(tg[:, j, :], lg[:, j, :], first[:, col], None, ALU.subtract))
                link(v.scalar_tensor_tensor(out=pen[:, :], in0=tg[:, j, :], scalar=0.0, in1=down4[:, :], op0=ALU.is_ge, op1=ALU.mult))
                link(v.reduce_max(logit[0][:, col], pen[:, :], axis=AX.X))
                link(v.tensor_scalar(pen[:, :], pen[:, :], logit[0][:, col], -1.0, ALU.is_equal, ALU.add))
                grp = L.rearrange("p (g e) -> p g e", g=NG)
                link(v.scalar_tensor_tensor(out=grp, in0=pen[:, :].unsqueeze(2).broadcast_to([P, NG, EPG]), scalar=-MASKED, in1=grp, op0=ALU.mult, op1=ALU.add))
                for c in range(2):
                    top = logit[c][:, col]
                    link(v.reduce_max(top, L, axis=AX.X))
                    link(v.scalar_tensor_tensor(out=te[:, :], in0=L, scalar=top, in1=down32[:, :], op0=ALU.is_ge, op1=ALU.mult))
                    link(v.reduce_max(first[:, col], te[:, :], axis=AX.X))
                    link(v.tensor_scalar(oh[c][:, j, :], te[:, :], first[:, col], None, ALU.is_equal))
                    if c == 0:
                        link(v.scalar_tensor_tensor(out=L, in0=oh[0][:, j, :], scalar=2 * MASKED, in1=L, op0=ALU.mult, op1=ALU.add))
                v.tensor_tensor(ab[:, j, :], oh[0][:, j, :], oh[1][:, j, :], ALU.add).then_inc(a_ok, 1)

            dve.wait_ge(gff_in, 16 * 5)
            for j in range(NTILE):
                dve.wait_ge(x1_ps, j + 1)
                dve.wait_ge(xb_in[j % 2], 16 * (j // 2 + 1))
                v.tensor_tensor(x1[:, j, :], xb[:, j % 2, :], banks(2 * (j % 2), 2), ALU.add).then_inc(x1_ok, 1)
                dve.wait_ge(ss7, j + 1)
                dve.wait_ge(rs7, j + 1)
                if j >= 2:
                    dve.wait_ge(h2_out[j % 2], 16 * (j // 2))
                    dve.wait_ge(h2t_ps, j - 1)
                v.scalar_tensor_tensor(out=h2[:, j % 2, :], in0=x1[:, j, :], scalar=rs1[:, j:j + 1], in1=gffb[:, :], op0=ALU.mult, op1=ALU.mult).then_inc(h2_ok, 1)
                if j >= 2:
                    logits_out(j - 2)
                    route(j - 2)
            for j in (NTILE - 2, NTILE - 1):
                logits_out(j)
                route(j)
            dve.wait_ge(a_ok, NTILE)
            v.tensor_tensor(second[:, :], logit[1][:, :], logit[0][:, :], ALU.subtract).then_inc(r_in, 1)

            def row(t, n):
                return t.unsqueeze(1).broadcast_to([P, NTILE, n])

            dve.wait_ge(rc_ps, 1)
            total = pb[:, 0, NE * NTILE:NE * (NTILE + 1)]
            link(v.tensor_tensor(cmp8[:, :, :], total.unsqueeze(2).broadcast_to([P, NE, 8]), io8[:, :].unsqueeze(1).broadcast_to([P, NE, 8]), ALU.is_gt))
            link(v.reduce_sum(nb[:, :], cmp8[:, :, :], axis=AX.X))
            link(v.tensor_tensor_scan(incl[:, :], one32[:, :], nb[:, :], 0.0, ALU.mult, ALU.add))
            dve.wait_ge(iota_ok, 1)
            def block_experts(lo, hi):
                n = hi - lo
                link(v.tensor_tensor(cmpb[:, lo:hi, :], incl[0:1, :].unsqueeze(1).broadcast_to([1, n, NE]), iob[0:1, lo:hi].unsqueeze(2).broadcast_to([1, n, NE]), ALU.is_le))
                link(v.reduce_sum(bexp_f[:, lo:hi], cmpb[:, lo:hi, :], axis=AX.X))
                return v.tensor_scalar(bexp[:, lo:hi], bexp_f[:, lo:hi], float(NE - 1), None, ALU.min)

            v.tensor_scalar(cmp4[:, :], io4[:, :], incl[0:1, NE - 1:NE], None, ALU.is_lt)
            block_experts(0, SLOTS)
            link(v.reduce_sum(ntrip_f[:, :], cmp4[:, :], axis=AX.X))
            v.tensor_copy(ntrip_i[:, 0:1], ntrip_f[:, :])
            v.tensor_scalar(ntrip_i[:, 1:2], ntrip_f[:, :], 1.0, None, ALU.subtract).then_inc(route_ok, 1)
            link(v.tensor_tensor(b128[:, :], incl[:, :], nb[:, :], ALU.subtract))
            link(v.scalar_tensor_tensor(out=rank[:, :, :], in0=row(b128[:, :], NE), scalar=float(P), in1=pb[:, 0, 0:NE * NTILE].rearrange("p (j e) -> p j e", j=NTILE), op0=ALU.mult, op1=ALU.add))
            for c in range(2):
                link(v.tensor_tensor(oh[c][:, :, :], oh[c][:, :, :], rank[:, :, :], ALU.mult))
            for c in range(2):
                i = v.reduce_sum(pos2[:, c, :], oh[c][:, :, :], axis=AX.X)
            link(i)
            link(v.tensor_copy(pidx[:, :, :], pos2[:, :, :]))
            v.tensor_single_scalar(phi_i[:, :, :], pidx[:, :, :], 7, op=ALU.logical_shift_right)
            link(v.tensor_single_scalar(plo_i[:, :, :], pidx[:, :, :], P - 1, op=ALU.bitwise_and))
            v.tensor_copy(phi[:, :, :], phi_i[:, :, :])
            link(v.tensor_copy(plo[:, :, :], plo_i[:, :, :]))
            def flat(t):
                return t.rearrange("p c j -> p (c j)").unsqueeze(2)

            def count(t, n):
                return t.unsqueeze(1).broadcast_to([P, 2 * NTILE, n])

            v.tensor_tensor(ohp[:, :, :], flat(plo[:, :, :]).broadcast_to([P, 2 * NTILE, P]), count(iop[:, :], P), ALU.is_equal)
            link(v.tensor_tensor(ohb[:, :, :], flat(phi[:, :, :]).broadcast_to([P, 2 * NTILE, NBT]), count(iob[:, :], NBT), ALU.is_equal))
            for c in range(2):
                i = v.tensor_tensor(ohbt[:, c * NTILE:(c + 1) * NTILE, :], ohb[:, c * NTILE:(c + 1) * NTILE, :], trow[:, :].unsqueeze(2).broadcast_to([P, NTILE, NBT]), ALU.mult)
            i.then_inc(ohpb_ok, 1)
            dve.wait_ge(r_exp, 1)
            link(v.reduce_sum(denom[:, :], tg[:, :, :], axis=AX.X))
            dve.wait_ge(r_exp, 2)
            link(v.tensor_scalar(onep[:, :], second[:, :], 1.0, None, ALU.add))
            link(v.tensor_tensor(denom[:, :], denom[:, :], onep[:, :], ALU.mult))
            link(v.reciprocal(wt[:, 0, :], denom[:, :]))
            dve.wait_ge(slot_ps, 1)
            link(v.tensor_scalar(stok[:, :], pb[:, 6, 0:NBT], float(T), None, ALU.add))
            for b in range(2):
                v.tensor_scalar(icol[b][:, :], stok[:, b:b + 1], 0.0, None, ALU.add).then_inc(ic_ok, 1)
            link(v.tensor_tensor(wt[:, 1, :], wt[:, 0, :], second[:, :], ALU.mult))
            v.tensor_tensor(ohb[:, :, :], ohb[:, :, :], flat(wt[:, :, :]).broadcast_to([P, 2 * NTILE, NBT]), ALU.mult).then_inc(wt_ok, 1)
            block_experts(SLOTS, NBT).then_inc(bexp_ok, 1)
            dve.wait_ge(swt_ps, 1)
            v.tensor_copy(swt[:, :], pb[:, 7, 0:NBT]).then_inc(stok_ok, 1)

            ntrip = dve.value_load(ntrip_i[0:1, 0:1], min_val=2, max_val=MAXB // SLOTS)

            def gathered_T(b, count, col):
                dve.wait_ge(hgt_ps, count)
                v.tensor_copy(hgT[b][:, :, :], banks(0, 2).rearrange("p (k t) -> p k t", k=KD)).then_inc(hgt_ok, 1)
                v.tensor_scalar(icol[b][:, :], stok[:, bass.ds(col, 1)], 0.0, None, ALU.add).then_inc(ic_ok, 1)

            for k in range(2):
                gathered_T(k, k + 1, k + 2)
            with dve.Fori(0, ntrip) as i:
                for q in range(SLOTS):
                    b, nth = q % 2, i * SLOTS + (q + 1)
                    dve.wait_ge(sil_ok, nth)
                    v.tensor_tensor(mid[:, :], sil[:, :], pb[:, GU_BANK[b], FF:2 * FF], ALU.mult).then_inc(mid_ok, 1)
                    dve.wait_ge(mt_ps, nth)
                    v.tensor_copy(midT[:, :, :], pb[:, 3, 0:FF].rearrange("p (f t) -> p f t", f=2)).then_inc(mt_ok, 1)
                    gathered_T(b, i * SLOTS + (q + 3), i * SLOTS + (q + SLOTS))
                    dve.wait_ge(y_out[b], i * (8 * SLOTS) + 16 * (q // 2 + 1))
                    v.tensor_scalar(rcol[b][:, :], stok[:, bass.ds(i * SLOTS + q, 1)], 0.0, None, ALU.add)
                    v.tensor_scalar(wcol[b][:, :], swt[:, bass.ds(i * SLOTS + q, 1)], 1.0, None, ALU.mult).then_inc(wc_ok, 1)
                    dve.wait_ge(wc_ok, nth)
                    dve.wait_ge(y_ps, nth)
                    v.tensor_scalar(yb[b][:, 512:1024], pb[:, 5, :], wcol[b][:, :], None, ALU.mult).then_inc(y_d_ok, 1)

        @block.tensor
        def _(pe):
            t_ = nc.tensor

            def three(out, w, m, start, stop):
                t_.matmul(out, w(0), m(0), start=start, stop=False)
                t_.matmul(out, w(0), m(1), start=False, stop=False)
                return t_.matmul(out, w(1), m(0), start=False, stop=stop)

            def scaled_T(j):
                pe.wait_ge(s_xn, j + 1)
                pe.wait_ge(x_in[j], 16)
                if j >= 2:
                    pe.wait_ge(s_hp, j - 1)
                for k in range(KD):
                    i = t_.matmul(banks(2 * (j % 2), 2)[:, k * P:(k + 1) * P], xs[:, j, k * P:(k + 1) * P], diag[:, j % 2, :], start=True, stop=True)
                i.then_inc(s_xt, 1)

            scaled_T(0)
            pe.wait_ge(ident_ok, 1)
            pe.wait_ge(consts, 1)
            pe.wait_ge(small_in, 16 * 13)
            pe.wait_ge(vec_c, 1)
            t_.transpose(pb[:, 6, 0:NV], vecs[0:NV, :], ident[0:NV, 0:NV])
            t_.transpose(pb[:, 6, 64:64 + TAPS * NC], dwr[:, :], ident[0:TAPS * NC, 0:TAPS * NC])
            t_.transpose(pb[:, 6, 256:256 + NTILE], posf[:, :], ident[0:NTILE, 0:NTILE]).then_inc(vec_t, 1)
            scaled_T(1)
            for j in range(NTILE):
                if j + 2 < NTILE:
                    scaled_T(j + 2)
                if j == 0:
                    pe.wait_ge(dn_lo, 2)
                pe.wait_ge(s_lo, j + 1)
                if j >= 2:
                    pe.wait_ge(dn_ev, j - 1)
                for k in range(KD):
                    i = three(pb[:, 6 + j % 2, 0:DOWN], lambda s: hT[s][:, k, j * P:(j + 1) * P], lambda s: wdn[s][:, k, :], k == 0, k == KD - 1)
                i.then_inc(dn_ps, 1)
            def misc(kind, t):
                s = at_stage[kind, t]
                M = pb[:, 7, :]
                if s:
                    pe.wait_ge(m_free, s)
                if kind == "qdT":
                    pe.wait_ge(qd_ok, 1)
                    for c in range(3):
                        i = t_.transpose(M[:, c * P:(c + 1) * P], qd[:, t, c * P:(c + 1) * P], ident[:, :])
                if kind in ("q0", "q1"):
                    pe.wait_ge(uq_in, 16)
                    c0 = 4 * QK * (kind == "q1")
                    for k in range(2):
                        i = t_.matmul(M[:, 0:4 * QK], qdT[:, k, :], wuq[:, k, c0:c0 + 4 * QK], start=(k == 0), stop=(k == 1))
                if kind in ("kv0", "kv1"):
                    pe.wait_ge(ukv_in, 16)
                    c0 = 512 * (kind == "kv1")
                    i = t_.matmul(M, qdT[:, 2, :], wukv[:, c0:c0 + 512], start=True, stop=True)
                if kind in ("qT0", "qT1", "kT0", "kT1"):
                    src = qn if kind[0] == "q" else kn if t else kn_first
                    pe.wait_ge(qk_ok, 2 * t + (1 if kind[0] == "q" else 2))
                    h0 = 4 * (kind[2] == "1")
                    for h in range(4):
                        i = t_.transpose(M[0:QK, h * P:(h + 1) * P], src[:, h0 + h, :], ident[:, :])
                if kind == "oT":
                    pe.wait_ge(on_ok, t + 1)
                    for c in range(4):
                        i = t_.transpose(M[:, c * P:(c + 1) * P], On[:, c * P:(c + 1) * P], ident[:, :])
                i.then_inc(m_full, 1)

            def unit(b, between=None):
                for f in range(2):
                    for k in range(KD):
                        if between and (f, k) in between:
                            misc(between[f, k], 0)
                        i = three(pb[:, 2 * b + 2 + f, :], lambda s: ws[s][:, b, k, :], lambda s: hT[s][:, k, f * 512:(f + 1) * 512], k == 0, k == KD - 1)
                i.then_inc(u_mm, 1)

            for b in range(2):
                pe.wait_ge(u_lo, b + 1)
                unit(b)
            with pe.Fori(1, LN_UNIT // 2) as i:
                for b in range(2):
                    pe.wait_ge(u_lo, i * 2 + (b + 1))
                    pe.wait_ge(u_ev, i * 2 + (b - 1))
                    unit(b)
            for u in range(LN_UNIT, IN_UNITS):
                pe.wait_ge(u_lo, u + 1)
                pe.wait_ge(u_ev, u - 1)
                if u < IN_UNITS - 1:
                    unit(u % 2)
                else:
                    pe.wait_ge(ln_sd, 1)
                    unit(u % 2, {(0, 0): "qdT", (0, 4): "q0", (0, 7): "q1", (1, 2): "kv0", (1, 5): "kv1"})
                if u == LN_UNIT:
                    pe.wait_ge(conv_done, NC)
                    for f in range(2):
                        for c in range(NC):
                            i = t_.matmul(pb[:, f, :], mean_w[:, :], cv[:, c, f * 512:(f + 1) * 512], start=(c == 0), stop=(c == NC - 1))
                    i.then_inc(ln_mu, 1)
                if u == LN_UNIT + 1:
                    for c in range(NC):
                        pe.wait_ge(ln_sq, c + 1)
                        for f in range(2):
                            i = t_.matmul(pb[:, 6 + f, :], mean_w[:, :], lnt[c][:, f * 512:(f + 1) * 512], start=(c == 0), stop=(c == NC - 1))
                    i.then_inc(ln_var, 1)

            def scores(n):
                j, h = divmod(n, HEADS)
                w = (j + 1) * P
                if h % 4 == 0:
                    pe.wait_ge(m_free, at_stage[f"kT{h // 4}", j] + 1)
                if n >= 2:
                    pe.wait_ge(ex_ok, n - 1)
                S = banks(2 * (n % 2), 2)
                for f in range(0, w, 512):
                    e = min(w, f + 512)
                    t_.matmul(S[:, f:e], qT[0:QK, j % 2, h * P:(h + 1) * P], kT[0:QK, h, f:e], start=True, stop=(e < w))
                t_.matmul(S[:, w - P:w], mrow[0:1, 0, :], mrow[0:1, 1, :], start=False, stop=True).then_inc(sc_ok, 1)

            def probs_T(n):
                j, h = divmod(n, HEADS)
                pe.wait_ge(ex_ok, n + 1)
                if n >= 1:
                    pe.wait_ge(pt_d, n)
                    if (n - 1) // HEADS >= 4:
                        pe.wait_ge(pt_a, n - 4 * HEADS)
                for k in range(j + 1):
                    i = t_.transpose(banks(4, 2)[:, k * P:(k + 1) * P], pr[:, n % 2, k * P:(k + 1) * P], ident[:, :])
                i.then_inc(pt_ok, 1)

            def pv(n):
                j, h = divmod(n, HEADS)
                pe.wait_ge(pt_d, n + 1)
                if j >= 4:
                    pe.wait_ge(pt_a, n + 1 - 4 * HEADS)
                if h == 0 and j:
                    pe.wait_ge(on_ok, j)
                for k in range(j + 1):
                    i = t_.matmul(pb[:, 6, h * VD:(h + 1) * VD], pT[:, n % 2, k * P:(k + 1) * P], vv[:, k, h * VD:(h + 1) * VD], start=(k == 0), stop=(k == j))
                i.then_inc(pv_ok, 1)

            pe.wait_ge(ln_y, 1)
            pe.wait_ge(u_ev, IN_UNITS)
            for k in PREP[5:]:
                misc(k, 0)
            scores(0)
            scores(1)
            for n in range(NTILE * HEADS):
                j, h = divmod(n, HEADS)
                probs_T(n)
                for k, t in slots(j, h, 0):
                    misc(k, t)
                if n + 2 < NTILE * HEADS:
                    scores(n + 2)
                for k, t in slots(j, h, 1):
                    misc(k, t)
                pv(n)
            misc("oT", NTILE - 1)

            pe.wait_ge(m_free, len(order))
            def branches(b, first=False):
                for br_ in (1, 0):
                    for f in range(2):
                        for k in range(4):
                            if first and f == 0 and k % 2 == 0:
                                pe.wait_ge(sp_lo, 1 + k // 2 + 2 * (1 - br_))
                            i = three(pb[:, 4 * b + 2 * br_ + f, :], lambda s: ws[s][:, b, 4 * br_ + k, :],
                                      lambda s: aT[s][:, 4 * br_ + k, f * 512:(f + 1) * 512], k == 0, k == 3)
                i.then_inc(u_mm, 1)

            for b in range(2):
                pe.wait_ge(u_lo, IN_UNITS + b + 1)
                branches(b, b == 0)
            with pe.Fori(1, OUT_UNITS // 2) as i:
                for b in range(2):
                    pe.wait_ge(u_lo, i * 2 + (IN_UNITS + b + 1))
                    pe.wait_ge(yab_used, i * 2 + (b - 1))
                    branches(b)
            pe.wait_ge(wo_lo_ok, 6)
            pe.wait_ge(mg_lo_ok, OUT_UNITS - 1)
            wout_pair = (lambda k: wout_hi[k][:, :], lambda k: wout_lo[:, k, :])

            def h2_T(j):
                pe.wait_ge(h2_ok, j + 1)
                if j >= 1:
                    pe.wait_ge(h2t_ok, j)
                for k in range(KD):
                    i = t_.transpose(banks(4, 2)[:, k * P:(k + 1) * P], h2[:, j % 2, k * P:(k + 1) * P], ident[:, :])
                i.then_inc(h2t_ps, 1)

            def logits(j):
                pe.wait_ge(h2t_ok, j + 1)
                if j >= 1:
                    pe.wait_ge(lg_ok, j)
                for k in range(KD):
                    t_.matmul(pb[:, 6, 0:NG + NE], h2T[:, j % 2, k, :], wr[:, k, :], start=(k == 0), stop=False)
                t_.matmul(pb[:, 6, 0:NG + NE], one_row[0:1, :], br[0:1, :], start=False, stop=True).then_inc(lg_ps, 1)

            for j in range(NTILE):
                if j >= 2:
                    pe.wait_ge(x1_ok, j - 1)
                for f in range(2):
                    for n, k in enumerate(WOUT_ORDER):
                        if j == 0 and f == 0 and k in (2, 3):
                            pe.wait_ge(wo_lo_ok, 5 + k)
                        if j == 0 and f == 0 and k == OUT_UNITS - 1:
                            pe.wait_ge(mg_lo_ok, OUT_UNITS)
                        i = three(pb[:, 2 * (j % 2) + f, :], lambda s: mg[s][:, k, j * P:(j + 1) * P], lambda s: wout_pair[s](k)[:, f * 512:(f + 1) * 512], n == 0, n == KD - 1)
                if j == 0:
                    pe.wait_ge(gff_in, 16 * 5)
                i.then_inc(x1_ps, 1)
                if j >= 1:
                    h2_T(j - 1)
                if j >= 2:
                    logits(j - 2)
            logits(NTILE - 2)
            h2_T(NTILE - 1)
            logits(NTILE - 1)
            pe.wait_ge(a_ok, NTILE)
            N = NE * (NTILE + 1)
            t_.matmul(pb[:, 0, 0:N], before[:, :], ab[:, :, :].rearrange("p j e -> p (j e)"), start=True, stop=False)
            for j in range(NTILE):
                i = t_.matmul(pb[:, 0, NE * (j + 1):N].rearrange("p (j e) -> p j e", e=NE), ones_b[:, :],
                              ab[:, j:j + 1, :].broadcast_to([P, NTILE - j, NE]), start=False, stop=(j == NTILE - 1))
            i.then_inc(rc_ps, 1)
            pe.wait_ge(ohpb_ok, 1)
            for m in range(2 * NTILE):
                i = t_.matmul(pb[:, 6, 0:NBT], ohp[:, m, :], ohbt[:, m, :], start=(m == 0), stop=(m == 2 * NTILE - 1))
            i.then_inc(slot_ps, 1)
            pe.wait_ge(wt_ok, 1)
            for m in range(2 * NTILE):
                i = t_.matmul(pb[:, 7, 0:NBT], ohp[:, m, :].bitcast(F32), ohb[:, m, :], start=(m == 0), stop=(m == 2 * NTILE - 1))
            i.then_inc(swt_ps, 1)

            pe.wait_ge(route_ok, 1)
            pe.sem_inc(y_a, 1)
            pe.sem_inc(y_d_ok, 1)
            last = pe.value_load(ntrip_i[0:1, 1:2], min_val=1, max_val=MAXB // SLOTS - 1)

            def gather_T(b, gathers):
                pe.wait_ge(hg_in[b], gathers)
                for k in range(KD):
                    i = t_.transpose(banks(0, 2)[:, k * P:(k + 1) * P], hg[b][:, k * P:(k + 1) * P], ident[:, :])
                i.then_inc(hgt_ps, 1)

            def gate_up(q, i, hgts):
                pe.wait_ge(w_in0[q], i * 32 + 32)
                pe.wait_ge(hgt_ok, hgts)
                for k in range(KD):
                    m = t_.matmul(pb[:, GU_BANK[q % 2], :], hgT[q % 2][:, k, :], wgu[q][:, k, :], start=(k == 0), stop=(k == KD - 1))
                m.then_inc(gu_ps, 1)

            def finish(q, i):
                nth = i * SLOTS + (q + 1)
                pe.wait_ge(mid_ok, nth)
                for f in range(2):
                    m = t_.transpose(pb[:, 3, f * P:(f + 1) * P], mid[:, f * P:(f + 1) * P], ident[:, :])
                m.then_inc(mt_ps, 1)
                gather_T(q % 2, i * (8 * SLOTS) + 16 * (q // 2 + 2))
                pe.wait_ge(mt_ok, nth)
                pe.wait_ge(w_in1[q], i * 16 + 16)
                pe.wait_ge(y_a, nth)
                pe.wait_ge(y_d_ok, nth)
                for h in range(2):
                    for f in range(2):
                        m = t_.matmul(pb[:, 4 + h, :], midT[:, f, :], wed[q][:, f, h * 512:(h + 1) * 512], start=(f == 0), stop=(f == 1))
                m.then_inc(y_ps, 1)

            for k in range(2):
                if k:
                    pe.wait_ge(hgt_ok, k)
                gather_T(k, 16)
            gate_up(0, 0, 1)
            with pe.Fori(0, last) as i:
                for q in range(SLOTS):
                    gate_up((q + 1) % SLOTS, i + (q + 1) // SLOTS, i * SLOTS + (q + 2))
                    finish(q, i)
            for q in range(SLOTS):
                if q + 1 < SLOTS:
                    gate_up(q + 1, last, last * SLOTS + (q + 2))
                finish(q, last)


_INS = ["x", "positions", "g_mix", "w_in", "g_q_lora", "w_uq", "g_kv_lora", "w_ukv", "g_qk_q", "g_qk_k",
        "w_o_mla", "w_dw", "b_dw", "g_conv_ln", "b_conv_ln", "w_conv_out", "b_gates", "w_out", "g_ffn",
        "w_group_router", "b_group_router", "w_expert_router", "b_expert_router",
        "w_e_gate", "w_e_up", "w_e_down"]
_OUTS = [((1, T, D), "float32")]


def kernel(**inputs):
    import numpy as np
    import concourse.bacc as bacc
    from concourse.bass_utils import run_bass_kernel_spmd

    nc = bacc.Bacc("TRN2", target_bir_lowering=False, num_devices=1, dynamic_dma_scratch_size=4096)
    arrays, args = {}, []
    for name in _INS:
        a = np.ascontiguousarray(inputs[name])
        arrays[f"in_{name}"] = a
        args.append(nc.dram_tensor(f"in_{name}", a.shape, mybir.dt.from_np(a.dtype), kind="ExternalInput").ap())
    for i, (shape, dtype) in enumerate(_OUTS):
        args.append(nc.dram_tensor(f"out_{i}", shape, mybir.dt.from_np(np.dtype(dtype)), kind="ExternalOutput").ap())
    build(nc, *args)
    r = run_bass_kernel_spmd(nc, [arrays], core_ids=[0])
    return r.results[0]["out_0"]
```
